# Optimizing a Trainium2 kernel written in Bass

```python
import math
import jax, jax.numpy as jnp
from jax import lax
import numpy as np

D_MODEL = 1024
BATCH = 1
SEQ = 2048
DEPTH = 1

CHUNK = 64
ROPE_THETA = 10000.0
A_HEADS = 8
A_KV_HEADS = 2
A_HEAD_DIM = 64
A_WINDOW = 128
A_WINDOW_CHUNKS = A_WINDOW // CHUNK
B_HEADS = 4
B_HEAD_DIM = 64
B_V_DIM = 2 * B_HEAD_DIM
Q_BLOCK = 128
N_GROUPS = 4
EXPERTS_PER_GROUP = 8
N_EXPERTS = N_GROUPS * EXPERTS_PER_GROUP
TOP_K = 2
EXPERT_FF = 512
ALPHA = (2.0 * DEPTH) ** 0.25
BETA = (8.0 * DEPTH) ** -0.25
LN_EPS = 1e-5
RMS_EPS = 1e-5
NEG_INF = -1e30

A_Q_W = A_HEADS * A_HEAD_DIM
A_KV_W = A_KV_HEADS * A_HEAD_DIM
B_QK_W = B_HEADS * 2 * B_HEAD_DIM
B_V_W = B_HEADS * B_V_DIM
GATE_W = 2 * D_MODEL
IN_SIZES = [A_Q_W, A_KV_W, A_KV_W, B_QK_W, B_QK_W, B_V_W, GATE_W]
IN_W = sum(IN_SIZES)
IN_SPLITS = [int(v) for v in np.cumsum(IN_SIZES[:-1])]

kernel_name = 'hybrid_swa_sink_diffattn_hmoe_deepnorm'

def layer_norm(x, g, b):
    xf = x.astype(jnp.float32)
    mu = jnp.mean(xf, -1, keepdims=True)
    var = jnp.mean(jnp.square(xf - mu), -1, keepdims=True)
    y = (xf - mu) * lax.rsqrt(var + LN_EPS) * g.astype(jnp.float32) + b.astype(jnp.float32)
    return y.astype(x.dtype)

def rope_tables(positions, dim):
    inv = 1.0 / (ROPE_THETA ** (jnp.arange(0, dim, 2, dtype=jnp.float32) / dim))
    ang = positions.astype(jnp.float32)[..., None] * inv
    return jnp.cos(ang)[:, :, None, :], jnp.sin(ang)[:, :, None, :]

def apply_rope(x, cos, sin):
    xf = x.astype(jnp.float32)
    x1, x2 = jnp.split(xf, 2, axis=-1)
    return jnp.concatenate([x1 * cos - x2 * sin, x2 * cos + x1 * sin], -1).astype(x.dtype)

def window_chunks(t, n):
    nc = t.shape[1]
    pad = [(0, 0), (0, 0)] + [(0, 0)] * (t.ndim - 2)
    parts = []
    for s in range(n - 1, -1, -1):
        pad[1] = (s, 0)
        parts.append(jnp.pad(t[:, :nc - s], pad))
    return jnp.concatenate(parts, axis=2)

def swa_sink_attention(q, k, v, sinks):
    b, s, _, d = q.shape
    nc = s // CHUNK
    grp = A_HEADS // A_KV_HEADS
    qc = q.reshape(b, nc, CHUNK, A_KV_HEADS, grp, d)
    kb = window_chunks(k.reshape(b, nc, CHUNK, A_KV_HEADS, d), A_WINDOW_CHUNKS)
    vb = window_chunks(v.reshape(b, nc, CHUNK, A_KV_HEADS, d), A_WINDOW_CHUNKS)
    sc = jnp.einsum('bnqkgd,bnjkd->bnkgqj', qc, kb).astype(jnp.float32) * (d ** -0.5)
    shift = A_WINDOW_CHUNKS - 1 - jnp.arange(A_WINDOW_CHUNKS * CHUNK) // CHUNK
    valid = jnp.arange(nc)[:, None] >= shift[None, :]
    sc = jnp.where(valid[None, :, None, None, None, :], sc, NEG_INF)
    sink = sinks.astype(jnp.float32).reshape(1, 1, A_KV_HEADS, grp, 1, 1)
    m = jnp.maximum(jnp.max(sc, -1, keepdims=True), sink)
    e = jnp.exp(sc - m)
    p = e / (jnp.sum(e, -1, keepdims=True) + jnp.exp(sink - m))
    o = jnp.einsum('bnkgqj,bnjkd->bnqkgd', p.astype(v.dtype), vb)
    return o.reshape(b, s, A_HEADS * d)

def diff_attention(q, k, v, lam, subln_g, lambda_init):
    b, s, h, _, d = q.shape
    nb = s // Q_BLOCK
    q_blocks = jnp.moveaxis(q.reshape(b, nb, Q_BLOCK, h, 2, d), 1, 0)
    key_chunk = jnp.arange(s) // CHUNK
    scale = d ** -0.5

    def block(args):
        qb, i = args
        sc = jnp.einsum('bqhmd,bshmd->bhmqs', qb, k).astype(jnp.float32) * scale
        q_chunk = (i * Q_BLOCK + jnp.arange(Q_BLOCK)) // CHUNK
        mask = key_chunk[None, :] <= q_chunk[:, None]
        p = jax.nn.softmax(jnp.where(mask, sc, NEG_INF), axis=-1)
        a = p[:, :, 0] - lam * p[:, :, 1]
        return jnp.einsum('bhqs,bshe->bqhe', a.astype(v.dtype), v)

    o = lax.map(block, (q_blocks, jnp.arange(nb)))
    o = jnp.moveaxis(o, 0, 1).reshape(b, s, h, B_V_DIM)
    of = o.astype(jnp.float32)
    of = of * lax.rsqrt(jnp.mean(jnp.square(of), -1, keepdims=True) + RMS_EPS)
    of = of * subln_g.astype(jnp.float32) * (1.0 - lambda_init)
    return of.astype(v.dtype).reshape(b, s, h * B_V_DIM)

def hierarchical_moe(x, w_group, b_group, w_router, b_router, w_gate_up, w_down):
    b, s, dm = x.shape
    t = b * s
    xt = x.reshape(t, dm)
    glog = (xt @ w_group + b_group).astype(jnp.float32)
    pg = jax.nn.softmax(glog, -1)
    gsel = jnp.argmax(glog, -1)
    pg_sel = jnp.take_along_axis(pg, gsel[:, None], 1)[:, 0]
    elog = (xt @ w_router + b_router).astype(jnp.float32).reshape(t, N_GROUPS, EXPERTS_PER_GROUP)
    elog = jnp.take_along_axis(elog, gsel[:, None, None], 1)[:, 0]
    pe = jax.nn.softmax(elog, -1)
    topv, topi = lax.top_k(pe, TOP_K)
    wts = pg_sel[:, None] * topv / jnp.sum(topv, -1, keepdims=True)
    eid = (gsel[:, None] * EXPERTS_PER_GROUP + topi).reshape(-1)
    order = jnp.argsort(eid)
    tok = order // TOP_K
    sizes = jnp.bincount(eid, length=N_EXPERTS).astype(jnp.int32)
    xs = xt[tok]
    hgu = lax.ragged_dot(xs, w_gate_up, sizes)
    g, u = jnp.split(hgu, 2, axis=-1)
    ys = lax.ragged_dot(jax.nn.silu(g) * u, w_down, sizes)
    ys = ys * wts.reshape(-1)[order][:, None].astype(ys.dtype)
    out = jnp.zeros((t, dm), ys.dtype).at[tok].add(ys)
    return out.reshape(b, s, dm)

def setup_inputs(seed: int = 0) -> dict:
    key = jax.random.key(seed)
    ks = jax.random.split(key, 24)
    L, D = DEPTH, D_MODEL
    f32 = jnp.float32
    nrm = lambda k, shape, std: (jax.random.normal(k, shape, f32) * std)
    x = jax.random.normal(ks[0], (BATCH, SEQ, D), f32)
    offs = jax.random.randint(ks[1], (BATCH, 1), 0, 1024, dtype=jnp.int32)
    positions = (jnp.arange(SEQ, dtype=jnp.int32)[None, :] + offs).astype(jnp.int32)
    return {
        'x': x,
        'positions': positions,
        'w_in': nrm(ks[2], (L, D, IN_W), D ** -0.5),
        'b_gate': nrm(ks[3], (L, GATE_W), 0.02),
        'sinks': nrm(ks[4], (L, A_HEADS), 0.5),
        'lambda_q1': nrm(ks[5], (L, B_HEAD_DIM), 0.1),
        'lambda_k1': nrm(ks[6], (L, B_HEAD_DIM), 0.1),
        'lambda_q2': nrm(ks[7], (L, B_HEAD_DIM), 0.1),
        'lambda_k2': nrm(ks[8], (L, B_HEAD_DIM), 0.1),
        'subln_g': 1.0 + nrm(ks[9], (L, B_V_DIM), 0.02),
        'w_proj_a': nrm(ks[10], (L, A_Q_W, D), BETA * A_Q_W ** -0.5),
        'w_proj_b': nrm(ks[11], (L, B_V_W, D), BETA * B_V_W ** -0.5),
        'w_out': nrm(ks[12], (L, D, D), BETA * D ** -0.5),
        'ln1_g': 1.0 + nrm(ks[13], (L, D), 0.02),
        'ln1_b': nrm(ks[14], (L, D), 0.02),
        'w_group': nrm(ks[15], (L, D, N_GROUPS), D ** -0.5),
        'b_group': nrm(ks[16], (L, N_GROUPS), 0.01),
        'w_router': nrm(ks[17], (L, D, N_EXPERTS), D ** -0.5),
        'b_router': nrm(ks[18], (L, N_EXPERTS), 0.01),
        'w_gate_up': nrm(ks[19], (L, N_EXPERTS, D, 2 * EXPERT_FF), D ** -0.5),
        'w_down': nrm(ks[20], (L, N_EXPERTS, EXPERT_FF, D), BETA * EXPERT_FF ** -0.5),
        'ln2_g': 1.0 + nrm(ks[21], (L, D), 0.02),
        'ln2_b': nrm(ks[22], (L, D), 0.02),
    }

def reference(x, positions, w_in, b_gate, sinks, lambda_q1, lambda_k1, lambda_q2, lambda_k2,
              subln_g, w_proj_a, w_proj_b, w_out, ln1_g, ln1_b, w_group, b_group, w_router,
              b_router, w_gate_up, w_down, ln2_g, ln2_b):
    b, s, _ = x.shape
    cos, sin = rope_tables(positions, A_HEAD_DIM)
    for l in range(DEPTH):
        h = x
        proj = h @ w_in[l]
        aq, ak, av, bq, bk, bv, gpre = jnp.split(proj, IN_SPLITS, axis=-1)
        aq = apply_rope(aq.reshape(b, s, A_HEADS, A_HEAD_DIM), cos, sin)
        ak = apply_rope(ak.reshape(b, s, A_KV_HEADS, A_HEAD_DIM), cos, sin)
        av = av.reshape(b, s, A_KV_HEADS, A_HEAD_DIM)
        oa = swa_sink_attention(aq, ak, av, sinks[l])
        lambda_init = 0.8 - 0.6 * math.exp(-0.3 * l)
        lam = (jnp.exp(jnp.sum(lambda_q1[l].astype(jnp.float32) * lambda_k1[l].astype(jnp.float32)))
               - jnp.exp(jnp.sum(lambda_q2[l].astype(jnp.float32) * lambda_k2[l].astype(jnp.float32)))
               + lambda_init)
        bq = apply_rope(bq.reshape(b, s, 2 * B_HEADS, B_HEAD_DIM), cos, sin).reshape(b, s, B_HEADS, 2, B_HEAD_DIM)
        bk = apply_rope(bk.reshape(b, s, 2 * B_HEADS, B_HEAD_DIM), cos, sin).reshape(b, s, B_HEADS, 2, B_HEAD_DIM)
        bv = bv.reshape(b, s, B_HEADS, B_V_DIM)
        ob = diff_attention(bq, bk, bv, lam, subln_g[l], lambda_init)
        ga, gb = jnp.split(jax.nn.sigmoid(gpre + b_gate[l]), 2, axis=-1)
        mix = (ga * (oa @ w_proj_a[l]) + gb * (ob @ w_proj_b[l])) @ w_out[l]
        x = layer_norm(ALPHA * h + mix, ln1_g[l], ln1_b[l])
        ff = hierarchical_moe(x, w_group[l], b_group[l], w_router[l], b_router[l], w_gate_up[l], w_down[l])
        x = layer_norm(ALPHA * x + ff, ln2_g[l], ln2_b[l])
    return x


_drawn_inputs = setup_inputs


def setup_inputs(seed=0):
    import zlib

    import numpy as np

    out = dict(_drawn_inputs(seed))
    spreads = {}
    factors = {'b_gate': 8.0,
     'sinks': 200.0,
     'lambda_q1': 176.275,
     'lambda_k1': 3.495,
     'lambda_q2': 4.37,
     'lambda_k2': 5.533,
     'subln_g': 20.618,
     'b_group': 22.554,
     'b_router': 15.597,
     'ln2_g': 20.683,
     'ln2_b': 21.381,
     'w_proj_a': 4.61}
    for name, (base, spread) in spreads.items():
        noise = np.random.default_rng([zlib.crc32(name.encode()), seed]).standard_normal(out[name].shape)
        drawn = base * np.exp(spread * noise) if base else spread * noise
        out[name] = __import__('jax').numpy.asarray(drawn.astype(out[name].dtype))
    for name, factor in factors.items():
        out[name] = (out[name] * factor).astype(out[name].dtype)
    return out
```

```python
import math
from contextlib import ExitStack

import numpy as np

import concourse.bass as bass
from concourse import mybir
from concourse.alu_op_type import AluOpType as ALU

F32 = mybir.dt.float32
F32R = mybir.dt.float32r
I32 = mybir.dt.int32
ACT = mybir.ActivationFunctionType
AX = mybir.AxisListType

P = 128
SEQ = 2048
D = 1024
KD = D // P
NT = SEQ // P
CHUNK = 64
HD = 64
HALF = HD // 2
A_HEADS = 8
A_KV = 2
B_HEADS = 4
BV = 128
NG = 4
EPG = 8
NE = NG * EPG
FF = 512
ALPHA = 2.0 ** 0.25
EPS = 1e-5
NEG = -1e30
SCALE = HD ** -0.5
LAM_INIT = 0.8 - 0.6 * math.exp(0.0)

A_Q = A_HEADS * HD
A_K = A_KV * HD
B_QK = B_HEADS * 2 * HD
B_V = B_HEADS * BV
QKV = A_Q + 2 * A_K + 2 * B_QK + B_V
GATE = 2 * D
BANK = 512

GROUPS = [(0, 512, 0), (512, 128, 128), (768, 512, 0), (1280, 512, 0), (1792, 0, 512)]
PIECE0 = [0, 4, 5, 9]
NPIECE = 13
VW = A_K + B_V
MAXT = (2 * SEQ) // P + NE - 1


class Phase:

    def __init__(self, nc, name):
        self.nc, self.name, self.ctx, self.used = nc, name, ExitStack(), []

    def __enter__(self):
        self.ctx.__enter__()
        return self

    def __exit__(self, *a):
        done = self.ctx.__exit__(*a)
        if self.used:
            self.nc.clear_and_free_semaphores(self.used)
            self.nc.all_engine_barrier()
        return done

    def sb(self, name, shape, dt=F32):
        return self.ctx.enter_context(self.nc.sbuf_tensor(f"{self.name}_{name}", shape, dt))

    def ps(self, name, shape, dt=F32):
        return self.ctx.enter_context(self.nc.psum_tensor(f"{self.name}_{name}", shape, dt))

    def sem(self, name):
        self.used.append(self.nc.alloc_semaphore(f"{self.name}_{name}"))
        return self.used[-1]

    def sems(self, name, n):
        return [self.sem(f"{name}{i}") for i in range(n)]

    def block(self):
        return self.ctx.enter_context(self.nc.Block())


def settled(eng, passed):
    eng.sem_inc(passed, 1)


def f(ap):
    return ap.bitcast(F32)


def constants_phase(nc, ident, identr):
    with Phase(nc, "c") as ph:
        zeroed, made = ph.sem("zeroed"), ph.sem("made")
        block = ph.block()

        @block.gpsimd
        def _(pool):
            nc.gpsimd.memset(ident[:], 0.0).then_inc(zeroed, 1)
            pool.wait_ge(zeroed, 1)
            nc.gpsimd.affine_select(out=ident[:], in_=ident[:], compare_op=ALU.not_equal, fill=1.0, base=0,
                                    pattern=[[-1, P]], channel_multiplier=1).then_inc(made, 1)
            pool.wait_ge(made, 1)


def prepare_phase(nc, x, w_in, positions, inv_freq, ident, w_hi, w_lo, cos_t, sin_t, nsin_t, xt_hi, xt_lo):
    two_pi = 2.0 * math.pi
    PI_IN = 3.1415925
    c1 = 6.28125
    c2 = float(np.float32(1.934051513671875e-3))
    c3 = float(two_pi - c1 - c2)
    with Phase(nc, "p") as ph:
        x_in = ph.sb("x_in", [P, 2, D])
        xh = ph.sb("xh", [P, 2, D], F32R)
        xl = ph.sb("xl", [P, 2, D], F32R)
        raw = ph.sb("raw", [P, 2, QKV])
        pos_i = ph.sb("pos_i", [P, NT], I32)
        pos_f = ph.sb("pos_f", [P, NT])
        inv = ph.sb("inv", [P, HALF])
        ang = ph.sb("ang", [P, NT, HALF])
        turns = ph.sb("turns", [P, NT, HALF])
        turns_i = ph.sb("turns_i", [P, NT, HALF], I32)
        red = ph.sb("red", [P, NT, HALF])
        psx = ph.ps("psx", [P, 2, D])
        x_loaded = ph.sems("x_loaded", 2)
        w_loaded = ph.sems("w_loaded", 2)
        x_turned, x_hi, x_lo = ph.sem("x_turned"), ph.sem("x_hi"), ph.sem("x_lo")
        x_stored = ph.sems("x_stored", 2)
        w_his, w_los = ph.sem("w_his"), ph.sem("w_los")
        tables_in, table_step, angles, tables = ph.sem("tables_in"), ph.sem("table_step"), ph.sems("angles", 2), ph.sem("tables")
        tmp = ph.sb("tmp", [P, NT, HALF])
        block = ph.block()

        @block.gpsimd
        def _(pool):
            with nc.allow_non_contiguous_dma("one position a partition"):
                pool.dma_start(pos_i[:], positions.rearrange("b (t p) -> p (b t)", p=P)).then_inc(tables_in, 16)
            pool.dma_start(inv[:], inv_freq.to_broadcast([P, HALF])).then_inc(tables_in, 16)
            with pool.Fori(0, NT // 4) as i:
                for v in range(4):
                    u, t = v % 2, 4 * i + v
                    pool.wait_ge(x_turned, t + 1)
                    pool.dma_start(x_in[:, u, :], x[0, bass.ts(t, P), :]).then_inc(x_loaded[u], 16)
                    if v % 2 == 0:
                        w, k = v // 2, 2 * i + v // 2
                        pool.wait_ge(w_los, k + 1)
                        pool.dma_start(raw[:, w, :], w_in[0, bass.ts(k, P), 0:QKV]).then_inc(w_loaded[w], 16)

        @block.tensor
        def _(pe):
            pe.sem_inc(x_turned, 2)
            with pe.Fori(0, NT // 4) as i:
                for v in range(4):
                    u, t = v % 2, 4 * i + v
                    pe.wait_ge(x_loaded[u], 16 * (2 * i + v // 2 + 1))
                    pe.wait_ge(x_hi, t + 1)
                    pe.wait_ge(x_lo, t + 1)
                    for k in range(KD):
                        last = nc.tensor.transpose(psx[:, u, bass.ts(k, P)], x_in[:, u, bass.ts(k, P)], ident[:])
                    last.then_inc(x_turned, 1)

        @block.scalar
        def _(act):
            act.sem_inc(x_hi, 2)
            with act.Fori(0, NT // 4) as i:
                for v in range(4):
                    u, t = v % 2, 4 * i + v
                    act.wait_ge(x_turned, t + 3)
                    act.wait_ge(x_stored[u], 32 * (2 * i + v // 2 + 1))
                    nc.scalar.activation(xh[:, u, :], psx[:, u, :], ACT.Copy).then_inc(x_hi, 1)
                    if v % 2 == 0:
                        w, k = v // 2, 2 * i + v // 2
                        act.wait_ge(w_loaded[w], 16 * (i + 1))
                        nc.scalar.activation(w_hi[:, bass.ds(k, 1), 0:QKV], raw[:, w:w + 1, :], ACT.Copy).then_inc(w_his, 1)
            for n, (table, reduced) in enumerate(((sin_t, red), (cos_t, turns))):
                act.wait_ge(angles[n], 1)
                nc.scalar.activation(table[:], reduced[:], ACT.Sin).then_inc(tables, 1)
            act.wait_ge(tables, 2)
            nc.scalar.activation(nsin_t[:], sin_t[:], ACT.Copy, scale=-1.0).then_inc(tables, 1)
            act.wait_ge(tables, 3)

        @block.vector
        def _(dve):
            steps = [0]

            def link(ins):
                steps[0] += 1
                ins.then_inc(table_step, 1)
                dve.wait_ge(table_step, steps[0])

            dve.sem_inc(x_lo, 2)
            dve.sem_inc(w_los, 2)
            with dve.Fori(0, NT // 4) as i:
                for v in range(4):
                    u, t = v % 2, 4 * i + v
                    dve.wait_ge(x_hi, t + 3)
                    nc.vector.tensor_tensor(xl[:, u, :], psx[:, u, :], f(xh[:, u, :]), ALU.subtract).then_inc(x_lo, 1)
                    if v % 2 == 0:
                        w, k = v // 2, 2 * i + v // 2
                        dve.wait_ge(w_his, k + 1)
                        nc.vector.tensor_tensor(w_lo[:, bass.ds(k, 1), 0:QKV], raw[:, w:w + 1, :],
                                                f(w_hi[:, bass.ds(k, 1), 0:QKV]), ALU.subtract).then_inc(w_los, 1)
            dve.wait_ge(tables_in, 32)
            link(nc.vector.tensor_copy(pos_f[:], pos_i[:]))
            link(nc.vector.tensor_tensor(ang[:], pos_f[:].unsqueeze(2).to_broadcast([P, NT, HALF]),
                                         inv[:].unsqueeze(1).to_broadcast([P, NT, HALF]), ALU.mult))
            for n, out in enumerate((red, turns)):
                link(nc.vector.tensor_scalar(out[:], ang[:], 1.0 / two_pi, 0.25 * n, ALU.mult, ALU.add))
                link(nc.vector.tensor_copy(turns_i[:], out[:]))
                link(nc.vector.tensor_copy(out[:], turns_i[:]))
                link(nc.vector.scalar_tensor_tensor(tmp[:], out[:], -c1, ang[:], ALU.mult, ALU.add))
                link(nc.vector.scalar_tensor_tensor(tmp[:], out[:], -c2, tmp[:], ALU.mult, ALU.add))
                link(nc.vector.scalar_tensor_tensor(tmp[:], out[:], -c3, tmp[:], ALU.mult, ALU.add))
                link(nc.vector.tensor_scalar(tmp[:], tmp[:], 0.5 * math.pi * n, None, ALU.add))
                link(nc.vector.tensor_scalar(out[:], tmp[:], math.pi, -two_pi, ALU.is_gt, ALU.mult))
                link(nc.vector.tensor_tensor(tmp[:], tmp[:], out[:], ALU.add))
                link(nc.vector.tensor_scalar(out[:], tmp[:], -math.pi, two_pi, ALU.is_lt, ALU.mult))
                link(nc.vector.tensor_tensor(tmp[:], tmp[:], out[:], ALU.add))
                link(nc.vector.tensor_scalar(tmp[:], tmp[:], PI_IN, None, ALU.min))
                nc.vector.tensor_scalar(out[:], tmp[:], -PI_IN, None, ALU.max).then_inc(angles[n], 1)

        @block.sync
        def _(sp):
            for u in range(2):
                sp.sem_inc(x_stored[u], 32)
            with sp.Fori(0, NT // 4) as i:
                for v in range(4):
                    u, t = v % 2, 4 * i + v
                    sp.wait_ge(x_lo, t + 3)
                    sp.dma_start(xt_hi[bass.ds(t, 1)], f(xh[:, u, :])).then_inc(x_stored[u], 16)
                    sp.dma_start(xt_lo[bass.ds(t, 1)], f(xl[:, u, :])).then_inc(x_stored[u], 16)
            for u in range(2):
                sp.wait_ge(x_stored[u], 32 * (NT // 2 + 1))


def project_phase(nc, w_hi, w_lo, cos_t, sin_t, nsin_t, ident, xt_hi, xt_lo, qk_hi, qk_lo, v_hi, v_lo):
    with Phase(nc, "j") as ph:
        xh = ph.sb("xh", [P, 2, D], F32R)
        xl = ph.sb("xl", [P, 2, D], F32R)
        by_cos = ph.sb("by_cos", [P, 2, BANK])
        by_sin = ph.sb("by_sin", [P, 2, BANK])
        turned = ph.sb("turned", [P, 2, BANK])
        qkh = ph.sb("qkh", [P, NPIECE, P], F32R)
        qkl = ph.sb("qkl", [P, NPIECE, P], F32R)
        vh = ph.sb("vh", [P, VW], F32R)
        vl = ph.sb("vl", [P, VW], F32R)
        pg = [ph.ps(f"pg{j}", [P, BANK]) for j in range(5)]
        pt = [ph.ps(f"pt{j}", [P, BANK]) for j in range(2)]
        x_loaded = ph.sems("x_loaded", 2)
        product = ph.sems("product", 5)
        v_hi_done, v_lo_done = ph.sem("v_hi_done"), ph.sem("v_lo_done")
        scaled, rotated = ph.sem("scaled"), ph.sem("rotated")
        transposed, qk_hi_done, qk_lo_done = ph.sem("transposed"), ph.sem("qk_hi_done"), ph.sem("qk_lo_done")
        stored = ph.sem("stored")
        block = ph.block()
        ROT = [j for j, g in enumerate(GROUPS) if g[1]]
        VOFF = {1: 0, 4: A_K}

        @block.sync
        def _(sp):
            with sp.Fori(0, NT // 2) as i:
                for u in range(2):
                    t = 2 * i + u
                    sp.wait_ge(product[4], t + 1)
                    sp.dma_start(f(xh[:, u, :]), xt_hi[bass.ds(t, 1)]).then_inc(x_loaded[u], 16)
                    sp.dma_start(f(xl[:, u, :]), xt_lo[bass.ds(t, 1)]).then_inc(x_loaded[u], 16)

        @block.tensor
        def _(pe):
            pe.sem_inc(product[4], 2)
            pe.sem_inc(transposed, 2)

            def group(i, u, j):
                t = 2 * i + u
                c0, rot, v = GROUPS[j]
                if v:
                    pe.wait_ge(v_lo_done, 2 * t + (1 if j == 1 else 2))
                if rot:
                    pe.wait_ge(scaled, 4 * t + ROT.index(j) + 1)
                for k in range(KD):
                    ks, cs = slice(k * P, (k + 1) * P), slice(c0, c0 + rot + v)
                    out = pg[j][:, 0:rot + v]
                    nc.tensor.matmul(out, xh[:, u, ks], w_hi[:, k, cs], start=(k == 0), stop=False)
                    nc.tensor.matmul(out, xl[:, u, ks], w_hi[:, k, cs], start=False, stop=False)
                    last = nc.tensor.matmul(out, xh[:, u, ks], w_lo[:, k, cs], start=False, stop=(k == KD - 1))
                last.then_inc(product[j], 1)

            def turn(i, u, r):
                n = 4 * (2 * i + u) + r
                pe.wait_ge(rotated, n + 3)
                pe.wait_ge(qk_lo_done, n + 1)
                for c in range(GROUPS[ROT[r]][1] // P):
                    last = nc.tensor.transpose(pt[r % 2][:, c * P:(c + 1) * P], turned[:, r % 2, c * P:(c + 1) * P], ident[:])
                last.then_inc(transposed, 1)

            with pe.Fori(0, NT // 2) as i:
                for u in range(2):
                    pe.wait_ge(x_loaded[u], 32 * (i + 1))
                    group(i, u, 0)
                    group(i, u, 1)
                    group(i, u, 2)
                    turn(i, u, 0)
                    group(i, u, 3)
                    turn(i, u, 1)
                    turn(i, u, 2)
                    group(i, u, 4)
                    turn(i, u, 3)

        @block.gpsimd
        def _(pool):
            pool.sem_inc(rotated, 2)
            with pool.Fori(0, NT) as t:
                for r in range(4):
                    n, w = 4 * t + r, GROUPS[ROT[r]][1]
                    pool.wait_ge(scaled, n + 5)
                    pool.wait_ge(transposed, n + 1)
                    nc.gpsimd.tensor_tensor(turned[:, r % 2, 0:w], by_cos[:, r % 2, 0:w], by_sin[:, r % 2, 0:w],
                                            ALU.add).then_inc(rotated, 1)

        @block.scalar
        def _(act):
            act.sem_inc(stored, 64)
            with act.Fori(0, NT) as t:
                def pieces(r):
                    w = GROUPS[ROT[r]][1]
                    act.wait_ge(transposed, 4 * t + r + 3)
                    out = qkh[:, PIECE0[r]:PIECE0[r] + w // P, :].rearrange("p c n -> p (c n)")
                    nc.scalar.activation(out, pt[r % 2][:, 0:w], ACT.Copy).then_inc(qk_hi_done, 1)

                def v_part(j):
                    _, rot, v = GROUPS[j]
                    act.wait_ge(product[j], t + (3 if j == 4 else 1))
                    nc.scalar.activation(vh[:, VOFF[j]:VOFF[j] + v], pg[j][:, rot:rot + v], ACT.Copy).then_inc(v_hi_done, 1)

                act.wait_ge(stored, 64 * (t + 1))
                v_part(1)
                pieces(0)
                pieces(1)
                pieces(2)
                v_part(4)
                pieces(3)
                act.wait_ge(v_lo_done, 2 * t + 4)
                act.wait_ge(qk_lo_done, 4 * t + 6)
                cols = bass.ts(t, P)
                act.dma_start(qk_hi[:, :, cols].rearrange("c p n -> p c n"), f(qkh[:])).then_inc(stored, 16)
                act.dma_start(qk_lo[:, :, cols].rearrange("c p n -> p c n"), f(qkl[:])).then_inc(stored, 16)
                act.dma_start(v_hi[bass.ds(t, 1)].rearrange("a p n -> p (a n)"), f(vh[:])).then_inc(stored, 16)
                act.dma_start(v_lo[bass.ds(t, 1)].rearrange("a p n -> p (a n)"), f(vl[:])).then_inc(stored, 16)
            act.wait_ge(stored, 64 * (NT + 1))

        @block.vector
        def _(dve):
            dve.sem_inc(scaled, 4)
            dve.sem_inc(v_lo_done, 2)
            dve.sem_inc(qk_lo_done, 2)
            with dve.Fori(0, NT) as t:
                def rotate(r):
                    j = ROT[r]
                    w, b = GROUPS[j][1], r % 2
                    n = w // HD
                    dve.wait_ge(product[j], t + 1)
                    if j == 1:
                        dve.wait_ge(v_hi_done, 2 * t + 1)
                    dve.wait_ge(rotated, 4 * t + r + 1)
                    src = pg[j][:, 0:w].rearrange("p (h s d) -> p h s d", h=n, s=2)
                    out = by_sin[:, b, 0:w].rearrange("p (h s d) -> p h s d", h=n, s=2)
                    nc.vector.tensor_tensor(by_cos[:, b, 0:w].rearrange("p (h d) -> p h d", d=HALF),
                                            pg[j][:, 0:w].rearrange("p (h d) -> p h d", d=HALF),
                                            cos_t[:, bass.ds(t, 1), :].to_broadcast([P, 2 * n, HALF]), ALU.mult)
                    nc.vector.tensor_tensor(out[:, :, 0, :], src[:, :, 1, :],
                                            nsin_t[:, bass.ds(t, 1), :].to_broadcast([P, n, HALF]), ALU.mult)
                    last = nc.vector.tensor_tensor(out[:, :, 1, :], src[:, :, 0, :],
                                                   sin_t[:, bass.ds(t, 1), :].to_broadcast([P, n, HALF]), ALU.mult)
                    last.then_inc(scaled, 1)

                def low_v(j):
                    _, rot, v = GROUPS[j]
                    dve.wait_ge(v_hi_done, 2 * t + (1 if j == 1 else 2))
                    at = slice(VOFF[j], VOFF[j] + v)
                    nc.vector.tensor_tensor(vl[:, at], pg[j][:, rot:rot + v], f(vh[:, at]), ALU.subtract).then_inc(v_lo_done, 1)

                def low(r):
                    w = GROUPS[ROT[r]][1]
                    dve.wait_ge(qk_hi_done, 4 * t + r + 1)
                    at = slice(PIECE0[r], PIECE0[r] + w // P)
                    nc.vector.tensor_tensor(qkl[:, at, :].rearrange("p c n -> p (c n)"), pt[r % 2][:, 0:w],
                                            f(qkh[:, at, :]).rearrange("p c n -> p (c n)"), ALU.subtract).then_inc(qk_lo_done, 1)

                dve.wait_ge(stored, 64 * (t + 1))
                rotate(0)
                rotate(1)
                low_v(1)
                rotate(2)
                low(0)
                rotate(3)
                low(1)
                low(2)
                low_v(4)
                low(3)


def gates_phase(nc, w_in, b_gate, xt_hi, xt_lo, gates):
    with Phase(nc, "g") as ph:
        raw = ph.sb("raw", [P, 2, GATE])
        w_hi = ph.sb("w_hi", [P, KD, GATE], F32R)
        w_lo = ph.sb("w_lo", [P, KD, GATE], F32R)
        xh = ph.sb("xh", [P, 2, D], F32R)
        xl = ph.sb("xl", [P, 2, D], F32R)
        bias = ph.sb("bias", [P, GATE])
        out = ph.sb("out", [P, GATE])
        pg = [ph.ps(f"pg{j}", [P, BANK]) for j in range(8)]
        w_loaded, w_his, w_los = ph.sems("w_loaded", 2), ph.sem("w_his"), ph.sem("w_los")
        x_loaded, b_loaded = ph.sems("x_loaded", 2), ph.sem("b_loaded")
        product, biased, gated, stored = ph.sem("product"), ph.sem("biased"), ph.sem("gated"), ph.sem("stored")
        block = ph.block()
        NG4 = GATE // BANK

        @block.sync
        def _(sp):
            sp.dma_start(bias[:], b_gate.to_broadcast([P, GATE])).then_inc(b_loaded, 16)
            with sp.Fori(0, KD // 2) as i:
                for w in range(2):
                    k = 2 * i + w
                    sp.wait_ge(w_los, k + 1)
                    sp.dma_start(raw[:, w, :], w_in[0, bass.ts(k, P), QKV:QKV + GATE]).then_inc(w_loaded[w], 16)
            with sp.Fori(0, NT // 2) as i:
                for u in range(2):
                    t = 2 * i + u
                    sp.wait_ge(product, NG4 * t + NG4)
                    sp.dma_start(f(xh[:, u, :]), xt_hi[bass.ds(t, 1)]).then_inc(x_loaded[u], 16)
                    sp.dma_start(f(xl[:, u, :]), xt_lo[bass.ds(t, 1)]).then_inc(x_loaded[u], 16)

        @block.tensor
        def _(pe):
            pe.sem_inc(product, 2 * NG4)
            with pe.Fori(0, NT // 2) as i:
                for u in range(2):
                    t = 2 * i + u
                    pe.wait_ge(x_loaded[u], 32 * (i + 1))
                    for j in range(NG4):
                        pe.wait_ge(biased, NG4 * t + j + 1)
                        bank = pg[4 * u + j]
                        for k in range(KD):
                            if u == 0 and j == 0:
                                pe.wait_ge(w_los, 3 + k)
                            ks, cs = slice(k * P, (k + 1) * P), slice(j * BANK, (j + 1) * BANK)
                            nc.tensor.matmul(bank[:], xh[:, u, ks], w_hi[:, k, cs], start=(k == 0), stop=False)
                            nc.tensor.matmul(bank[:], xl[:, u, ks], w_hi[:, k, cs], start=False, stop=False)
                            last = nc.tensor.matmul(bank[:], xh[:, u, ks], w_lo[:, k, cs], start=False, stop=(k == KD - 1))
                        last.then_inc(product, 1)

        @block.vector
        def _(dve):
            dve.sem_inc(w_los, 2)
            dve.sem_inc(biased, 2 * NG4)
            with dve.Fori(0, KD) as k:
                dve.wait_ge(w_his, k + 1)
                nc.vector.tensor_tensor(w_lo[:, bass.ds(k, 1), :], raw[:, bass.ds(k % 2, 1), :],
                                        f(w_hi[:, bass.ds(k, 1), :]), ALU.subtract).then_inc(w_los, 1)
            dve.wait_ge(b_loaded, 16)
            with dve.Fori(0, NT // 2) as i:
                for u in range(2):
                    for j in range(NG4):
                        t = 2 * i + u
                        dve.wait_ge(product, NG4 * t + j + 1 + 2 * NG4)
                        if j == 0:
                            dve.wait_ge(stored, 16 * (t + 1))
                        at = slice(j * BANK, (j + 1) * BANK)
                        nc.vector.tensor_tensor(out[:, at], pg[4 * u + j][:], bias[:, at], ALU.add).then_inc(biased, 1)

        @block.scalar
        def _(act):
            act.sem_inc(stored, 16)
            with act.Fori(0, KD // 2) as i:
                for w in range(2):
                    k = 2 * i + w
                    act.wait_ge(w_loaded[w], 16 * (i + 1))
                    nc.scalar.activation(w_hi[:, bass.ds(k, 1), :], raw[:, w:w + 1, :], ACT.Copy).then_inc(w_his, 1)
            with act.Fori(0, NT) as t:
                act.wait_ge(biased, NG4 * t + 3 * NG4)
                nc.scalar.activation(out[:], out[:], ACT.Sigmoid).then_inc(gated, 1)
                act.wait_ge(gated, t + 1)
                act.dma_start(gates[bass.ts(t, P), :], out[:]).then_inc(stored, 16)
            act.wait_ge(stored, 16 * (NT + 1))


def window_attention_phase(nc, sinks, ident, qk_hi, qk_lo, v_hi, v_lo, oa):
    W = CHUNK + P
    GH = A_HEADS // A_KV
    with Phase(nc, "a") as ph:
        qs = ph.sb("qs", [P, 2, A_HEADS, P], F32R)
        kh = ph.sb("kh", [P, 2, A_KV, W], F32R)
        kl = ph.sb("kl", [P, 2, A_KV, W], F32R)
        vph = ph.sb("vph", [CHUNK, 2, A_K], F32R)
        vpl = ph.sb("vpl", [CHUNK, 2, A_K], F32R)
        vch = ph.sb("vch", [P, 2, A_K], F32R)
        vcl = ph.sb("vcl", [P, 2, A_K], F32R)
        pr = ph.sb("pr", [P, A_HEADS, W])
        tph = ph.sb("tph", [CHUNK, A_HEADS, P], F32R)
        tpl = ph.sb("tpl", [CHUNK, A_HEADS, P], F32R)
        tch = ph.sb("tch", [P, A_HEADS, P], F32R)
        tcl = ph.sb("tcl", [P, A_HEADS, P], F32R)
        o = ph.sb("o", [P, A_Q])
        sink = ph.sb("sink", [P, A_HEADS])
        mx, m, nb, se, den, inv = (ph.sb(n, [P, A_HEADS]) for n in ("mx", "m", "nb", "se", "den", "inv"))
        sums = ph.sb("sums", [P, A_HEADS])
        diff = ph.sb("diff", [P, A_HEADS])
        mask_f = ph.sb("mask_f", [P, P + 2 * W])
        mask = ph.sb("mask", [P, P + 2 * W], F32R)
        bank = ph.ps("s", [P, 4, BANK])
        tp = ph.ps("tp", [CHUNK, GH, P])
        tc = ph.ps("tc", [P, GH, P])
        po = ph.ps("o_", [P, A_Q])
        loaded = ph.sems("loaded", 2)
        mask_step, sink_in = ph.sem("mask_step"), ph.sem("sink_in")
        scores, chain, exped, sunk = ph.sem("scores"), ph.sem("chain"), ph.sem("exped"), ph.sem("sunk")
        turned, t_hi, t_lo, pv, scaled, stored = (ph.sem(n) for n in ("turned", "t_hi", "t_lo", "pv", "scaled", "stored"))
        block = ph.block()
        CH = 5

        def score(hd):
            return bank[:, hd // 2, (hd % 2) * W:(hd % 2 + 1) * W]

        @block.sync
        def _(sp):
            sp.dma_start(sink[:], sinks.to_broadcast([P, A_HEADS])).then_inc(sink_in, 16)

            def load(u, t, prev_cols, prev_tile, prev_rows):
                cols = bass.ts(t, P)
                for half, src in ((0, qk_hi), (1, qk_lo)):
                    rows = slice(half * HD, (half + 1) * HD)
                    sp.dma_start(f(qs[rows, u]), src[0:4, :, cols].rearrange("c (b p) n -> p (c b) n", b=2)).then_inc(loaded[u], 16)
                    for dst, ksrc in ((kh, qk_hi), (kl, qk_lo)):
                        k = ksrc[4].rearrange("(g p) n -> p g n", g=A_KV)
                        sp.dma_start(f(dst[rows, u, :, 0:CHUNK]), k[:, :, prev_cols]).then_inc(loaded[u], 16)
                        sp.dma_start(f(dst[rows, u, :, CHUNK:W]), k[:, :, cols]).then_inc(loaded[u], 16)
                for dp, dc, src in ((vph, vch, v_hi), (vpl, vcl, v_lo)):
                    sp.dma_start(f(dp[:, u, :]), src[prev_tile, prev_rows, 0:A_K].rearrange("a p n -> p (a n)")).then_inc(loaded[u], 16)
                    sp.dma_start(f(dc[:, u, :]), src[bass.ds(t, 1), :, 0:A_K].rearrange("a p n -> p (a n)")).then_inc(loaded[u], 16)

            load(0, 0, slice(0, CHUNK), slice(0, 1), slice(0, CHUNK))
            load(1, 1, slice(CHUNK, P), slice(0, 1), slice(CHUNK, P))
            with sp.Fori(1, NT // 2) as i:
                for u in range(2):
                    t = 2 * i + u
                    sp.wait_ge(pv, t - 1)
                    load(u, t, bass.ds(t * P - CHUNK, CHUNK), bass.ds(t - 1, 1), slice(CHUNK, P))

        @block.gpsimd
        def _(pool):
            nc.gpsimd.memset(mask_f[:], 0.0).then_inc(mask_step, 1)
            pool.wait_ge(mask_step, 1)
            nc.gpsimd.memset(mask_f[0:1, 0:CHUNK], 1.0).then_inc(mask_step, 1)
            nc.gpsimd.memset(mask_f[32:33, CHUNK:P], 1.0).then_inc(mask_step, 1)
            for first in range(2):
                m0 = P + W * first
                nc.gpsimd.memset(mask_f[0:1, m0 + P:m0 + W], NEG).then_inc(mask_step, 1)
                nc.gpsimd.memset(mask_f[32:33, m0:m0 + CHUNK], NEG).then_inc(mask_step, 1)
            nc.gpsimd.memset(mask_f[0:1, P + W:P + W + CHUNK], NEG).then_inc(mask_step, 1)

        @block.tensor
        def _(pe):
            pe.wait_ge(mask_step, 9)

            def scores_of(t, u, first):
                pe.wait_ge(exped, A_HEADS * t + 1)
                for hd in range(A_HEADS):
                    q, g = qs[:, u, hd, :], hd // GH
                    nc.tensor.matmul(score(hd), q, kh[:, u, g, :], start=True, stop=False)
                    nc.tensor.matmul(score(hd), q, kl[:, u, g, :], start=False, stop=False)
                    m0 = P + W * first
                    last = nc.tensor.matmul(score(hd), mask[:, 0:P], mask[:, m0:m0 + W], start=False, stop=True)
                last.then_inc(scores, 1)

            def values_of(t, u):
                pe.wait_ge(exped, A_HEADS * (t + 1) + 1)
                for g in range(A_KV):
                    pe.wait_ge(t_lo, 2 * (2 * t + g) + 1)
                    for j in range(GH):
                        hd = GH * g + j
                        nc.tensor.transpose(tc[:, j, :], pr[:, hd, CHUNK:W], ident[:])
                        last = nc.tensor.transpose(tp[:, j, :], pr[:, hd, 0:CHUNK], ident[:])
                    last.then_inc(turned, 1)
                pe.wait_ge(scaled, t + 1)
                for g in range(A_KV):
                    pe.wait_ge(t_lo, 2 * (2 * t + g + 1) + 1)
                    vs = slice(g * HD, (g + 1) * HD)
                    for j in range(GH):
                        hd = GH * g + j
                        out = po[:, hd * HD:(hd + 1) * HD]
                        nc.tensor.matmul(out, tch[:, hd, :], vch[:, u, vs], start=True, stop=False)
                        nc.tensor.matmul(out, tcl[:, hd, :], vch[:, u, vs], start=False, stop=False)
                        nc.tensor.matmul(out, tch[:, hd, :], vcl[:, u, vs], start=False, stop=False)
                        nc.tensor.matmul(out, tph[:, hd, :], vph[:, u, vs], start=False, stop=False)
                        nc.tensor.matmul(out, tpl[:, hd, :], vph[:, u, vs], start=False, stop=False)
                        last = nc.tensor.matmul(out, tph[:, hd, :], vpl[:, u, vs], start=False, stop=True)
                last.then_inc(pv, 1)

            def tile(t, i, u, first):
                pe.wait_ge(loaded[u], 14 * 16 * (i + 1))
                scores_of(t, u, first)
                values_of(t, u)

            tile(0, 0, 0, 1)
            tile(1, 0, 1, 0)
            with pe.Fori(1, NT // 2) as i:
                for u in range(2):
                    tile(2 * i + u, i, u, 0)

        @block.scalar
        def _(act):
            act.sem_inc(exped, 1)
            act.sem_inc(stored, 16)
            with act.Fori(0, NT) as t:
                act.wait_ge(chain, CH * t + 3)
                for hd in range(A_HEADS):
                    nc.scalar.activation(pr[:, hd, :], score(hd), ACT.Exp, bias=nb[:, hd:hd + 1], scale=SCALE,
                                         accum_out=sums[:, hd:hd + 1]).then_inc(exped, 1)
                nc.scalar.activation(se[:], diff[:], ACT.Exp).then_inc(sunk, 1)
                for g in range(A_KV):
                    act.wait_ge(turned, A_KV * t + g + 1)
                    hs = slice(GH * g, GH * (g + 1))
                    nc.scalar.activation(tph[:, hs, :], tp[:], ACT.Copy).then_inc(t_hi, 1)
                    nc.scalar.activation(tch[:, hs, :], tc[:], ACT.Copy).then_inc(t_hi, 1)
                act.wait_ge(scaled, t + 2)
                act.dma_start(oa[bass.ts(t, P), :], o[:]).then_inc(stored, 16)
            act.wait_ge(stored, 16 * (NT + 1))

        @block.vector
        def _(dve):
            dve.sem_inc(t_lo, 1)
            dve.sem_inc(scaled, 1)
            dve.wait_ge(mask_step, 8)
            nc.vector.tensor_copy(mask[:], mask_f[:]).then_inc(mask_step, 1)
            dve.wait_ge(sink_in, 16)
            with dve.Fori(0, NT) as t:
                step = [0]

                def link(ins):
                    step[0] += 1
                    ins.then_inc(chain, 1)
                    dve.wait_ge(chain, CH * t + step[0])

                dve.wait_ge(scores, t + 1)
                nc_in = bank[:, :, 0:2 * W].rearrange("p a (b w) -> p a b w", b=2)
                nc_out = mx[:].rearrange("p (a b) -> p a b", b=2)
                dve_in = nc.vector.tensor_reduce(nc_out, nc_in, axis=AX.X, op=ALU.max)
                link(dve_in)
                link(nc.vector.scalar_tensor_tensor(m[:], mx[:], SCALE, sink[:], ALU.mult, ALU.max))
                nc.vector.tensor_tensor(diff[:], sink[:], m[:], ALU.subtract)
                link(nc.vector.tensor_scalar(nb[:], m[:], -1.0, None, ALU.mult))
                dve.wait_ge(exped, A_HEADS * (t + 1) + 1)
                dve.wait_ge(sunk, t + 1)
                link(nc.vector.tensor_tensor(den[:], sums[:], se[:], ALU.add))
                link(nc.vector.reciprocal(inv[:], den[:]))
                for g in range(A_KV):
                    hs = slice(GH * g, GH * (g + 1))
                    dve.wait_ge(t_hi, 2 * (A_KV * t + g + 1))
                    nc.vector.tensor_tensor(tpl[:, hs, :], tp[:], f(tph[:, hs, :]), ALU.subtract).then_inc(t_lo, 1)
                    nc.vector.tensor_tensor(tcl[:, hs, :], tc[:], f(tch[:, hs, :]), ALU.subtract).then_inc(t_lo, 1)
                dve.wait_ge(pv, t + 1)
                dve.wait_ge(stored, 16 * (t + 1))
                (nc.vector.tensor_tensor(o[:].rearrange("p (h d) -> p h d", h=A_HEADS),
                                             po[:].rearrange("p (h d) -> p h d", h=A_HEADS),
                                             inv[:].unsqueeze(2).to_broadcast([P, A_HEADS, HD]), ALU.mult)).then_inc(scaled, 1)


def diff_attention_phase(nc, lambdas, ident, qk_hi, qk_lo, v_hi, v_lo, ob):
    MAPS = 2
    NQ = SEQ // P
    NCH = SEQ // BANK
    chunks = [[(m, c) for m in range(MAPS) for c in range((i * P + P + BANK - 1) // BANK)] for i in range(NQ)]
    before = [sum(len(x) for x in chunks[:i]) for i in range(NQ + 1)]
    SB = before[NQ]
    GB = SB // 2
    with Phase(nc, "b") as ph:
        qs = ph.sb("qs", [P, MAPS, SEQ], F32R)
        kh = ph.sb("kh", [P, MAPS, SEQ], F32R)
        kl = ph.sb("kl", [P, MAPS, SEQ], F32R)
        vh = ph.sb("vh", [P, NT, BV], F32R)
        vl = ph.sb("vl", [P, NT, BV], F32R)
        sc = ph.sb("sc", [P, 2, MAPS, SEQ])
        at = ph.sb("at", [P, SEQ])
        th = ph.sb("th", [P, SEQ], F32R)
        tl = ph.sb("tl", [P, SEQ], F32R)
        o = ph.sb("o", [P, 2, BV])
        mx = ph.sb("mx", [P, 2, MAPS, NCH])
        mall = ph.sb("mall", [P, 2, MAPS])
        nb = ph.sb("nb", [P, 2, MAPS])
        sums = ph.sb("sums", [P, 2, MAPS])
        inv = ph.sb("inv", [P, 2, MAPS])
        coef = ph.sb("coef", [P, 2])
        lam_in = ph.sb("lam_in", [P, 4, HD])
        lam_prod = ph.sb("lam_prod", [P, 2, HD])
        lam_sum = ph.sb("lam_sum", [P, 2])
        lam_exp = ph.sb("lam_exp", [P, 2])
        neg_lam = ph.sb("neg_lam", [P, 1])
        mask_f = ph.sb("mask_f", [P, 2, P])
        mask = ph.sb("mask", [P, 2, P], F32R)
        bank = [ph.ps(f"s{j}", [P, BANK]) for j in range(4)]
        pt = [ph.ps(f"t{j}", [P, BANK]) for j in range(2)]
        po = [ph.ps(f"o{j}", [P, BV]) for j in range(2)]
        qk_loaded, v_loaded = ph.sems("qk_loaded", NCH), ph.sems("v_loaded", NCH)
        scores, copied, biased, exped = ph.sem("scores"), ph.sem("copied"), ph.sem("biased"), ph.sem("exped")
        combined, turned, t_hi, t_lo = ph.sem("combined"), ph.sem("turned"), ph.sem("t_hi"), ph.sem("t_lo")
        pv, scaled, stored = ph.sem("pv"), ph.sem("scaled"), ph.sems("stored", 2)
        lam_loaded, lam_step, lam_ready, mask_step = ph.sem("lam_loaded"), ph.sem("lam_step"), ph.sem("lam_ready"), ph.sem("mask_step")
        maxed, inverted, coefed = ph.sem("maxed"), ph.sem("inverted"), ph.sem("coefed")
        block = ph.block()

        @block.sync
        def _(sp):
            for n, lam in enumerate(lambdas):
                sp.dma_start(lam_in[:, n, :], lam.to_broadcast([P, HD])).then_inc(lam_loaded, 16)
            with sp.Fori(0, B_HEADS) as h:
                sp.wait_ge(scores, SB * h + 1)
                for c in range(NCH):
                    cols = slice(c * BANK, (c + 1) * BANK)

                    def part(src, piece):
                        return src[bass.ds(h + piece, 1), :, cols].rearrange("a (m p) n -> p (a m) n", m=MAPS)

                    for half, q_src in ((0, qk_hi), (1, qk_lo)):
                        at_ = slice(half * HD, (half + 1) * HD)
                        sp.dma_start(f(qs[at_, :, cols]), part(q_src, 5)).then_inc(qk_loaded[c], 16)
                        sp.dma_start(f(kh[at_, :, cols]), part(qk_hi, 9)).then_inc(qk_loaded[c], 16)
                        sp.dma_start(f(kl[at_, :, cols]), part(qk_lo, 9)).then_inc(qk_loaded[c], 16)
                sp.wait_ge(pv, NQ * h + 1)
                for c in range(NCH):
                    ts = slice(4 * c, 4 * c + 4)
                    vc = bass.ds(h * BV + A_K, BV)
                    sp.dma_start(f(vh[:, ts, :]), v_hi[ts, :, vc].rearrange("t p n -> p t n")).then_inc(v_loaded[c], 16)
                    sp.dma_start(f(vl[:, ts, :]), v_lo[ts, :, vc].rearrange("t p n -> p t n")).then_inc(v_loaded[c], 16)

        @block.gpsimd
        def _(pool):
            nc.gpsimd.memset(mask_f[:], 0.0).then_inc(mask_step, 1)
            pool.wait_ge(mask_step, 1)
            nc.gpsimd.memset(mask_f[0:1, 0, 0:CHUNK], 1.0).then_inc(mask_step, 1)
            nc.gpsimd.memset(mask_f[0:1, 1, CHUNK:P], NEG).then_inc(mask_step, 1)
            with pool.Fori(0, B_HEADS) as h:
                for i in range(NQ):
                    pool.wait_ge(scaled, NQ * h + i + 3)
                    pool.dma_start(ob[i * P:(i + 1) * P, bass.ds(h * BV, BV)], o[:, i % 2, :]).then_inc(stored[i % 2], 16)
            for u in range(2):
                pool.wait_ge(stored[u], 16 * NQ * B_HEADS // 2)

        @block.tensor
        def _(pe):
            pe.sem_inc(scores, 1)
            pe.sem_inc(pv, 1)
            pe.wait_ge(mask_step, 4)

            def scores_of(h, i):
                for n, (m, c) in enumerate(chunks[i]):
                    n += before[i]
                    if m == 0 and i % 4 == 0 and c == i // 4:
                        pe.wait_ge(qk_loaded[c], 96 * (h + 1))
                    pe.wait_ge(copied, SB * h + n + 1)
                    c0, c1 = c * BANK, min((c + 1) * BANK, (i + 1) * P)
                    q = qs[:, m, i * P:(i + 1) * P]
                    out = bank[n % 4]
                    diag = c1 == (i + 1) * P
                    nc.tensor.matmul(out[:, 0:c1 - c0], q, kh[:, m, c0:c1], start=True, stop=False)
                    last = nc.tensor.matmul(out[:, 0:c1 - c0], q, kl[:, m, c0:c1], start=False, stop=not diag)
                    if diag:
                        last = nc.tensor.matmul(out[:, i * P - c0:c1 - c0], mask[:, 0, :], mask[:, 1, :], start=False, stop=True)
                    last.then_inc(scores, 1)

            def values_of(h, i):
                g0 = before[i] // 2
                pe.wait_ge(combined, NQ * h + i + 1)
                for g in range(len(chunks[i]) // 2):
                    pe.wait_ge(t_lo, GB * h + g0 + g + 1)
                    for b in range(4 * g, min(4 * g + 4, i + 1)):
                        last = nc.tensor.transpose(pt[(g0 + g) % 2][:, (b % 4) * P:(b % 4 + 1) * P], at[:, b * P:(b + 1) * P], ident[:])
                    last.then_inc(turned, 1)
                pe.wait_ge(scaled, NQ * h + i + 1)
                for b in range(i + 1):
                    if b % 4 == 0:
                        pe.wait_ge(t_lo, GB * h + g0 + b // 4 + 3)
                    if i % 4 == 0 and b == i:
                        pe.wait_ge(v_loaded[b // 4], 32 * (h + 1))
                    bs = slice(b * P, (b + 1) * P)
                    nc.tensor.matmul(po[i % 2][:], th[:, bs], vh[:, b, :], start=(b == 0), stop=False)
                    nc.tensor.matmul(po[i % 2][:], tl[:, bs], vh[:, b, :], start=False, stop=False)
                    last = nc.tensor.matmul(po[i % 2][:], th[:, bs], vl[:, b, :], start=False, stop=(b == i))
                last.then_inc(pv, 1)

            with pe.Fori(0, B_HEADS) as h:
                scores_of(h, 0)
                for i in range(NQ):
                    if i + 1 < NQ:
                        scores_of(h, i + 1)
                    values_of(h, i)

        @block.scalar
        def _(act):
            act.wait_ge(lam_step, 2)
            nc.scalar.activation(lam_exp[:], lam_sum[:], ACT.Exp).then_inc(lam_ready, 1)

            def exps(h, i):
                for m in range(MAPS):
                    act.wait_ge(biased, MAPS * (NQ * h + i) + m + 1)
                    L = (i + 1) * P
                    nc.scalar.activation(sc[:, i % 2, m, 0:L], sc[:, i % 2, m, 0:L], ACT.Exp, bias=nb[:, i % 2, m:m + 1],
                                         scale=SCALE, accum_out=sums[:, i % 2, m:m + 1]).then_inc(exped, 1)

            def high(h, i):
                g0 = before[i] // 2
                for g in range(len(chunks[i]) // 2):
                    act.wait_ge(turned, GB * h + g0 + g + 1)
                    c0, c1 = g * BANK, min((g + 1) * BANK, (i + 1) * P)
                    nc.scalar.activation(th[:, c0:c1], pt[(g0 + g) % 2][:, 0:c1 - c0], ACT.Copy).then_inc(t_hi, 1)

            with act.Fori(0, B_HEADS) as h:
                exps(h, 0)
                for i in range(NQ):
                    if i + 1 < NQ:
                        exps(h, i + 1)
                    high(h, i)

        @block.vector
        def _(dve):
            dve.sem_inc(copied, 4)
            dve.sem_inc(t_lo, 2)
            dve.wait_ge(mask_step, 3)
            nc.vector.tensor_copy(mask[:], mask_f[:]).then_inc(mask_step, 1)
            dve.wait_ge(lam_loaded, 64)
            nc.vector.tensor_tensor(lam_prod[:], lam_in[:, 0:4:2, :], lam_in[:, 1:4:2, :], ALU.mult).then_inc(lam_step, 1)
            dve.wait_ge(lam_step, 1)
            nc.vector.reduce_sum(lam_sum[:], lam_prod[:], axis=AX.X).then_inc(lam_step, 1)
            dve.wait_ge(lam_ready, 1)
            nc.vector.tensor_tensor(neg_lam[:], lam_exp[:, 1:2], lam_exp[:, 0:1], ALU.subtract).then_inc(lam_step, 1)
            dve.wait_ge(lam_step, 3)
            nc.vector.tensor_scalar(neg_lam[:], neg_lam[:], -LAM_INIT, None, ALU.add).then_inc(lam_step, 1)
            dve.wait_ge(lam_step, 4)
            dve.sem_inc(scaled, 2)

            def copies(h, i):
                u = i % 2
                for n, (m, c) in enumerate(chunks[i]):
                    n += before[i]
                    dve.wait_ge(scores, SB * h + n + 2)
                    c0, c1 = c * BANK, min((c + 1) * BANK, (i + 1) * P)
                    nc.vector.tensor_scalar(sc[:, u, m, c0:c1], bank[n % 4][:, 0:c1 - c0], 1.0, NEG, ALU.mult, ALU.max,
                                            accum_out=mx[:, u, m, c:c + 1]).then_inc(copied, 1)
                    if c1 == (i + 1) * P:
                        k = MAPS * (NQ * h + i) + m
                        dve.wait_ge(copied, SB * h + n + 5)
                        nc.vector.reduce_max(mall[:, u, m:m + 1], mx[:, u, m, 0:c + 1], axis=AX.X).then_inc(maxed, 1)
                        dve.wait_ge(maxed, k + 1)
                        nc.vector.tensor_scalar(nb[:, u, m:m + 1], mall[:, u, m:m + 1], -SCALE, None, ALU.mult).then_inc(biased, 1)

            def combine(h, i):
                u, L, k = i % 2, (i + 1) * P, NQ * h + i
                dve.wait_ge(exped, MAPS * (k + 1))
                nc.vector.reciprocal(inv[:, u, :], sums[:, u, :]).then_inc(inverted, 1)
                dve.wait_ge(inverted, k + 1)
                nc.vector.scalar_tensor_tensor(coef[:, u:u + 1], inv[:, u, 1:2], neg_lam[:], sums[:, u, 0:1],
                                               ALU.mult, ALU.mult).then_inc(coefed, 1)
                dve.wait_ge(coefed, k + 1)
                if i:
                    dve.wait_ge(turned, GB * h + before[i] // 2)
                nc.vector.scalar_tensor_tensor(at[:, 0:L], sc[:, u, 1, 0:L], coef[:, u:u + 1], sc[:, u, 0, 0:L],
                                               ALU.mult, ALU.add).then_inc(combined, 1)

            def low(h, i):
                g0 = before[i] // 2
                for g in range(len(chunks[i]) // 2):
                    dve.wait_ge(t_hi, GB * h + g0 + g + 1)
                    c0, c1 = g * BANK, min((g + 1) * BANK, (i + 1) * P)
                    nc.vector.tensor_tensor(tl[:, c0:c1], pt[(g0 + g) % 2][:, 0:c1 - c0], f(th[:, c0:c1]),
                                            ALU.subtract).then_inc(t_lo, 1)

            def finish(h, i):
                dve.wait_ge(pv, NQ * h + i + 2)
                if i >= 2:
                    dve.wait_ge(stored[i % 2], 16 * (NQ // 2 * h + i // 2))
                nc.vector.tensor_scalar(o[:, i % 2, :], po[i % 2][:], inv[:, i % 2, 0:1], None, ALU.mult).then_inc(scaled, 1)

            with dve.Fori(0, B_HEADS) as h:
                copies(h, 0)
                for i in range(NQ):
                    if i + 1 < NQ:
                        copies(h, i + 1)
                    combine(h, i)
                    if i:
                        finish(h, i - 1)
                    low(h, i)
                finish(h, NQ - 1)
                dve.wait_ge(stored[0], 16 * (NQ // 2) * (h + 1))
                dve.wait_ge(stored[1], 16 * (NQ // 2) * (h + 1))


def merge_phase(nc, ident, oa, ob, gates, x, subln_g, w_a, w_b, w_out, ln_g, ln_b, x1):
    KA, KB = A_Q // P, B_V // P
    KW = KA + KB + KD
    with Phase(nc, "m") as ph:
        w_hi = ph.sb("w_hi", [P, KW, D], F32R)
        w_lo = ph.sb("w_lo", [P, KW, D], F32R)
        gt = ph.sb("gt", [P, 2, GATE])
        xin = ph.sb("xin", [P, 2, D])
        oin = ph.sb("oin", [P, 2, A_Q + B_V])
        th = ph.sb("th", [P, 2, D], F32R)
        tl = ph.sb("tl", [P, 2, D], F32R)
        pa = ph.sb("pa", [P, D])
        pb = ph.sb("pb", [P, D])
        y = ph.sb("y", [P, 2, D])
        gam = ph.sb("gam", [P, D])
        bet = ph.sb("bet", [P, D])
        sg = ph.sb("sg", [P, BV])
        eps = ph.sb("eps", [P, 1])
        ss, rt, ri = (ph.sb(n, [P, B_HEADS]) for n in ("ss", "rt", "ri"))
        st = ph.sb("st", [P, 2, 6])
        mv = ph.sb("mv", [P, 2])
        sd, rs = ph.sb("sd", [P, 1]), ph.sb("rs", [P, 1])
        pt = ph.ps("pt", [P, D])
        psa, psb, psw = ph.ps("psa", [P, D]), ph.ps("psb", [P, D]), ph.ps("psw", [P, D])
        passed = ph.sem("passed")
        w_loaded, w_his, w_los = ph.sems("w_loaded", 2), ph.sem("w_his"), ph.sem("w_los")
        vec_in, vec_step = ph.sem("vec_in"), ph.sem("vec_step")
        loaded = ph.sems("loaded", 2)
        squared, rooted, normed, chain = (ph.sem(n) for n in ("squared", "rooted", "normed", "chain"))
        turned, t_hi, t_lo = ph.sem("turned"), ph.sem("t_hi"), ph.sem("t_lo")
        a_done, b_done, w_done = ph.sem("a_done"), ph.sem("b_done"), ph.sem("w_done")
        gated_a, gated_b, mixed, y_done = (ph.sem(n) for n in ("gated_a", "gated_b", "mixed", "y_done"))
        var_done, sd_done, centred, affine, stored = (ph.sem(n) for n in ("var_done", "sd_done", "centred", "affine", "stored"))
        out_step = ph.sem("out_step")
        block = ph.block()
        W2 = 2 * D

        @block.sync
        def _(sp):
            for src, dst in ((ln_g, gam), (ln_b, bet)):
                sp.dma_start(dst[:], src.to_broadcast([P, D])).then_inc(vec_in, 16)
            sp.dma_start(sg[:], subln_g.to_broadcast([P, BV])).then_inc(vec_in, 16)
            for n, (src, k) in enumerate([(w_a, 0), (w_a, 2), (w_b, 0), (w_b, 2), (w_out, 0), (w_out, 2), (w_out, 4), (w_out, 6)]):
                u = n % 2
                if n >= 2:
                    sp.wait_ge(w_los, n - 1)
                sp.dma_start(gt[:, u, :].rearrange("p (k n) -> p k n", k=2),
                             src[0, k * P:(k + 2) * P, :].rearrange("(k p) n -> p k n", p=P)).then_inc(w_loaded[u], 16)
            sp.wait_ge(w_los, KW // 2)

            def load(t, u):
                rows = bass.ts(t, P)
                sp.dma_start(oin[:, u, 0:A_Q], oa[rows, :]).then_inc(loaded[u], 16)
                sp.dma_start(oin[:, u, A_Q:], ob[rows, :]).then_inc(loaded[u], 16)
                sp.dma_start(gt[:, u, :], gates[rows, :]).then_inc(loaded[u], 16)
                sp.dma_start(xin[:, u, :], x[0, rows, :]).then_inc(loaded[u], 16)

            load(0, 0)
            load(1, 1)
            with sp.Fori(1, NT // 2) as i:
                for u in range(2):
                    t = 2 * i + u
                    sp.wait_ge(y_done, t)
                    load(t, u)

        @block.tensor
        def _(pe):
            def turn(src, n):
                pe.wait_ge(t_lo, n + 1)
                for k in range(KD):
                    last = nc.tensor.transpose(pt[:, k * P:(k + 1) * P], src[:, k * P:(k + 1) * P], ident[:])
                last.then_inc(turned, 1)

            def product(out, u, ks, w0, done):
                for j in range(D // BANK):
                    js = slice(j * BANK, (j + 1) * BANK)
                    for k in ks:
                        at, kw = slice(k * P, (k + 1) * P), w0 + k
                        nc.tensor.matmul(out[:, js], th[:, u, at], w_hi[:, kw, js], start=(k == ks[0]), stop=False)
                        nc.tensor.matmul(out[:, js], tl[:, u, at], w_hi[:, kw, js], start=False, stop=False)
                        last = nc.tensor.matmul(out[:, js], th[:, u, at], w_lo[:, kw, js], start=False, stop=(k == ks[-1]))
                last.then_inc(done, 1)

            A, B, W = range(0, KA), range(KA, KA + KB), range(KD)
            pe.wait_ge(w_los, KW // 2)
            with pe.Fori(0, NT // 2) as i:
                t0 = 2 * i

                def ab_turn(u):
                    pe.wait_ge(normed, t0 + u + 1)
                    turn(oin[:, u, :], 2 * t0 + u)

                def a_part(u):
                    pe.wait_ge(t_lo, 2 * t0 + u + 2)
                    pe.wait_ge(gated_a, t0 + u + 1)
                    product(psa, u, A, 0, a_done)

                def b_part(u):
                    pe.wait_ge(gated_b, t0 + u + 1)
                    product(psb, u, B, 0, b_done)

                def w_part(u):
                    pe.wait_ge(mixed, t0 + u + 1)
                    turn(oin[:, u, :], 2 * t0 + 2 + u)
                    pe.wait_ge(t_lo, 2 * t0 + 4 + u)
                    pe.wait_ge(y_done, t0 + u + 1)
                    product(psw, u, W, KA + KB, w_done)

                ab_turn(0)
                a_part(0)
                ab_turn(1)
                b_part(0)
                a_part(1)
                b_part(1)
                w_part(0)
                w_part(1)


        @block.scalar
        def _(act):
            for n in range(KW // 2):
                act.wait_ge(w_loaded[n % 2], 16 * (n // 2 + 1))
                nc.scalar.activation(w_hi[:, 2 * n:2 * n + 2, :].rearrange("p k n -> p (k n)"), gt[:, n % 2, :], ACT.Copy).then_inc(w_his, 1)
            act.wait_ge(vec_step, 2)
            act.sem_inc(stored, 16)
            with act.Fori(0, NT // 2) as i:
                t0 = 2 * i

                def root(u):
                    act.wait_ge(squared, t0 + u + 1)
                    nc.scalar.activation(rt[:], ss[:], ACT.Sqrt, bias=eps[:], scale=1.0 / BV).then_inc(rooted, 1)

                def high(u, n):
                    act.wait_ge(turned, n + 1)
                    nc.scalar.activation(th[:, u, :], pt[:], ACT.Copy).then_inc(t_hi, 1)

                def deviation(u):
                    act.wait_ge(var_done, t0 + u + 1)
                    nc.scalar.activation(sd[:], mv[:, 1:2], ACT.Sqrt, bias=eps[:]).then_inc(sd_done, 1)

                root(0)
                high(0, 2 * t0)
                root(1)
                high(1, 2 * t0 + 1)
                high(0, 2 * t0 + 2)
                high(1, 2 * t0 + 3)
                deviation(0)
                deviation(1)
                for u in range(2):
                    act.wait_ge(affine, t0 + u + 1)
                    act.dma_start(x1[bass.ts(t0 + u, P), :], y[:, u, :]).then_inc(stored, 16)
            act.wait_ge(stored, 16 * (NT + 1))

        @block.gpsimd
        def _(pool):
            nc.gpsimd.memset(eps[:], EPS).then_inc(vec_step, 1)
            pool.wait_ge(vec_in, 48)
            with pool.Fori(0, NT // 2) as i:
                def mix(u):
                    pool.wait_ge(gated_b, 2 * i + u + 2)
                    nc.gpsimd.tensor_tensor(oin[:, u, :], pa[:], pb[:], ALU.add).then_inc(mixed, 1)

                def finish(u):
                    t = 2 * i + u
                    pool.wait_ge(centred, t + 1)
                    nc.gpsimd.tensor_tensor(y[:, u, :], y[:, u, :], gam[:], ALU.mult).then_inc(out_step, 1)
                    pool.wait_ge(out_step, t + 1)
                    nc.gpsimd.tensor_tensor(y[:, u, :], y[:, u, :], bet[:], ALU.add).then_inc(affine, 1)

                mix(0)
                mix(1)
                finish(0)
                finish(1)

        @block.vector
        def _(dve):
            dve.sem_inc(t_lo, 1)
            for free in (gated_a, gated_b, y_done):
                dve.sem_inc(free, 1)
            for n in range(KW // 2):
                dve.wait_ge(w_his, n + 1)
                nc.vector.tensor_tensor(w_lo[:, 2 * n:2 * n + 2, :].rearrange("p k n -> p (k n)"), gt[:, n % 2, :],
                                        f(w_hi[:, 2 * n:2 * n + 2, :]).rearrange("p k n -> p (k n)"), ALU.subtract).then_inc(w_los, 1)
            dve.wait_ge(vec_in, 48)
            nc.vector.tensor_scalar(sg[:], sg[:], 1.0 - LAM_INIT, None, ALU.mult).then_inc(vec_step, 1)
            dve.wait_ge(vec_step, 2)
            STEPS = 5
            with dve.Fori(0, NT // 2) as i:
                t0 = 2 * i
                step = [0]

                def link(ins):
                    step[0] += 1
                    ins.then_inc(chain, 1)
                    dve.wait_ge(chain, 2 * STEPS * i + step[0])

                def heads(ap):
                    return ap.rearrange("p (h d) -> p h d", h=B_HEADS)

                def rms(u):
                    b = oin[:, u, A_Q:]
                    dve.wait_ge(loaded[u], 64 * (i + 1))
                    link(nc.vector.tensor_tensor(pb[:, 0:B_V], b, b, ALU.mult))
                    nc.vector.reduce_sum(ss[:], heads(pb[:, 0:B_V]), axis=AX.X).then_inc(squared, 1)
                    dve.wait_ge(rooted, t0 + u + 1)
                    link(nc.vector.reciprocal(ri[:], rt[:]))
                    link(nc.vector.tensor_tensor(heads(b), heads(b), ri[:].unsqueeze(2).to_broadcast([P, B_HEADS, BV]), ALU.mult))
                    nc.vector.tensor_tensor(heads(b), heads(b), sg[:].unsqueeze(1).to_broadcast([P, B_HEADS, BV]), ALU.mult).then_inc(normed, 1)

                def low(u, n):
                    dve.wait_ge(t_hi, n + 1)
                    nc.vector.tensor_tensor(tl[:, u, :], pt[:], f(th[:, u, :]), ALU.subtract).then_inc(t_lo, 1)

                def gate(u):
                    t = t0 + u
                    dve.wait_ge(a_done, t + 1)
                    if u:
                        dve.wait_ge(mixed, t)
                    nc.vector.tensor_tensor(pa[:], psa[:], gt[:, u, 0:D], ALU.mult).then_inc(gated_a, 1)
                    dve.wait_ge(b_done, t + 1)
                    nc.vector.tensor_tensor(pb[:], psb[:], gt[:, u, D:], ALU.mult).then_inc(gated_b, 1)

                def norm(u):
                    t = t0 + u
                    dve.wait_ge(w_done, t + 1)
                    if u == 0:
                        dve.wait_ge(stored, 16 * (t + 1))
                    nc.vector.scalar_tensor_tensor(y[:, u, :], xin[:, u, :], ALPHA, psw[:], ALU.mult, ALU.add).then_inc(y_done, 1)
                    dve.wait_ge(y_done, t + 2)
                    nc.vector.bn_stats(st[:, 0, :], y[:, u, 0:BANK])
                    link(nc.vector.bn_stats(st[:, 1, :], y[:, u, BANK:]))
                    settled(dve, passed)
                    nc.vector.bn_aggr(mv[:], st[:]).then_inc(var_done, 1)
                    dve.wait_ge(sd_done, t + 1)
                    link(nc.vector.reciprocal(rs[:], sd[:]))
                    nc.vector.tensor_scalar(y[:, u, :], y[:, u, :], mv[:, 0:1], rs[:], ALU.subtract, ALU.mult).then_inc(centred, 1)

                rms(0)
                low(0, 2 * t0)
                rms(1)
                low(1, 2 * t0 + 1)
                gate(0)
                gate(1)
                low(0, 2 * t0 + 2)
                low(1, 2 * t0 + 3)
                norm(0)
                norm(1)
                assert step[0] == 2 * STEPS


def route_phase(nc, ident, x1, w_group, b_group, w_router, b_router, slots, wts, bounds, slot_token):
    NL = NG + NE
    with Phase(nc, "r") as ph:
        xin = ph.sb("xin", [P, 2, D])
        th = ph.sb("th", [P, 2, D], F32R)
        tl = ph.sb("tl", [P, 2, D], F32R)
        wr = ph.sb("wr", [P, KD, NL])
        wr_hi = ph.sb("wr_hi", [P, KD, NL], F32R)
        wr_lo = ph.sb("wr_lo", [P, KD, NL], F32R)
        br = ph.sb("br", [P, NL])
        lg = ph.sb("lg", [P, NT, NL])
        tri, ones = ph.sb("tri", [P, P]), ph.sb("ones", [P, P])
        desc_i, desc = ph.sb("desc_i", [P, EPG], I32), ph.sb("desc", [P, EPG])
        tok_i, tok = ph.sb("tok_i", [P, NT], I32), ph.sb("tok", [P, NT])
        zero = ph.sb("zero", [MAXT + 1, P])
        gm, km, z, pg, m1, m2, e2, rr = (ph.sb(n, [P, NT, 1]) for n in ("gm", "km", "z", "pg", "m1", "m2", "e2", "rr"))
        gk, gsel, gexp = (ph.sb(n, [P, NT, NG]) for n in ("gk", "gsel", "gexp"))
        el, ek, sel1, sel2, el2 = (ph.sb(n, [P, NT, EPG]) for n in ("el", "ek", "sel1", "sel2", "el2"))
        o1, o2, both, wide = (ph.sb(n, [P, NT, NG, EPG]) for n in ("o1", "o2", "both", "wide"))
        before = ph.sb("before", [P, NT + 1, NE])
        place = ph.sb("place", [P, NT, NE])
        cnt, cnt_f, tiles, first, ones32 = ph.sb("cnt", [P, NE], I32), *(ph.sb(n, [P, NE]) for n in ("cnt_f", "tiles", "first", "ones32"))
        incl = ph.sb("incl", [P, NE])
        base = ph.sb("base", [P, NE])
        slot_f = ph.sb("slot_f", [P, 2, NT])
        pt = ph.ps("pt", [P, 2, D])
        pl = ph.ps("pl", [P, 2, BANK])
        pp = ph.ps("pp", [P, NT, NE])
        pc = ph.ps("pc", [P, NE])
        loaded, w_loaded, consts, split = ph.sems("loaded", 2), ph.sem("w_loaded"), ph.sem("consts"), ph.sem("split")
        turned, t_hi, t_lo, product, logits = (ph.sem(n) for n in ("turned", "t_hi", "t_lo", "product", "logits"))
        chain, exp_in, exp_out, counted, zeroed, scattered = (ph.sem(n) for n in ("chain", "exp_in", "exp_out", "counted", "zeroed", "scattered"))
        placed, ones_ready = ph.sem("placed"), ph.sem("ones_ready")
        block = ph.block()

        @block.sync
        def _(sp):
            with nc.allow_non_contiguous_dma("short rows of the router's weights"):
                sp.dma_start(wr[:, :, 0:NG], w_group[0].rearrange("(k p) n -> p k n", p=P)).then_inc(w_loaded, 16)
                sp.dma_start(wr[:, :, NG:], w_router[0].rearrange("(k p) n -> p k n", p=P)).then_inc(w_loaded, 16)
            sp.dma_start(br[:, 0:NG], b_group.to_broadcast([P, NG])).then_inc(w_loaded, 16)
            sp.dma_start(br[:, NG:], b_router.to_broadcast([P, NE])).then_inc(w_loaded, 16)
            sp.wait_ge(consts, 7)
            sp.dma_start(slot_token.rearrange("(t p) n -> t (p n)", p=P), zero[:]).then_inc(zeroed, 16)
            with sp.Fori(0, NT // 2) as i:
                for u in range(2):
                    sp.wait_ge(turned, 2 * i + u + 1)
                    sp.dma_start(xin[:, u, :], x1[bass.ts(2 * i + u, P), :]).then_inc(loaded[u], 16)

        @block.gpsimd
        def _(pool):
            nc.gpsimd.memset(ones[:], 1.0).then_inc(consts, 1)
            nc.gpsimd.memset(tri[:], 1.0).then_inc(consts, 1)
            pool.wait_ge(consts, 2)
            nc.gpsimd.affine_select(out=tri[:], in_=tri[:], compare_op=ALU.is_ge, fill=0.0, base=-1,
                                    pattern=[[1, P]], channel_multiplier=-1).then_inc(consts, 1)
            nc.gpsimd.iota(desc_i[:], [[-1, EPG]], base=EPG, channel_multiplier=0).then_inc(consts, 1)
            nc.gpsimd.iota(tok_i[:], [[P, NT]], base=0, channel_multiplier=1).then_inc(consts, 1)
            nc.gpsimd.memset(ones32[:], 1.0).then_inc(consts, 1)
            nc.gpsimd.memset(zero[:], 0.0).then_inc(consts, 1)
            pool.wait_ge(zeroed, 16)
            pool.wait_ge(placed, 1)
            for t in range(NT):
                for c in range(2):
                    pool.indirect_dma_start(out=slot_token, out_offset=bass.IndirectOffsetOnAxis(ap=slots[:, c, t:t + 1], axis=0),
                                            in_=tok[:, t:t + 1], in_offset=None).then_inc(scattered, 16)
            pool.wait_ge(scattered, 16 * 2 * NT)

        @block.tensor
        def _(pe):
            pe.sem_inc(turned, 2)
            pe.wait_ge(split, 2)
            with pe.Fori(0, NT // 2) as i:
                for u in range(2):
                    t = 2 * i + u
                    pe.wait_ge(loaded[u], 16 * (i + 1))
                    pe.wait_ge(t_lo, t + 1)
                    for k in range(KD):
                        last = nc.tensor.transpose(pt[:, u, k * P:(k + 1) * P], xin[:, u, k * P:(k + 1) * P], ident[:])
                    last.then_inc(turned, 1)
                    pe.wait_ge(t_lo, t + 3)
                    pe.wait_ge(logits, t + 1)
                    for k in range(KD):
                        at = slice(k * P, (k + 1) * P)
                        nc.tensor.matmul(pl[:, u, 0:NL], th[:, u, at], wr_hi[:, k, :], start=(k == 0), stop=False)
                        nc.tensor.matmul(pl[:, u, 0:NL], tl[:, u, at], wr_hi[:, k, :], start=False, stop=False)
                        last = nc.tensor.matmul(pl[:, u, 0:NL], th[:, u, at], wr_lo[:, k, :], start=False, stop=(k == KD - 1))
                    last.then_inc(product, 1)
            pe.wait_ge(counted, 1)
            nc.tensor.matmul(pp[:].rearrange("p t e -> p (t e)"), tri[:], both[:].rearrange("p t g e -> p (t g e)"), start=True, stop=False)
            nc.tensor.matmul(pp[:].rearrange("p t e -> p (t e)"), ones[:], before[:, 0:NT, :].rearrange("p t e -> p (t e)"), start=False, stop=True)
            nc.tensor.matmul(pc[:], ones[:], before[:, NT, :], start=True, stop=True).then_inc(product, 1)

        @block.scalar
        def _(act):
            act.wait_ge(w_loaded, 64)
            nc.scalar.activation(wr_hi[:], wr[:], ACT.Copy).then_inc(split, 1)
            with act.Fori(0, NT // 2) as i:
                for u in range(2):
                    act.wait_ge(turned, 2 * i + u + 3)
                    nc.scalar.activation(th[:, u, :], pt[:, u, :], ACT.Copy).then_inc(t_hi, 1)
            act.wait_ge(exp_in, 1)
            nc.scalar.activation(gexp[:], gexp[:], ACT.Exp).then_inc(exp_out, 1)
            act.wait_ge(exp_in, 2)
            nc.scalar.activation(e2[:], e2[:], ACT.Exp).then_inc(exp_out, 1)

        @block.vector
        def _(dve):
            dve.sem_inc(t_lo, 2)
            dve.sem_inc(logits, 2)
            dve.wait_ge(split, 1)
            nc.vector.tensor_tensor(wr_lo[:], wr[:], f(wr_hi[:]), ALU.subtract).then_inc(split, 1)
            with dve.Fori(0, NT // 2) as i:
                for u in range(2):
                    t = 2 * i + u
                    dve.wait_ge(t_hi, t + 1)
                    nc.vector.tensor_tensor(tl[:, u, :], pt[:, u, :], f(th[:, u, :]), ALU.subtract).then_inc(t_lo, 1)
                    dve.wait_ge(product, t + 1)
                    nc.vector.tensor_tensor(lg[:, bass.ds(t, 1), :], pl[:, u:u + 1, 0:NL], br[:].unsqueeze(1), ALU.add).then_inc(logits, 1)
            dve.wait_ge(logits, NT + 2)
            step = [0]

            def link(ins):
                step[0] += 1
                ins.then_inc(chain, 1)
                dve.wait_ge(chain, step[0])

            def over(ap, n):
                return ap.to_broadcast([P, NT, n])

            tt, ts, red = nc.vector.tensor_tensor, nc.vector.tensor_scalar, nc.vector.tensor_reduce
            dve.wait_ge(consts, 7)
            link(nc.vector.tensor_copy(desc[:], desc_i[:]))
            link(nc.vector.tensor_copy(tok[:], tok_i[:]))

            def first_of_best(vals, best, key, sel, n):
                link(red(best[:], vals, axis=AX.X, op=ALU.max))
                link(tt(key[:], vals, over(best[:], n), ALU.is_equal))
                link(tt(key[:], key[:], desc[:, 0:n].unsqueeze(1).to_broadcast([P, NT, n]), ALU.mult))
                link(red(km[:], key[:], axis=AX.X, op=ALU.max))
                link(tt(sel[:], key[:], over(km[:], n), ALU.is_equal))

            first_of_best(lg[:, :, 0:NG], gm, gk, gsel, NG)
            tt(gexp[:], lg[:, :, 0:NG], over(gm[:], NG), ALU.subtract).then_inc(exp_in, 1)
            gate4 = gsel[:].unsqueeze(3).to_broadcast([P, NT, NG, EPG])
            link(tt(wide[:], lg[:, :, NG:].rearrange("p t (g e) -> p t g e", g=NG), gate4, ALU.mult))
            link(red(el[:], wide[:].rearrange("p t g e -> p t e g"), axis=AX.X, op=ALU.add))
            first_of_best(el[:], m1, ek, sel1, EPG)
            link(nc.vector.scalar_tensor_tensor(el2[:], sel1[:], NEG, el[:], ALU.mult, ALU.add))
            first_of_best(el2[:], m2, ek, sel2, EPG)
            tt(e2[:], m2[:], m1[:], ALU.subtract).then_inc(exp_in, 1)
            for sel, o in ((sel1, o1), (sel2, o2)):
                link(tt(o[:], sel[:].unsqueeze(2).to_broadcast([P, NT, NG, EPG]), gate4, ALU.mult))
            nc.vector.memset(before[:, 0, :], 0.0)
            link(tt(both[:], o1[:], o2[:], ALU.add))
            for t in range(NT):
                ins = tt(before[:, t + 1, :], before[:, t, :], both[:, t].rearrange("p g e -> p (g e)"), ALU.add)
                if t < NT - 1:
                    link(ins)
            ins.then_inc(counted, 1)
            dve.wait_ge(exp_out, 2)
            link(red(z[:], gexp[:], axis=AX.X, op=ALU.add))
            link(nc.vector.reciprocal(pg[:], z[:]))
            link(ts(rr[:], e2[:], 1.0, None, ALU.add))
            link(nc.vector.reciprocal(rr[:], rr[:]))
            link(tt(wts[:, 0, :].unsqueeze(2), pg[:], rr[:], ALU.mult))
            link(tt(wts[:, 1, :].unsqueeze(2), wts[:, 0, :].unsqueeze(2), e2[:], ALU.mult))
            dve.wait_ge(product, NT + 1)
            link(ts(cnt_f[:], pc[:], float(P - 1), None, ALU.add))
            link(nc.vector.tensor_copy(cnt[:], cnt_f[:]))
            link(ts(cnt[:], cnt[:], 7, None, ALU.arith_shift_right))
            link(nc.vector.tensor_copy(tiles[:], cnt[:]))
            link(ts(tiles[:], tiles[:], 1.0, None, ALU.max))
            link(nc.vector.tensor_tensor_scan(incl[:], ones32[:], tiles[:], 0.0, ALU.mult, ALU.add))
            link(tt(first[:], incl[:], tiles[:], ALU.subtract))
            nc.vector.memset(bounds[:, 0:1], 0)
            link(nc.vector.tensor_copy(bounds[:, 1:NE + 1], incl[:]))
            link(ts(base[:], first[:], float(P), None, ALU.mult))
            link(tt(place[:], pp[:], base[:].unsqueeze(1).to_broadcast([P, NT, NE]), ALU.add))
            for c, o in enumerate((o1, o2)):
                link(tt(wide[:].rearrange("p t g e -> p t (g e)"), o[:].rearrange("p t g e -> p t (g e)"), place[:], ALU.mult))
                link(red(slot_f[:, c, :].unsqueeze(2), wide[:].rearrange("p t g e -> p t (g e)"), axis=AX.X, op=ALU.add))
            nc.vector.tensor_copy(slots[:], slot_f[:]).then_inc(placed, 1)


def expert_phase(nc, ident, x1, slot_token, bounds, w_gate_up, w_down, ys):
    KF = FF // P
    NEARLY = 2
    NS = KD + KF
    NL = NS - NEARLY
    with Phase(nc, "e") as ph:
        raw = ph.sb("raw", [P, NS, D])
        eh = ph.sb("eh", [P, 2, NEARLY, D], F32R)
        el = ph.sb("el", [P, 2, NEARLY, D], F32R)
        wh = ph.sb("wh", [P, NL, D], F32R)
        wl = ph.sb("wl", [P, NL, D], F32R)
        xg = ph.sb("xg", [P, D])
        xh = ph.sb("xh", [P, D], F32R)
        xl = ph.sb("xl", [P, D], F32R)
        act_g = ph.sb("act_g", [P, FF])
        h = ph.sb("h", [P, FF])
        hh = ph.sb("hh", [P, FF], F32R)
        hl = ph.sb("hl", [P, FF], F32R)
        yo = ph.sb("yo", [P, D])
        zero = ph.sb("zero", [P, D])
        tab = ph.sb("tab", [MAXT + 1, P])
        idx = ph.sb("idx", [P, MAXT + 1], I32)
        idx1 = ph.sb("idx1", [P, 1], I32)
        pg, py, px = ph.ps("pg", [P, D]), ph.ps("py", [P, D]), ph.ps("px", [P, D])
        phh = ph.ps("phh", [P, FF])
        passed = ph.sem("passed")
        tab_in, tab_turned, tab_done = ph.sem("tab_in"), ph.sem("tab_turned"), ph.sem("tab_done")
        raw_in = ph.sems("raw_in", NS)
        early_hi, early_lo, w_hi, w_lo = (ph.sem(n) for n in ("early_hi", "early_lo", "w_hi", "w_lo"))
        picked, gathered, x_turned, x_hi, x_lo = (ph.sem(n) for n in ("picked", "gathered", "x_turned", "x_hi", "x_lo"))
        gu_done, silu_done, h_done, h_turned, h_hi, h_lo = (ph.sem(n) for n in ("gu_done", "silu_done", "h_done", "h_turned", "h_hi", "h_lo"))
        down_done, y_out, stored = ph.sem("down_done"), ph.sem("y_out"), ph.sem("stored")
        zeroed, rest = ph.sem("zeroed"), ph.sem("rest")
        block = ph.block()

        def tiles(eng, e):
            b0 = eng.value_load(bounds[0:1, bass.ds(e, 1)], min_val=0, max_val=MAXT - 1)
            b1 = eng.value_load(bounds[0:1, bass.ds(e + 1, 1)], min_val=1, max_val=MAXT)
            return b0, b1

        def all_tiles(eng):
            return eng.value_load(bounds[0:1, NE:NE + 1], min_val=NE, max_val=MAXT)

        @block.sync
        def _(sp):
            sp.dma_start(tab[:], slot_token.rearrange("(t p) n -> t (p n)", p=P)).then_inc(tab_in, 16)

            def load(e, s):
                src = w_gate_up if s < KD else w_down
                k = s if s < KD else s - KD
                sp.dma_start(raw[:, s, :], src[0, bass.ds(e, 1), k * P:(k + 1) * P, :].rearrange("a p n -> p (a n)")).then_inc(raw_in[s], 16)

            for s in range(NS):
                load(0, s)
            sp.wait_ge(zeroed, 1)
            n = all_tiles(sp)
            with sp.Fori(0, n) as _g:
                sp.sem_inc(rest, 16)
            with sp.Fori(n, MAXT + 1) as g:
                sp.dma_start(ys[bass.ts(g, P), :], zero[:]).then_inc(rest, 16)
            with sp.Fori(0, NE - 1) as e:
                for s in range(NS):
                    if s < NEARLY:
                        sp.wait_ge(early_lo, NEARLY * e + s + 1)
                    else:
                        sp.wait_ge(w_lo, NL * e + s - NEARLY + 1)
                    load(e + 1, s)
            sp.wait_ge(rest, (MAXT + 1) * 16)

        @block.gpsimd
        def _(pool):
            nc.gpsimd.memset(zero[:], 0.0).then_inc(zeroed, 1)

            def gather(g):
                settled(pool, passed)
                nc.gpsimd.tensor_copy(idx1[:], idx[:, bass.ds(g, 1)]).then_inc(picked, 1)
                pool.wait_ge(picked, g + 1)
                settled(pool, passed)
                pool.indirect_dma_start(out=xg[:], out_offset=None, in_=x1,
                                        in_offset=bass.IndirectOffsetOnAxis(ap=idx1[:, 0:1], axis=0)).then_inc(gathered, 16)

            def early(e, v):
                for s in range(NEARLY):
                    pool.wait_ge(raw_in[s], 16 * (e + 1))
                    settled(pool, passed)
                    nc.gpsimd.tensor_copy(eh[:, v, s, :], raw[:, s, :]).then_inc(early_hi, 1)
                    pool.wait_ge(early_hi, NEARLY * e + s + 1)
                    nc.gpsimd.tensor_tensor(el[:, v, s, :], raw[:, s, :], f(eh[:, v, s, :]), ALU.subtract).then_inc(early_lo, 1)

            pool.wait_ge(tab_done, 1)
            gather(0)
            early(0, 0)
            with pool.Fori(0, NE // 2) as i:
                for v in range(2):
                    e = 2 * i + v
                    b0, b1 = tiles(pool, e)
                    with pool.Fori(b0, b1) as g:
                        pool.wait_ge(x_turned, g + 1)
                        gather(g + 1)
                    if v == 0:
                        pool.wait_ge(gu_done, b0 + 1)
                        early(e + 1, 1)
                    else:
                        with pool.If(i < NE // 2 - 1):
                            pool.wait_ge(gu_done, b0 + 1)
                            early(e + 1, 0)
            pool.wait_ge(gathered, 16 * (all_tiles(pool) + 1))

        @block.tensor
        def _(pe):
            pe.sem_inc(gu_done, 1)
            pe.wait_ge(tab_in, 16)
            nc.tensor.transpose(px[:, 0:MAXT + 1], tab[:], ident[0:MAXT + 1, 0:MAXT + 1]).then_inc(tab_turned, 1)

            def turn_x(g):
                pe.wait_ge(gathered, 16 * (g + 1))
                pe.wait_ge(x_lo, g + 1)
                for k in range(KD):
                    last = nc.tensor.transpose(px[:, k * P:(k + 1) * P], xg[:, k * P:(k + 1) * P], ident[:])
                last.then_inc(x_turned, 1)

            turn_x(0)
            with pe.Fori(0, NE // 2) as i:
                for v in range(2):
                    e = 2 * i + v
                    b0, b1 = tiles(pe, e)
                    with pe.Fori(b0, b1) as g:
                        pe.wait_ge(x_lo, g + 2)
                        pe.wait_ge(h_done, g + 1)
                        for k in range(KD):
                            early = k < NEARLY
                            if early:
                                pe.wait_ge(early_lo, NEARLY * e + k + 1)
                            else:
                                pe.wait_ge(w_lo, NL * e + k - NEARLY + 1)
                            hi = eh[:, v, k, :] if early else wh[:, k - NEARLY, :]
                            lo = el[:, v, k, :] if early else wl[:, k - NEARLY, :]
                            at = slice(k * P, (k + 1) * P)
                            for j in range(D // BANK):
                                js = slice(j * BANK, (j + 1) * BANK)
                                nc.tensor.matmul(pg[:, js], xh[:, at], hi[:, js], start=(k == 0), stop=False)
                                nc.tensor.matmul(pg[:, js], xl[:, at], hi[:, js], start=False, stop=False)
                                last = nc.tensor.matmul(pg[:, js], xh[:, at], lo[:, js], start=False, stop=(k == KD - 1))
                        last.then_inc(gu_done, 1)
                        turn_x(g + 1)
                        pe.wait_ge(h_done, g + 2)
                        for k in range(KF):
                            last = nc.tensor.transpose(phh[:, k * P:(k + 1) * P], h[:, k * P:(k + 1) * P], ident[:])
                        last.then_inc(h_turned, 1)
                        pe.wait_ge(h_lo, g + 1)
                        pe.wait_ge(y_out, g + 1)
                        for k in range(KF):
                            pe.wait_ge(w_lo, NL * e + KD - NEARLY + k + 1)
                            n, at = KD - NEARLY + k, slice(k * P, (k + 1) * P)
                            for j in range(D // BANK):
                                js = slice(j * BANK, (j + 1) * BANK)
                                nc.tensor.matmul(py[:, js], hh[:, at], wh[:, n, js], start=(k == 0), stop=False)
                                nc.tensor.matmul(py[:, js], hl[:, at], wh[:, n, js], start=False, stop=False)
                                last = nc.tensor.matmul(py[:, js], hh[:, at], wl[:, n, js], start=False, stop=(k == KF - 1))
                        last.then_inc(down_done, 1)

        @block.scalar
        def _(act):
            act.sem_inc(y_out, 1)
            act.sem_inc(stored, 16)

            def high_x(g):
                act.wait_ge(x_turned, g + 1)
                nc.scalar.activation(xh[:], px[:], ACT.Copy).then_inc(x_hi, 1)

            high_x(0)
            with act.Fori(0, NE) as e:
                for s in range(NEARLY, NS):
                    act.wait_ge(raw_in[s], 16 * (e + 1))
                    nc.scalar.activation(wh[:, s - NEARLY, :], raw[:, s, :], ACT.Copy).then_inc(w_hi, 1)
                b0, b1 = tiles(act, e)
                with act.Fori(b0, b1) as g:
                    act.wait_ge(gu_done, g + 2)
                    nc.scalar.activation(act_g[:], pg[:, 0:FF], ACT.Silu).then_inc(silu_done, 1)
                    high_x(g + 1)
                    act.wait_ge(h_turned, g + 1)
                    nc.scalar.activation(hh[:], phh[:], ACT.Copy).then_inc(h_hi, 1)
                    act.wait_ge(down_done, g + 1)
                    act.wait_ge(stored, 16 * (g + 1))
                    nc.scalar.activation(yo[:], py[:], ACT.Copy).then_inc(y_out, 1)
                    act.wait_ge(y_out, g + 2)
                    act.dma_start(ys[bass.ts(g, P), :], yo[:]).then_inc(stored, 16)
            act.wait_ge(stored, 16 * (all_tiles(act) + 1))
            settled(act, passed)

        @block.vector
        def _(dve):
            dve.wait_ge(tab_turned, 1)
            nc.vector.tensor_copy(idx[:], px[:, 0:MAXT + 1]).then_inc(tab_done, 1)
            dve.wait_ge(tab_done, 1)
            dve.sem_inc(x_lo, 1)
            dve.sem_inc(h_done, 1)

            def low_x(g):
                dve.wait_ge(x_hi, g + 1)
                nc.vector.tensor_tensor(xl[:], px[:], f(xh[:]), ALU.subtract).then_inc(x_lo, 1)

            low_x(0)
            with dve.Fori(0, NE) as e:
                for s in range(NEARLY, NS):
                    dve.wait_ge(w_hi, NL * e + s - NEARLY + 1)
                    nc.vector.tensor_tensor(wl[:, s - NEARLY, :], raw[:, s, :], f(wh[:, s - NEARLY, :]), ALU.subtract).then_inc(w_lo, 1)
                b0, b1 = tiles(dve, e)
                with dve.Fori(b0, b1) as g:
                    dve.wait_ge(silu_done, g + 1)
                    nc.vector.tensor_tensor(h[:], act_g[:], pg[:, FF:], ALU.mult).then_inc(h_done, 1)
                    low_x(g + 1)
                    dve.wait_ge(h_hi, g + 1)
                    nc.vector.tensor_tensor(hl[:], phh[:], f(hh[:]), ALU.subtract).then_inc(h_lo, 1)


def combine_phase(nc, x1, ys, slots, wts, ln_g, ln_b, out):
    with Phase(nc, "o") as ph:
        xin, y1, y2, z = (ph.sb(n, [P, 2, D]) for n in ("xin", "y1", "y2", "z"))
        sl = ph.sb("sl", [P, 2, 2, 1], I32)
        ww = ph.sb("ww", [P, 2, 2, 1])
        gam, bet = ph.sb("gam", [P, D]), ph.sb("bet", [P, D])
        st, mv, sd, rs = ph.sb("st", [P, 2, 6]), ph.sb("mv", [P, 2]), ph.sb("sd", [P, 1]), ph.sb("rs", [P, 1])
        eps = ph.sb("eps", [P, 1])
        passed = ph.sem("passed")
        vec_in, eps_set, loaded = ph.sem("vec_in"), ph.sem("eps_set"), ph.sems("loaded", 2)
        picked, got = ph.sem("picked"), ph.sems("got", 2)
        scaled, chain, var_done, sd_done, centred, finished = (ph.sem(n) for n in ("scaled", "chain", "var_done", "sd_done", "centred", "finished"))
        stored = ph.sem("stored")
        summed, weighed, times = ph.sem("summed"), ph.sem("weighed"), ph.sem("times")
        block = ph.block()

        @block.sync
        def _(sp):
            for src, dst in ((ln_g, gam), (ln_b, bet)):
                sp.dma_start(dst[:], src.to_broadcast([P, D])).then_inc(vec_in, 16)
            with sp.Fori(0, NT // 2) as i:
                for u in range(2):
                    t = 2 * i + u
                    sp.wait_ge(summed, t + 1)
                    sp.dma_start(xin[:, u, :], x1[bass.ts(t, P), :]).then_inc(loaded[u], 16)

        @block.gpsimd
        def _(pool):
            with pool.Fori(0, NT // 2) as i:
                for u in range(2):
                    t = 2 * i + u
                    pool.wait_ge(summed, t + 1)
                    settled(pool, passed)
                    nc.gpsimd.tensor_copy(sl[:, u, :, :], slots[:, :, bass.ds(t, 1)]).then_inc(picked, 1)
                    pool.wait_ge(picked, t + 1)
                    settled(pool, passed)
                    for c, y in enumerate((y1, y2)):
                        pool.indirect_dma_start(out=y[:, u, :], out_offset=None, in_=ys,
                                                in_offset=bass.IndirectOffsetOnAxis(ap=sl[:, u, c, :], axis=0)).then_inc(got[u], 16)

        @block.scalar
        def _(act):
            act.sem_inc(stored, 32)
            act.wait_ge(eps_set, 1)
            with act.Fori(0, NT // 2) as i:
                for u in range(2):
                    t = 2 * i + u
                    act.wait_ge(loaded[u], 16 * (i + 1))
                    act.wait_ge(stored, 32 * (i + 1))
                    nc.scalar.activation(z[:, u, :], xin[:, u, :], ACT.Copy, scale=ALPHA).then_inc(scaled, 1)
                for u in range(2):
                    t = 2 * i + u
                    act.wait_ge(var_done, t + 1)
                    nc.scalar.activation(sd[:], mv[:, 1:2], ACT.Sqrt, bias=eps[:]).then_inc(sd_done, 1)
                for u in range(2):
                    act.wait_ge(finished, 2 * i + u + 1)
                    act.dma_start(out[0, bass.ts(2 * i + u, P), :], z[:, u, :]).then_inc(stored, 16)
            act.wait_ge(stored, 16 * (NT + 2))

        @block.vector
        def _(dve):
            nc.vector.memset(eps[:], EPS).then_inc(eps_set, 1)
            dve.sem_inc(summed, 2)
            dve.wait_ge(vec_in, 32)
            STEPS = 4
            with dve.Fori(0, NT // 2) as i:
                step = [0]

                def link(ins):
                    step[0] += 1
                    ins.then_inc(chain, 1)
                    dve.wait_ge(chain, 2 * STEPS * i + step[0])

                for u in range(2):
                    t = 2 * i + u
                    zu = z[:, u, :]
                    nc.vector.tensor_copy(ww[:, u, :, :], wts[:, :, bass.ds(t, 1)]).then_inc(weighed, 1)
                    dve.wait_ge(weighed, t + 1)
                    dve.wait_ge(scaled, t + 1)
                    dve.wait_ge(got[u], 32 * (i + 1))
                    link(nc.vector.scalar_tensor_tensor(zu, y1[:, u, :], ww[:, u, 0, :], zu, ALU.mult, ALU.add))
                    nc.vector.scalar_tensor_tensor(zu, y2[:, u, :], ww[:, u, 1, :], zu, ALU.mult, ALU.add).then_inc(summed, 1)
                    dve.wait_ge(summed, t + 3)
                    nc.vector.bn_stats(st[:, 0, :], z[:, u, 0:BANK])
                    link(nc.vector.bn_stats(st[:, 1, :], z[:, u, BANK:]))
                    settled(dve, passed)
                    nc.vector.bn_aggr(mv[:], st[:]).then_inc(var_done, 1)
                    dve.wait_ge(sd_done, t + 1)
                    link(nc.vector.reciprocal(rs[:], sd[:]))
                    nc.vector.tensor_scalar(zu, zu, mv[:, 0:1], rs[:], ALU.subtract, ALU.mult).then_inc(centred, 1)
                    dve.wait_ge(centred, t + 1)
                    link(nc.vector.tensor_tensor(zu, zu, gam[:], ALU.mult))
                    nc.vector.tensor_tensor(zu, zu, bet[:], ALU.add).then_inc(finished, 1)
                assert step[0] == 2 * STEPS


def program(nc, a, out, phases=99):
    def dram(name, shape):
        return nc.dram_tensor(name, shape, F32, kind="Internal").ap()

    xt_hi, xt_lo = dram("xt_hi", (NT, P, D)), dram("xt_lo", (NT, P, D))
    qk_hi, qk_lo = dram("qk_hi", (NPIECE, P, SEQ)), dram("qk_lo", (NPIECE, P, SEQ))
    v_hi, v_lo = dram("v_hi", (NT, P, VW)), dram("v_lo", (NT, P, VW))
    gates = dram("gates", (SEQ, GATE))
    with ExitStack() as ctx:
        ident = ctx.enter_context(nc.sbuf_tensor("ident", [P, P], F32))
        constants_phase(nc, ident, None)
        with Phase(nc, "qkv") as ph:
            w_hi = ph.sb("w_hi", [P, KD, QKV], F32R)
            w_lo = ph.sb("w_lo", [P, KD, QKV], F32R)
            cos_t, sin_t, nsin_t = (ph.sb(n, [P, NT, HALF]) for n in ("cos", "sin", "nsin"))
            prepare_phase(nc, a["x"], a["w_in"], a["positions"], a["inv_freq"], ident, w_hi, w_lo,
                          cos_t, sin_t, nsin_t, xt_hi, xt_lo)
            project_phase(nc, w_hi, w_lo, cos_t, sin_t, nsin_t, ident, xt_hi, xt_lo, qk_hi, qk_lo, v_hi, v_lo)
        gates_phase(nc, a["w_in"], a["b_gate"], xt_hi, xt_lo, gates)
        ob = dram("ob", (SEQ, B_V))
        diff_attention_phase(nc, [a["lambda_q1"], a["lambda_k1"], a["lambda_q2"], a["lambda_k2"]], ident, qk_hi, qk_lo, v_hi, v_lo, ob)
        oa = dram("oa", (SEQ, A_Q))
        window_attention_phase(nc, a["sinks"], ident, qk_hi, qk_lo, v_hi, v_lo, oa)
        x1 = dram("x1", (SEQ, D))
        merge_phase(nc, ident, oa, ob, gates, a["x"], a["subln_g"], a["w_proj_a"], a["w_proj_b"], a["w_out"], a["ln1_g"], a["ln1_b"], x1)
        slots = ctx.enter_context(nc.sbuf_tensor("slots", [P, 2, NT], I32))
        wts = ctx.enter_context(nc.sbuf_tensor("wts", [P, 2, NT], F32))
        bounds = ctx.enter_context(nc.sbuf_tensor("bounds", [P, NE + 1], I32))
        slot_token = dram("slot_token", ((MAXT + 1) * P, 1))
        ys = dram("ys", ((MAXT + 1) * P, D))
        route_phase(nc, ident, x1, a["w_group"], a["b_group"], a["w_router"], a["b_router"], slots, wts, bounds, slot_token)
        expert_phase(nc, ident, x1, slot_token, bounds, a["w_gate_up"], a["w_down"], ys)
        combine_phase(nc, x1, ys, slots, wts, a["ln2_g"], a["ln2_b"], out)


def rotary_frequencies():
    exponent = np.arange(0, HD, 2, dtype=np.float32) / np.float32(HD)
    return (np.float32(1.0) / np.float32(10000.0) ** exponent).astype(np.float32)[None]


_INS = ["x", "positions", "w_in", "b_gate", "sinks", "lambda_q1", "lambda_k1", "lambda_q2", "lambda_k2", "subln_g",
        "w_proj_a", "w_proj_b", "w_out", "ln1_g", "ln1_b", "w_group", "b_group", "w_router", "b_router", "w_gate_up",
        "w_down", "ln2_g", "ln2_b"]


def kernel(**inputs):
    import concourse.bacc as bacc
    from concourse.bass_utils import run_bass_kernel_spmd

    nc = bacc.Bacc("TRN2", target_bir_lowering=False, num_devices=1)
    arrays = {name: np.ascontiguousarray(inputs[name]) for name in _INS}
    arrays["inv_freq"] = rotary_frequencies()
    aps = {name: nc.dram_tensor(name, v.shape, mybir.dt.from_np(v.dtype), kind="ExternalInput").ap()
           for name, v in arrays.items()}
    out = nc.dram_tensor("out", (1, SEQ, D), F32, kind="ExternalOutput").ap()
    program(nc, aps, out)
    result = run_bass_kernel_spmd(nc, [arrays], core_ids=[0])
    return result.results[0]["out"]
```

```python
import math
from contextlib import ExitStack

import numpy as np

import concourse.bass as bass
from concourse import mybir
from concourse.alu_op_type import AluOpType as ALU

F32 = mybir.dt.float32
F32R = mybir.dt.float32r
I32 = mybir.dt.int32
ACT = mybir.ActivationFunctionType
AX = mybir.AxisListType

P = 128
SEQ = 2048
D = 1024
KD = D // P
NT = SEQ // P
CHUNK = 64
HD = 64
HALF = HD // 2
A_HEADS = 8
A_KV = 2
B_HEADS = 4
BV = 128
NG = 4
EPG = 8
NE = NG * EPG
FF = 512
ALPHA = 2.0 ** 0.25
EPS = 1e-5
NEG = -1e30
SCALE = HD ** -0.5
LAM_INIT = 0.8 - 0.6 * math.exp(0.0)

A_Q = A_HEADS * HD
A_K = A_KV * HD
B_QK = B_HEADS * 2 * HD
B_V = B_HEADS * BV
QKV = A_Q + 2 * A_K + 2 * B_QK + B_V
GATE = 2 * D
BANK = 512

GROUPS = [(0, 512, 0), (512, 128, 128), (768, 512, 0), (1280, 512, 0), (1792, 0, 512)]
PIECE0 = [0, 4, 5, 9]
NPIECE = 13
VW = A_K + B_V
MAXT = (2 * SEQ) // P + NE - 1


class Phase:

    def __init__(self, nc, name):
        self.nc, self.name, self.ctx, self.used = nc, name, ExitStack(), []

    def __enter__(self):
        self.ctx.__enter__()
        return self

    def __exit__(self, *a):
        done = self.ctx.__exit__(*a)
        if self.used:
            self.nc.clear_and_free_semaphores(self.used)
            self.nc.all_engine_barrier()
        return done

    def sb(self, name, shape, dt=F32):
        return self.ctx.enter_context(self.nc.sbuf_tensor(f"{self.name}_{name}", shape, dt))

    def ps(self, name, shape, dt=F32):
        return self.ctx.enter_context(self.nc.psum_tensor(f"{self.name}_{name}", shape, dt))

    def sem(self, name):
        self.used.append(self.nc.alloc_semaphore(f"{self.name}_{name}"))
        return self.used[-1]

    def sems(self, name, n):
        return [self.sem(f"{name}{i}") for i in range(n)]

    def block(self):
        return self.ctx.enter_context(self.nc.Block())


def settled(eng, passed):
    eng.sem_inc(passed, 1)


def f(ap):
    return ap.bitcast(F32)


def constants_phase(nc, ident, identr):
    with Phase(nc, "c") as ph:
        zeroed, made = ph.sem("zeroed"), ph.sem("made")
        block = ph.block()

        @block.gpsimd
        def _(pool):
            nc.gpsimd.memset(ident[:], 0.0).then_inc(zeroed, 1)
            pool.wait_ge(zeroed, 1)
            nc.gpsimd.affine_select(out=ident[:], in_=ident[:], compare_op=ALU.not_equal, fill=1.0, base=0,
                                    pattern=[[-1, P]], channel_multiplier=1).then_inc(made, 1)
            pool.wait_ge(made, 1)


def prepare_phase(nc, x, w_in, positions, inv_freq, ident, w_hi, w_lo, cos_t, sin_t, nsin_t, xt_hi, xt_lo):
    two_pi = 2.0 * math.pi
    PI_IN = 3.1415925
    c1 = 6.28125
    c2 = float(np.float32(1.934051513671875e-3))
    c3 = float(two_pi - c1 - c2)
    with Phase(nc, "p") as ph:
        x_in = ph.sb("x_in", [P, 2, D])
        xh = ph.sb("xh", [P, 2, D], F32R)
        xl = ph.sb("xl", [P, 2, D], F32R)
        raw = ph.sb("raw", [P, 2, QKV])
        pos_i = ph.sb("pos_i", [P, NT], I32)
        pos_f = ph.sb("pos_f", [P, NT])
        inv = ph.sb("inv", [P, HALF])
        ang = ph.sb("ang", [P, NT, HALF])
        turns = ph.sb("turns", [P, NT, HALF])
        turns_i = ph.sb("turns_i", [P, NT, HALF], I32)
        red = ph.sb("red", [P, NT, HALF])
        psx = ph.ps("psx", [P, 2, D])
        x_loaded = ph.sems("x_loaded", 2)
        w_loaded = ph.sems("w_loaded", 2)
        x_turned, x_hi, x_lo = ph.sem("x_turned"), ph.sem("x_hi"), ph.sem("x_lo")
        x_stored = ph.sems("x_stored", 2)
        w_his, w_los = ph.sem("w_his"), ph.sem("w_los")
        tables_in, table_step, angles, tables = ph.sem("tables_in"), ph.sem("table_step"), ph.sems("angles", 2), ph.sem("tables")
        tmp = ph.sb("tmp", [P, NT, HALF])
        block = ph.block()

        @block.gpsimd
        def _(pool):
            with nc.allow_non_contiguous_dma("one position a partition"):
                pool.dma_start(pos_i[:], positions.rearrange("b (t p) -> p (b t)", p=P)).then_inc(tables_in, 16)
            pool.dma_start(inv[:], inv_freq.to_broadcast([P, HALF])).then_inc(tables_in, 16)
            with pool.Fori(0, NT // 4) as i:
                for v in range(4):
                    u, t = v % 2, 4 * i + v
                    pool.wait_ge(x_turned, t + 1)
                    pool.dma_start(x_in[:, u, :], x[0, bass.ts(t, P), :]).then_inc(x_loaded[u], 16)
                    if v % 2 == 0:
                        w, k = v // 2, 2 * i + v // 2
                        pool.wait_ge(w_los, k + 1)
                        pool.dma_start(raw[:, w, :], w_in[0, bass.ts(k, P), 0:QKV]).then_inc(w_loaded[w], 16)

        @block.tensor
        def _(pe):
            pe.sem_inc(x_turned, 2)
            with pe.Fori(0, NT // 4) as i:
                for v in range(4):
                    u, t = v % 2, 4 * i + v
                    pe.wait_ge(x_loaded[u], 16 * (2 * i + v // 2 + 1))
                    pe.wait_ge(x_hi, t + 1)
                    pe.wait_ge(x_lo, t + 1)
                    for k in range(KD):
                        last = nc.tensor.transpose(psx[:, u, bass.ts(k, P)], x_in[:, u, bass.ts(k, P)], ident[:])
                    last.then_inc(x_turned, 1)

        @block.scalar
        def _(act):
            act.sem_inc(x_hi, 2)
            with act.Fori(0, NT // 4) as i:
                for v in range(4):
                    u, t = v % 2, 4 * i + v
                    act.wait_ge(x_turned, t + 3)
                    act.wait_ge(x_stored[u], 32 * (2 * i + v // 2 + 1))
                    nc.scalar.activation(xh[:, u, :], psx[:, u, :], ACT.Copy).then_inc(x_hi, 1)
                    if v % 2 == 0:
                        w, k = v // 2, 2 * i + v // 2
                        act.wait_ge(w_loaded[w], 16 * (i + 1))
                        nc.scalar.activation(w_hi[:, bass.ds(k, 1), 0:QKV], raw[:, w:w + 1, :], ACT.Copy).then_inc(w_his, 1)
            for n, (table, reduced) in enumerate(((sin_t, red), (cos_t, turns))):
                act.wait_ge(angles[n], 1)
                nc.scalar.activation(table[:], reduced[:], ACT.Sin).then_inc(tables, 1)
            act.wait_ge(tables, 2)
            nc.scalar.activation(nsin_t[:], sin_t[:], ACT.Copy, scale=-1.0).then_inc(tables, 1)
            act.wait_ge(tables, 3)

        @block.vector
        def _(dve):
            steps = [0]

            def link(ins):
                steps[0] += 1
                ins.then_inc(table_step, 1)
                dve.wait_ge(table_step, steps[0])

            dve.sem_inc(x_lo, 2)
            dve.sem_inc(w_los, 2)
            with dve.Fori(0, NT // 4) as i:
                for v in range(4):
                    u, t = v % 2, 4 * i + v
                    dve.wait_ge(x_hi, t + 3)
                    nc.vector.tensor_tensor(xl[:, u, :], psx[:, u, :], f(xh[:, u, :]), ALU.subtract).then_inc(x_lo, 1)
                    if v % 2 == 0:
                        w, k = v // 2, 2 * i + v // 2
                        dve.wait_ge(w_his, k + 1)
                        nc.vector.tensor_tensor(w_lo[:, bass.ds(k, 1), 0:QKV], raw[:, w:w + 1, :],
                                                f(w_hi[:, bass.ds(k, 1), 0:QKV]), ALU.subtract).then_inc(w_los, 1)
            dve.wait_ge(tables_in, 32)
            link(nc.vector.tensor_copy(pos_f[:], pos_i[:]))
            link(nc.vector.tensor_tensor(ang[:], pos_f[:].unsqueeze(2).to_broadcast([P, NT, HALF]),
                                         inv[:].unsqueeze(1).to_broadcast([P, NT, HALF]), ALU.mult))
            for n, out in enumerate((red, turns)):
                link(nc.vector.tensor_scalar(out[:], ang[:], 1.0 / two_pi, 0.25 * n, ALU.mult, ALU.add))
                link(nc.vector.tensor_copy(turns_i[:], out[:]))
                link(nc.vector.tensor_copy(out[:], turns_i[:]))
                link(nc.vector.scalar_tensor_tensor(tmp[:], out[:], -c1, ang[:], ALU.mult, ALU.add))
                link(nc.vector.scalar_tensor_tensor(tmp[:], out[:], -c2, tmp[:], ALU.mult, ALU.add))
                link(nc.vector.scalar_tensor_tensor(tmp[:], out[:], -c3, tmp[:], ALU.mult, ALU.add))
                link(nc.vector.tensor_scalar(tmp[:], tmp[:], 0.5 * math.pi * n, None, ALU.add))
                link(nc.vector.tensor_scalar(out[:], tmp[:], math.pi, -two_pi, ALU.is_gt, ALU.mult))
                link(nc.vector.tensor_tensor(tmp[:], tmp[:], out[:], ALU.add))
                link(nc.vector.tensor_scalar(out[:], tmp[:], -math.pi, two_pi, ALU.is_lt, ALU.mult))
                link(nc.vector.tensor_tensor(tmp[:], tmp[:], out[:], ALU.add))
                link(nc.vector.tensor_scalar(tmp[:], tmp[:], PI_IN, None, ALU.min))
                nc.vector.tensor_scalar(out[:], tmp[:], -PI_IN, None, ALU.max).then_inc(angles[n], 1)

        @block.sync
        def _(sp):
            for u in range(2):
                sp.sem_inc(x_stored[u], 32)
            with sp.Fori(0, NT // 4) as i:
                for v in range(4):
                    u, t = v % 2, 4 * i + v
                    sp.wait_ge(x_lo, t + 3)
                    sp.dma_start(xt_hi[bass.ds(t, 1)], f(xh[:, u, :])).then_inc(x_stored[u], 16)
                    sp.dma_start(xt_lo[bass.ds(t, 1)], f(xl[:, u, :])).then_inc(x_stored[u], 16)
            for u in range(2):
                sp.wait_ge(x_stored[u], 32 * (NT // 2 + 1))


def project_phase(nc, w_hi, w_lo, cos_t, sin_t, nsin_t, ident, xt_hi, xt_lo, qk_hi, qk_lo, v_hi, v_lo):
    with Phase(nc, "j") as ph:
        xh = ph.sb("xh", [P, 2, D], F32R)
        xl = ph.sb("xl", [P, 2, D], F32R)
        by_cos = ph.sb("by_cos", [P, 2, BANK])
        by_sin = ph.sb("by_sin", [P, 2, BANK])
        turned = ph.sb("turned", [P, 2, BANK])
        qkh = ph.sb("qkh", [P, NPIECE, P], F32R)
        qkl = ph.sb("qkl", [P, NPIECE, P], F32R)
        vh = ph.sb("vh", [P, VW], F32R)
        vl = ph.sb("vl", [P, VW], F32R)
        pg = [ph.ps(f"pg{j}", [P, BANK]) for j in range(5)]
        pt = [ph.ps(f"pt{j}", [P, BANK]) for j in range(2)]
        x_loaded = ph.sems("x_loaded", 2)
        product = ph.sems("product", 5)
        v_hi_done, v_lo_done = ph.sem("v_hi_done"), ph.sem("v_lo_done")
        scaled, rotated = ph.sem("scaled"), ph.sem("rotated")
        transposed, qk_hi_done, qk_lo_done = ph.sem("transposed"), ph.sem("qk_hi_done"), ph.sem("qk_lo_done")
        stored = ph.sem("stored")
        block = ph.block()
        ROT = [j for j, g in enumerate(GROUPS) if g[1]]
        VOFF = {1: 0, 4: A_K}

        @block.sync
        def _(sp):
            with sp.Fori(0, NT // 2) as i:
                for u in range(2):
                    t = 2 * i + u
                    sp.wait_ge(product[4], t + 1)
                    sp.dma_start(f(xh[:, u, :]), xt_hi[bass.ds(t, 1)]).then_inc(x_loaded[u], 16)
                    sp.dma_start(f(xl[:, u, :]), xt_lo[bass.ds(t, 1)]).then_inc(x_loaded[u], 16)

        @block.tensor
        def _(pe):
            pe.sem_inc(product[4], 2)
            pe.sem_inc(transposed, 2)

            def group(i, u, j):
                t = 2 * i + u
                c0, rot, v = GROUPS[j]
                if v:
                    pe.wait_ge(v_lo_done, 2 * t + (1 if j == 1 else 2))
                if rot:
                    pe.wait_ge(scaled, 4 * t + ROT.index(j) + 1)
                for k in range(KD):
                    ks, cs = slice(k * P, (k + 1) * P), slice(c0, c0 + rot + v)
                    out = pg[j][:, 0:rot + v]
                    nc.tensor.matmul(out, xh[:, u, ks], w_hi[:, k, cs], start=(k == 0), stop=False)
                    nc.tensor.matmul(out, xl[:, u, ks], w_hi[:, k, cs], start=False, stop=False)
                    last = nc.tensor.matmul(out, xh[:, u, ks], w_lo[:, k, cs], start=False, stop=(k == KD - 1))
                last.then_inc(product[j], 1)

            def turn(i, u, r):
                n = 4 * (2 * i + u) + r
                pe.wait_ge(rotated, n + 3)
                pe.wait_ge(qk_lo_done, n + 1)
                for c in range(GROUPS[ROT[r]][1] // P):
                    last = nc.tensor.transpose(pt[r % 2][:, c * P:(c + 1) * P], turned[:, r % 2, c * P:(c + 1) * P], ident[:])
                last.then_inc(transposed, 1)

            with pe.Fori(0, NT // 2) as i:
                for u in range(2):
                    pe.wait_ge(x_loaded[u], 32 * (i + 1))
                    group(i, u, 0)
                    group(i, u, 1)
                    group(i, u, 2)
                    turn(i, u, 0)
                    group(i, u, 3)
                    turn(i, u, 1)
                    turn(i, u, 2)
                    group(i, u, 4)
                    turn(i, u, 3)

        @block.gpsimd
        def _(pool):
            pool.sem_inc(rotated, 2)
            with pool.Fori(0, NT) as t:
                for r in range(4):
                    n, w = 4 * t + r, GROUPS[ROT[r]][1]
                    pool.wait_ge(scaled, n + 5)
                    pool.wait_ge(transposed, n + 1)
                    nc.gpsimd.tensor_tensor(turned[:, r % 2, 0:w], by_cos[:, r % 2, 0:w], by_sin[:, r % 2, 0:w],
                                            ALU.add).then_inc(rotated, 1)

        @block.scalar
        def _(act):
            act.sem_inc(stored, 64)
            with act.Fori(0, NT) as t:
                def pieces(r):
                    w = GROUPS[ROT[r]][1]
                    act.wait_ge(transposed, 4 * t + r + 3)
                    out = qkh[:, PIECE0[r]:PIECE0[r] + w // P, :].rearrange("p c n -> p (c n)")
                    nc.scalar.activation(out, pt[r % 2][:, 0:w], ACT.Copy).then_inc(qk_hi_done, 1)

                def v_part(j):
                    _, rot, v = GROUPS[j]
                    act.wait_ge(product[j], t + (3 if j == 4 else 1))
                    nc.scalar.activation(vh[:, VOFF[j]:VOFF[j] + v], pg[j][:, rot:rot + v], ACT.Copy).then_inc(v_hi_done, 1)

                act.wait_ge(stored, 64 * (t + 1))
                v_part(1)
                pieces(0)
                pieces(1)
                pieces(2)
                v_part(4)
                pieces(3)
                act.wait_ge(v_lo_done, 2 * t + 4)
                act.wait_ge(qk_lo_done, 4 * t + 6)
                cols = bass.ts(t, P)
                act.dma_start(qk_hi[:, :, cols].rearrange("c p n -> p c n"), f(qkh[:])).then_inc(stored, 16)
                act.dma_start(qk_lo[:, :, cols].rearrange("c p n -> p c n"), f(qkl[:])).then_inc(stored, 16)
                act.dma_start(v_hi[bass.ds(t, 1)].rearrange("a p n -> p (a n)"), f(vh[:])).then_inc(stored, 16)
                act.dma_start(v_lo[bass.ds(t, 1)].rearrange("a p n -> p (a n)"), f(vl[:])).then_inc(stored, 16)
            act.wait_ge(stored, 64 * (NT + 1))

        @block.vector
        def _(dve):
            dve.sem_inc(scaled, 4)
            dve.sem_inc(v_lo_done, 2)
            dve.sem_inc(qk_lo_done, 2)
            with dve.Fori(0, NT) as t:
                def rotate(r):
                    j = ROT[r]
                    w, b = GROUPS[j][1], r % 2
                    n = w // HD
                    dve.wait_ge(product[j], t + 1)
                    if j == 1:
                        dve.wait_ge(v_hi_done, 2 * t + 1)
                    dve.wait_ge(rotated, 4 * t + r + 1)
                    src = pg[j][:, 0:w].rearrange("p (h s d) -> p h s d", h=n, s=2)
                    out = by_sin[:, b, 0:w].rearrange("p (h s d) -> p h s d", h=n, s=2)
                    nc.vector.tensor_tensor(by_cos[:, b, 0:w].rearrange("p (h d) -> p h d", d=HALF),
                                            pg[j][:, 0:w].rearrange("p (h d) -> p h d", d=HALF),
                                            cos_t[:, bass.ds(t, 1), :].to_broadcast([P, 2 * n, HALF]), ALU.mult)
                    nc.vector.tensor_tensor(out[:, :, 0, :], src[:, :, 1, :],
                                            nsin_t[:, bass.ds(t, 1), :].to_broadcast([P, n, HALF]), ALU.mult)
                    last = nc.vector.tensor_tensor(out[:, :, 1, :], src[:, :, 0, :],
                                                   sin_t[:, bass.ds(t, 1), :].to_broadcast([P, n, HALF]), ALU.mult)
                    last.then_inc(scaled, 1)

                def low_v(j):
                    _, rot, v = GROUPS[j]
                    dve.wait_ge(v_hi_done, 2 * t + (1 if j == 1 else 2))
                    at = slice(VOFF[j], VOFF[j] + v)
                    nc.vector.tensor_tensor(vl[:, at], pg[j][:, rot:rot + v], f(vh[:, at]), ALU.subtract).then_inc(v_lo_done, 1)

                def low(r):
                    w = GROUPS[ROT[r]][1]
                    dve.wait_ge(qk_hi_done, 4 * t + r + 1)
                    at = slice(PIECE0[r], PIECE0[r] + w // P)
                    nc.vector.tensor_tensor(qkl[:, at, :].rearrange("p c n -> p (c n)"), pt[r % 2][:, 0:w],
                                            f(qkh[:, at, :]).rearrange("p c n -> p (c n)"), ALU.subtract).then_inc(qk_lo_done, 1)

                dve.wait_ge(stored, 64 * (t + 1))
                rotate(0)
                rotate(1)
                low_v(1)
                rotate(2)
                low(0)
                rotate(3)
                low(1)
                low(2)
                low_v(4)
                low(3)


def gates_phase(nc, w_in, b_gate, xt_hi, xt_lo, gates):
    with Phase(nc, "g") as ph:
        raw = ph.sb("raw", [P, 2, GATE])
        w_hi = ph.sb("w_hi", [P, KD, GATE], F32R)
        w_lo = ph.sb("w_lo", [P, KD, GATE], F32R)
        xh = ph.sb("xh", [P, 2, D], F32R)
        xl = ph.sb("xl", [P, 2, D], F32R)
        bias = ph.sb("bias", [P, GATE])
        out = ph.sb("out", [P, GATE])
        pg = [ph.ps(f"pg{j}", [P, BANK]) for j in range(8)]
        w_loaded, w_his, w_los = ph.sems("w_loaded", 2), ph.sem("w_his"), ph.sem("w_los")
        x_loaded, b_loaded = ph.sems("x_loaded", 2), ph.sem("b_loaded")
        product, biased, gated, stored = ph.sem("product"), ph.sem("biased"), ph.sem("gated"), ph.sem("stored")
        block = ph.block()
        NG4 = GATE // BANK

        @block.sync
        def _(sp):
            sp.dma_start(bias[:], b_gate.to_broadcast([P, GATE])).then_inc(b_loaded, 16)
            with sp.Fori(0, KD // 2) as i:
                for w in range(2):
                    k = 2 * i + w
                    sp.wait_ge(w_los, k + 1)
                    sp.dma_start(raw[:, w, :], w_in[0, bass.ts(k, P), QKV:QKV + GATE]).then_inc(w_loaded[w], 16)
            with sp.Fori(0, NT // 2) as i:
                for u in range(2):
                    t = 2 * i + u
                    sp.wait_ge(product, NG4 * t + NG4)
                    sp.dma_start(f(xh[:, u, :]), xt_hi[bass.ds(t, 1)]).then_inc(x_loaded[u], 16)
                    sp.dma_start(f(xl[:, u, :]), xt_lo[bass.ds(t, 1)]).then_inc(x_loaded[u], 16)

        @block.tensor
        def _(pe):
            pe.sem_inc(product, 2 * NG4)
            with pe.Fori(0, NT // 2) as i:
                for u in range(2):
                    t = 2 * i + u
                    pe.wait_ge(x_loaded[u], 32 * (i + 1))
                    for j in range(NG4):
                        pe.wait_ge(biased, NG4 * t + j + 1)
                        bank = pg[4 * u + j]
                        for k in range(KD):
                            if u == 0 and j == 0:
                                pe.wait_ge(w_los, 3 + k)
                            ks, cs = slice(k * P, (k + 1) * P), slice(j * BANK, (j + 1) * BANK)
                            nc.tensor.matmul(bank[:], xh[:, u, ks], w_hi[:, k, cs], start=(k == 0), stop=False)
                            nc.tensor.matmul(bank[:], xl[:, u, ks], w_hi[:, k, cs], start=False, stop=False)
                            last = nc.tensor.matmul(bank[:], xh[:, u, ks], w_lo[:, k, cs], start=False, stop=(k == KD - 1))
                        last.then_inc(product, 1)

        @block.vector
        def _(dve):
            dve.sem_inc(w_los, 2)
            dve.sem_inc(biased, 2 * NG4)
            with dve.Fori(0, KD) as k:
                dve.wait_ge(w_his, k + 1)
                nc.vector.tensor_tensor(w_lo[:, bass.ds(k, 1), :], raw[:, bass.ds(k % 2, 1), :],
                                        f(w_hi[:, bass.ds(k, 1), :]), ALU.subtract).then_inc(w_los, 1)
            dve.wait_ge(b_loaded, 16)
            with dve.Fori(0, NT // 2) as i:
                for u in range(2):
                    for j in range(NG4):
                        t = 2 * i + u
                        dve.wait_ge(product, NG4 * t + j + 1 + 2 * NG4)
                        if j == 0:
                            dve.wait_ge(stored, 16 * (t + 1))
                        at = slice(j * BANK, (j + 1) * BANK)
                        nc.vector.tensor_tensor(out[:, at], pg[4 * u + j][:], bias[:, at], ALU.add).then_inc(biased, 1)

        @block.scalar
        def _(act):
            act.sem_inc(stored, 16)
            with act.Fori(0, KD // 2) as i:
                for w in range(2):
                    k = 2 * i + w
                    act.wait_ge(w_loaded[w], 16 * (i + 1))
                    nc.scalar.activation(w_hi[:, bass.ds(k, 1), :], raw[:, w:w + 1, :], ACT.Copy).then_inc(w_his, 1)
            with act.Fori(0, NT) as t:
                act.wait_ge(biased, NG4 * t + 3 * NG4)
                nc.scalar.activation(out[:], out[:], ACT.Sigmoid).then_inc(gated, 1)
                act.wait_ge(gated, t + 1)
                act.dma_start(gates[bass.ts(t, P), :], out[:]).then_inc(stored, 16)
            act.wait_ge(stored, 16 * (NT + 1))


def window_attention_phase(nc, sinks, ident, qk_hi, qk_lo, v_hi, v_lo, oa, w_slices, w_hi, w_lo):
    assert len(w_slices) == NT
    W = CHUNK + P
    GH = A_HEADS // A_KV
    assert A_KV == 2
    UNITS = A_KV * NT
    with Phase(nc, "a") as ph:
        qs = ph.sb("qs", [P, 2, A_HEADS, P], F32R)
        kh = ph.sb("kh", [P, 2, A_KV, W], F32R)
        kl = ph.sb("kl", [P, 2, A_KV, W], F32R)
        vph = ph.sb("vph", [CHUNK, 2, A_K], F32R)
        vpl = ph.sb("vpl", [CHUNK, 2, A_K], F32R)
        vch = ph.sb("vch", [P, 2, A_K], F32R)
        vcl = ph.sb("vcl", [P, 2, A_K], F32R)
        pr = ph.sb("pr", [P, A_KV, GH, W])
        tph = ph.sb("tph", [CHUNK, A_KV, GH, P], F32R)
        tpl = ph.sb("tpl", [CHUNK, A_KV, GH, P], F32R)
        tch = ph.sb("tch", [P, A_KV, GH, P], F32R)
        tcl = ph.sb("tcl", [P, A_KV, GH, P], F32R)
        o = ph.sb("o", [P, 2, A_KV, GH, HD])
        sink = ph.sb("sink", [P, A_KV, GH])
        mx, m, nb, se, den, inv, sums, diff = (ph.sb(n, [P, A_KV, GH]) for n in
                                               ("mx", "m", "nb", "se", "den", "inv", "sums", "diff"))
        raw = ph.sb("raw", [P, 2, D])
        mask_f = ph.sb("mask_f", [P, P + 2 * W])
        mask = ph.sb("mask", [P, P + 2 * W], F32R)
        bank = [ph.ps(f"s{g}", [P, GH // 2, BANK]) for g in range(A_KV)]
        tp = ph.ps("tp", [CHUNK, GH, P])
        tc = ph.ps("tc", [P, GH, P])
        po = [ph.ps(f"o{g}", [P, BANK]) for g in range(A_KV)]
        qk_loaded, v_loaded = ph.sems("qk_loaded", 2), ph.sems("v_loaded", 2)
        mask_step, sink_in = ph.sem("mask_step"), ph.sem("sink_in")
        scores, maxed, summed, exped = ph.sem("scores"), ph.sem("maxed"), ph.sem("summed"), ph.sem("exped")
        turned, t_hi, t_lo, pv, scaled = (ph.sem(n) for n in ("turned", "t_hi", "t_lo", "pv", "scaled"))
        stored = ph.sems("stored", 2)
        w_in, w_his, w_los = ph.sems("w_in", 2), ph.sem("w_his"), ph.sem("w_los")
        block = ph.block()

        def score(g, j):
            return bank[g][:, j // 2, (j % 2) * W:(j % 2 + 1) * W]

        @block.sync
        def _(sp):
            sp.dma_start(sink[:], sinks.rearrange("a (g h) -> a g h", g=A_KV).to_broadcast([P, A_KV, GH])).then_inc(sink_in, 16)
            for u in range(2):
                sp.sem_inc(stored[u], 16)

            def load_qk(t, u):
                cols = bass.ts(t, P)
                prev = slice(0, CHUNK) if isinstance(t, int) and t == 0 else bass.ds(t * P - CHUNK, CHUNK)
                for half, src in ((0, qk_hi), (1, qk_lo)):
                    rows = slice(half * HD, (half + 1) * HD)
                    sp.dma_start(f(qs[rows, u]), src[0:4, :, cols].rearrange("c (b p) n -> p (c b) n", b=2)).then_inc(qk_loaded[u], 16)
                    for dst, ksrc in ((kh, qk_hi), (kl, qk_lo)):
                        k = ksrc[4].rearrange("(g p) n -> p g n", g=A_KV)
                        sp.dma_start(f(dst[rows, u, :, 0:CHUNK]), k[:, :, prev]).then_inc(qk_loaded[u], 16)
                        sp.dma_start(f(dst[rows, u, :, CHUNK:W]), k[:, :, cols]).then_inc(qk_loaded[u], 16)

            def load_v(t, u):
                first = isinstance(t, int) and t == 0
                tile, rows = (slice(0, 1), slice(0, CHUNK)) if first else (bass.ds(t - 1, 1), slice(CHUNK, P))
                for dp, dc, src in ((vph, vch, v_hi), (vpl, vcl, v_lo)):
                    sp.dma_start(f(dp[:, u, :]), src[tile, rows, 0:A_K].rearrange("a p n -> p (a n)")).then_inc(v_loaded[u], 16)
                    sp.dma_start(f(dc[:, u, :]), src[bass.ds(t, 1), :, 0:A_K].rearrange("a p n -> p (a n)")).then_inc(v_loaded[u], 16)

            def store(t, u):
                sp.wait_ge(scaled, 2 * t + 4)
                sp.dma_start(oa[bass.ts(t, P), :], o[:, u].rearrange("p g h d -> p (g h d)")).then_inc(stored[u], 16)

            def step(s, u):
                sp.wait_ge(scores, 2 * s + 2)
                load_qk(s + 2, u)
                sp.wait_ge(pv, 2 * s)
                load_v(s + 1, 1 - u)
                store(s - 1, 1 - u)

            load_qk(0, 0)
            load_v(0, 0)
            load_qk(1, 1)
            load_v(1, 1)
            sp.wait_ge(scores, 2)
            load_qk(2, 0)
            with sp.Fori(0, NT // 2 - 2) as i:
                step(2 * i + 1, 1)
                step(2 * i + 2, 0)
            step(NT - 3, 1)
            sp.wait_ge(pv, 2 * (NT - 2))
            load_v(NT - 1, 1)
            for t in range(NT - 3, NT):
                store(t, t % 2)
            for u in range(2):
                sp.wait_ge(stored[u], 16 * (NT // 2 + 1))

        @block.gpsimd
        def _(pool):
            nc.gpsimd.memset(mask_f[:], 0.0).then_inc(mask_step, 1)
            pool.wait_ge(mask_step, 1)
            nc.gpsimd.memset(mask_f[0:1, 0:CHUNK], 1.0).then_inc(mask_step, 1)
            nc.gpsimd.memset(mask_f[32:33, CHUNK:P], 1.0).then_inc(mask_step, 1)
            for first in range(2):
                m0 = P + W * first
                nc.gpsimd.memset(mask_f[0:1, m0 + P:m0 + W], NEG).then_inc(mask_step, 1)
                nc.gpsimd.memset(mask_f[32:33, m0:m0 + CHUNK], NEG).then_inc(mask_step, 1)
            nc.gpsimd.memset(mask_f[0:1, P + W:P + W + CHUNK], NEG).then_inc(mask_step, 1)
            for n, (w, k) in enumerate(w_slices):
                if n >= 2:
                    pool.wait_ge(w_los, n - 1)
                pool.dma_start(raw[:, n % 2, :], w[0, k * P:(k + 1) * P, :]).then_inc(w_in[n % 2], 16)

        def over_tiles(eng, unit):
            for g in range(A_KV):
                unit(g, 0, 0, g, n0=True if g == 0 else False, tail=False)
            with eng.Fori(0, NT // 2 - 1) as i:
                for w in range(2):
                    for g in range(A_KV):
                        unit(2 * (2 * i + 1 + w) + g, i + w, 1 - w, g, n0=False, tail=False)
            for g in range(A_KV):
                unit(UNITS - 2 + g, NT // 2 - 1, 1, g, n0=False, tail=True)

        def tile_of(k, u):
            return 2 * k + u

        @block.tensor
        def _(pe):
            pe.wait_ge(mask_step, 9)

            def scores_of(k, u, g, first):
                if g == 0:
                    pe.wait_ge(qk_loaded[u], 10 * 16 * (k + 1))
                for j in range(GH):
                    q = qs[:, u, GH * g + j, :]
                    nc.tensor.matmul(score(g, j), q, kh[:, u, g, :], start=True, stop=False)
                    nc.tensor.matmul(score(g, j), q, kl[:, u, g, :], start=False, stop=False)
                    m0 = P + W * first
                    last = nc.tensor.matmul(score(g, j), mask[:, 0:P], mask[:, m0:m0 + W], start=False, stop=True)
                last.then_inc(scores, 1)

            def values_of(n, k, u, g):
                pe.wait_ge(t_lo, 2 * n + 4)
                pe.wait_ge(scaled, n + 1)
                if g == 0:
                    pe.wait_ge(v_loaded[u], 4 * 16 * (k + 1))
                vs = slice(g * HD, (g + 1) * HD)
                for j in range(GH):
                    out = po[g][:, j * HD:(j + 1) * HD]
                    nc.tensor.matmul(out, tch[:, g, j, :], vch[:, u, vs], start=True, stop=False)
                    nc.tensor.matmul(out, tcl[:, g, j, :], vch[:, u, vs], start=False, stop=False)
                    nc.tensor.matmul(out, tch[:, g, j, :], vcl[:, u, vs], start=False, stop=False)
                    nc.tensor.matmul(out, tph[:, g, j, :], vph[:, u, vs], start=False, stop=False)
                    nc.tensor.matmul(out, tpl[:, g, j, :], vph[:, u, vs], start=False, stop=False)
                    last = nc.tensor.matmul(out, tph[:, g, j, :], vpl[:, u, vs], start=False, stop=True)
                last.then_inc(pv, 1)

            def unit(n, k, u, g, n0, tail):
                pe.wait_ge(exped, n + 1)
                pe.wait_ge(t_lo, 2 * n + 2)
                for j in range(GH):
                    nc.tensor.transpose(tc[:, j, :], pr[:, g, j, CHUNK:W], ident[:])
                    last = nc.tensor.transpose(tp[:, j, :], pr[:, g, j, 0:CHUNK], ident[:])
                last.then_inc(turned, 1)
                if not tail:
                    scores_of(k + u, 1 - u, g, 0)
                if not n0:
                    if g:
                        values_of(n - 1, k, u, 0)
                    else:
                        values_of(n - 1, k - (1 - u), 1 - u, 1)

            scores_of(0, 0, 0, 1)
            scores_of(0, 0, 1, 1)
            over_tiles(pe, unit)
            values_of(UNITS - 1, NT // 2 - 1, 1, 1)

        @block.scalar
        def _(act):
            def exps(n, g):
                act.wait_ge(maxed, 3 * n + 3)
                for j in range(GH):
                    nc.scalar.activation(pr[:, g, j, :], score(g, j), ACT.Exp, bias=nb[:, g, j:j + 1], scale=SCALE,
                                         accum_out=sums[:, g, j:j + 1])
                nc.scalar.activation(se[:, g, :], diff[:, g, :], ACT.Exp).then_inc(exped, 1)

            def unit(n, k, u, g, n0, tail):
                act.wait_ge(turned, n + 1)
                nc.scalar.activation(tph[:, g], tp[:], ACT.Copy).then_inc(t_hi, 1)
                nc.scalar.activation(tch[:, g], tc[:], ACT.Copy).then_inc(t_hi, 1)
                if not (tail and g):
                    exps(n + 1, 1 - g)
                if g:
                    act.wait_ge(w_in[u], 16 * (k + 1))
                    nc.scalar.activation(w_hi[:, bass.ds(tile_of(k, u), 1), :], raw[:, u:u + 1, :], ACT.Copy).then_inc(w_his, 1)

            exps(0, 0)
            over_tiles(act, unit)

        @block.vector
        def _(dve):
            dve.sem_inc(t_lo, 2)
            dve.sem_inc(scaled, 2)
            dve.wait_ge(mask_step, 8)
            nc.vector.tensor_copy(mask[:], mask_f[:]).then_inc(mask_step, 1)
            dve.wait_ge(sink_in, 16)

            def maxima(n, g):
                dve.wait_ge(scores, n + 1)
                nc.vector.tensor_reduce(mx[:, g, :].rearrange("p (a b) -> p a b", b=2),
                                        bank[g][:, :, 0:2 * W].rearrange("p a (b w) -> p a b w", b=2),
                                        axis=AX.X, op=ALU.max).then_inc(maxed, 1)
                dve.wait_ge(maxed, 3 * n + 1)
                nc.vector.scalar_tensor_tensor(m[:, g, :], mx[:, g, :], SCALE, sink[:, g, :], ALU.mult, ALU.max).then_inc(maxed, 1)
                dve.wait_ge(maxed, 3 * n + 2)
                nc.vector.tensor_tensor(diff[:, g, :], sink[:, g, :], m[:, g, :], ALU.subtract)
                nc.vector.tensor_scalar(nb[:, g, :], m[:, g, :], -1.0, None, ALU.mult).then_inc(maxed, 1)

            def scale(n, k, u, g):
                dve.wait_ge(pv, n + 1)
                if g == 0:
                    dve.wait_ge(stored[u], 16 * (k + 1))
                nc.vector.tensor_tensor(o[:, u, g], po[g][:, 0:GH * HD].rearrange("p (h d) -> p h d", h=GH),
                                        inv[:, g, :].unsqueeze(2).to_broadcast([P, GH, HD]), ALU.mult).then_inc(scaled, 1)

            def unit(n, k, u, g, n0, tail):
                dve.wait_ge(t_hi, 2 * n + 1)
                nc.vector.tensor_tensor(tpl[:, g], tp[:], f(tph[:, g]), ALU.subtract).then_inc(t_lo, 1)
                dve.wait_ge(t_hi, 2 * n + 2)
                nc.vector.tensor_tensor(tcl[:, g], tc[:], f(tch[:, g]), ALU.subtract).then_inc(t_lo, 1)
                dve.wait_ge(exped, n + 1)
                nc.vector.tensor_tensor(den[:, g, :], sums[:, g, :], se[:, g, :], ALU.add).then_inc(summed, 1)
                dve.wait_ge(summed, 2 * n + 1)
                nc.vector.reciprocal(inv[:, g, :], den[:, g, :]).then_inc(summed, 1)
                if not tail:
                    maxima(n + 2, g)
                if not n0:
                    dve.wait_ge(summed, 2 * n)
                    if g:
                        scale(n - 1, k, u, 0)
                    else:
                        scale(n - 1, k - (1 - u), 1 - u, 1)
                if g:
                    dve.wait_ge(w_his, tile_of(k, u) + 1)
                    nc.vector.tensor_tensor(w_lo[:, bass.ds(tile_of(k, u), 1), :], raw[:, u:u + 1, :],
                                            f(w_hi[:, bass.ds(tile_of(k, u), 1), :]), ALU.subtract).then_inc(w_los, 1)

            maxima(0, 0)
            maxima(1, 1)
            over_tiles(dve, unit)
            dve.wait_ge(summed, 2 * UNITS)
            scale(UNITS - 1, NT // 2 - 1, 1, 1)


def diff_attention_phase(nc, lambdas, ident, qk_hi, qk_lo, v_hi, v_lo, ob):
    MAPS = 2
    NQ = SEQ // P
    NCH = SEQ // BANK
    AHEAD = 2
    groups = [(i * P + P + BANK - 1) // BANK for i in range(NQ)]
    before = [sum(groups[:i]) for i in range(NQ + 1)]
    GB = before[NQ]
    SB = MAPS * GB

    def keys(i, g):
        return slice(g * BANK, min((g + 1) * BANK, (i + 1) * P))

    with Phase(nc, "b") as ph:
        qs = ph.sb("qs", [P, MAPS, SEQ], F32R)
        kh = ph.sb("kh", [P, MAPS, SEQ], F32R)
        kl = ph.sb("kl", [P, MAPS, SEQ], F32R)
        vh = ph.sb("vh", [P, NT, BV], F32R)
        vl = ph.sb("vl", [P, NT, BV], F32R)
        sc = ph.sb("sc", [P, AHEAD + 1, MAPS, SEQ])
        at = ph.sb("at", [P, SEQ])
        th = ph.sb("th", [P, SEQ], F32R)
        tl = ph.sb("tl", [P, SEQ], F32R)
        o = ph.sb("o", [P, 2, BV])
        mx = ph.sb("mx", [P, AHEAD + 1, MAPS, NCH])
        mall = ph.sb("mall", [P, AHEAD + 1, MAPS])
        nb = ph.sb("nb", [P, AHEAD + 1, MAPS])
        sums = ph.sb("sums", [P, AHEAD + 1, MAPS])
        inv = ph.sb("inv", [P, AHEAD + 1, MAPS])
        coef = ph.sb("coef", [P, AHEAD + 1])
        lam_in = ph.sb("lam_in", [P, 4, HD])
        lam_prod = ph.sb("lam_prod", [P, 2, HD])
        lam_sum = ph.sb("lam_sum", [P, 2])
        lam_exp = ph.sb("lam_exp", [P, 2])
        neg_lam = ph.sb("neg_lam", [P, 1])
        mask_f = ph.sb("mask_f", [P, 2, P])
        mask = ph.sb("mask", [P, 2, P], F32R)
        bank = [ph.ps(f"s{j}", [P, BANK]) for j in range(4)]
        pt = [ph.ps(f"t{j}", [P, BANK]) for j in range(2)]
        po = [ph.ps(f"o{j}", [P, BV]) for j in range(2)]
        qk_loaded, v_loaded = ph.sems("qk_loaded", NCH), ph.sems("v_loaded", NCH)
        scores, copied, biased, exped = ph.sem("scores"), ph.sem("copied"), ph.sem("biased"), ph.sem("exped")
        combined, turned, t_hi, t_lo = ph.sem("combined"), ph.sem("turned"), ph.sem("t_hi"), ph.sem("t_lo")
        pv, scaled, stored = ph.sem("pv"), ph.sem("scaled"), ph.sems("stored", 2)
        lam_loaded, lam_step, lam_ready, mask_step = ph.sem("lam_loaded"), ph.sem("lam_step"), ph.sem("lam_ready"), ph.sem("mask_step")
        maxed, inverted, coefed = ph.sem("maxed"), ph.sem("inverted"), ph.sem("coefed")
        block = ph.block()

        @block.sync
        def _(sp):
            for n, lam in enumerate(lambdas):
                sp.dma_start(lam_in[:, n, :], lam.to_broadcast([P, HD])).then_inc(lam_loaded, 16)
            with sp.Fori(0, B_HEADS) as h:
                sp.wait_ge(scores, SB * h + 1)
                for c in range(NCH):
                    cols = slice(c * BANK, (c + 1) * BANK)

                    def part(src, piece):
                        return src[bass.ds(h + piece, 1), :, cols].rearrange("a (m p) n -> p (a m) n", m=MAPS)

                    for half, q_src in ((0, qk_hi), (1, qk_lo)):
                        at_ = slice(half * HD, (half + 1) * HD)
                        sp.dma_start(f(qs[at_, :, cols]), part(q_src, 5)).then_inc(qk_loaded[c], 16)
                        sp.dma_start(f(kh[at_, :, cols]), part(qk_hi, 9)).then_inc(qk_loaded[c], 16)
                        sp.dma_start(f(kl[at_, :, cols]), part(qk_lo, 9)).then_inc(qk_loaded[c], 16)
                sp.wait_ge(pv, NQ * h + 1)
                for c in range(NCH):
                    ts = slice(4 * c, 4 * c + 4)
                    vc = bass.ds(h * BV + A_K, BV)
                    sp.dma_start(f(vh[:, ts, :]), v_hi[ts, :, vc].rearrange("t p n -> p t n")).then_inc(v_loaded[c], 16)
                    sp.dma_start(f(vl[:, ts, :]), v_lo[ts, :, vc].rearrange("t p n -> p t n")).then_inc(v_loaded[c], 16)

        @block.gpsimd
        def _(pool):
            nc.gpsimd.memset(mask_f[:], 0.0).then_inc(mask_step, 1)
            pool.wait_ge(mask_step, 1)
            nc.gpsimd.memset(mask_f[0:1, 0, 0:CHUNK], 1.0).then_inc(mask_step, 1)
            nc.gpsimd.memset(mask_f[0:1, 1, CHUNK:P], NEG).then_inc(mask_step, 1)
            with pool.Fori(0, B_HEADS) as h:
                for i in range(NQ):
                    pool.wait_ge(scaled, NQ * h + i + 3)
                    pool.dma_start(ob[i * P:(i + 1) * P, bass.ds(h * BV, BV)], o[:, i % 2, :]).then_inc(stored[i % 2], 16)
            for u in range(2):
                pool.wait_ge(stored[u], 16 * NQ * B_HEADS // 2)

        @block.tensor
        def _(pe):
            pe.sem_inc(scores, 1)
            pe.sem_inc(pv, 1)
            pe.wait_ge(mask_step, 4)

            def scores_of(h, i, g):
                ks = keys(i, g)
                diag = ks.stop == (i + 1) * P
                if i % 4 == 0 and diag:
                    pe.wait_ge(qk_loaded[g], 96 * (h + 1))
                for m in range(MAPS):
                    n = MAPS * (before[i] + g) + m
                    pe.wait_ge(copied, SB * h + n + 1)
                    q = qs[:, m, i * P:(i + 1) * P]
                    out = bank[n % 4][:, 0:ks.stop - ks.start]
                    nc.tensor.matmul(out, q, kh[:, m, ks], start=True, stop=False)
                    last = nc.tensor.matmul(out, q, kl[:, m, ks], start=False, stop=not diag)
                    if diag:
                        last = nc.tensor.matmul(out[:, i * P - ks.start:], mask[:, 0, :], mask[:, 1, :], start=False, stop=True)
                    last.then_inc(scores, 1)

            def turn(h, i, g):
                n = before[i] + g
                pe.wait_ge(combined, GB * h + n + 1)
                pe.wait_ge(t_lo, GB * h + n + 1)
                ks = keys(i, g)
                for c in range(ks.start, ks.stop, P):
                    last = nc.tensor.transpose(pt[n % 2][:, c - ks.start:c - ks.start + P], at[:, c:c + P], ident[:])
                last.then_inc(turned, 1)

            def values_of(h, i, g):
                pe.wait_ge(t_lo, GB * h + before[i] + g + 3)
                ks = keys(i, g)
                if g == 0:
                    pe.wait_ge(scaled, NQ * h + i + 1)
                if i % 4 == 0 and ks.stop == (i + 1) * P:
                    pe.wait_ge(v_loaded[g], 32 * (h + 1))
                for c in range(ks.start, ks.stop, P):
                    b, bs = c // P, slice(c, c + P)
                    nc.tensor.matmul(po[i % 2][:], th[:, bs], vh[:, b, :], start=(b == 0), stop=False)
                    nc.tensor.matmul(po[i % 2][:], tl[:, bs], vh[:, b, :], start=False, stop=False)
                    last = nc.tensor.matmul(po[i % 2][:], th[:, bs], vl[:, b, :], start=False, stop=(b == i))
                if ks.stop == (i + 1) * P:
                    last.then_inc(pv, 1)

            with pe.Fori(0, B_HEADS) as h:
                for i in range(AHEAD):
                    for g in range(groups[i]):
                        scores_of(h, i, g)
                for i in range(NQ):
                    nxt = groups[i + AHEAD] if i + AHEAD < NQ else 0
                    for g in range(min(2, groups[i])):
                        turn(h, i, g)
                    for g in range(max(groups[i], nxt)):
                        if g < nxt:
                            scores_of(h, i + AHEAD, g)
                        if g < groups[i]:
                            values_of(h, i, g)
                        if g + 2 < groups[i]:
                            turn(h, i, g + 2)

        @block.scalar
        def _(act):
            act.wait_ge(lam_step, 2)
            nc.scalar.activation(lam_exp[:], lam_sum[:], ACT.Exp).then_inc(lam_ready, 1)

            def exps(h, i, m):
                u, L = i % (AHEAD + 1), (i + 1) * P
                act.wait_ge(biased, NQ * h + i + 1)
                nc.scalar.activation(sc[:, u, m, 0:L], sc[:, u, m, 0:L], ACT.Exp, bias=nb[:, u, m:m + 1],
                                     scale=SCALE, accum_out=sums[:, u, m:m + 1]).then_inc(exped, 1)

            def high(h, i, g):
                n, ks = before[i] + g, keys(i, g)
                act.wait_ge(turned, GB * h + n + 1)
                nc.scalar.activation(th[:, ks], pt[n % 2][:, 0:ks.stop - ks.start], ACT.Copy).then_inc(t_hi, 1)

            with act.Fori(0, B_HEADS) as h:
                for m in range(MAPS):
                    exps(h, 0, m)
                for i in range(NQ):
                    for g in range(max(groups[i], 3)):
                        if g < groups[i]:
                            high(h, i, g)
                        if g >= 1 and g - 1 < MAPS and i + 1 < NQ:
                            exps(h, i + 1, g - 1)

        @block.vector
        def _(dve):
            dve.sem_inc(copied, 4)
            dve.sem_inc(t_lo, 2)
            dve.wait_ge(mask_step, 3)
            nc.vector.tensor_copy(mask[:], mask_f[:]).then_inc(mask_step, 1)
            dve.wait_ge(lam_loaded, 64)
            nc.vector.tensor_tensor(lam_prod[:], lam_in[:, 0:4:2, :], lam_in[:, 1:4:2, :], ALU.mult).then_inc(lam_step, 1)
            dve.wait_ge(lam_step, 1)
            nc.vector.reduce_sum(lam_sum[:], lam_prod[:], axis=AX.X).then_inc(lam_step, 1)
            dve.wait_ge(lam_ready, 1)
            nc.vector.tensor_tensor(neg_lam[:], lam_exp[:, 1:2], lam_exp[:, 0:1], ALU.subtract).then_inc(lam_step, 1)
            dve.wait_ge(lam_step, 3)
            nc.vector.tensor_scalar(neg_lam[:], neg_lam[:], -LAM_INIT, None, ALU.add).then_inc(lam_step, 1)
            dve.wait_ge(lam_step, 4)
            dve.sem_inc(scaled, 2)

            def copies(h, i, g):
                u, ks = i % (AHEAD + 1), keys(i, g)
                for m in range(MAPS):
                    n = MAPS * (before[i] + g) + m
                    dve.wait_ge(scores, SB * h + n + 2)
                    nc.vector.tensor_scalar(sc[:, u, m, ks], bank[n % 4][:, 0:ks.stop - ks.start], 1.0, NEG, ALU.mult, ALU.max,
                                            accum_out=mx[:, u, m, g:g + 1]).then_inc(copied, 1)
                if ks.stop == (i + 1) * P:
                    k = NQ * h + i
                    dve.wait_ge(copied, SB * h + n + 5)
                    nc.vector.reduce_max(mall[:, u, :], mx[:, u, :, 0:g + 1], axis=AX.X).then_inc(maxed, 1)
                    dve.wait_ge(maxed, k + 1)
                    nc.vector.tensor_scalar(nb[:, u, :], mall[:, u, :], -SCALE, None, ALU.mult).then_inc(biased, 1)

            def weigh(h, i):
                u, k = i % (AHEAD + 1), NQ * h + i
                dve.wait_ge(exped, MAPS * (k + 1))
                nc.vector.reciprocal(inv[:, u, :], sums[:, u, :]).then_inc(inverted, 1)
                dve.wait_ge(inverted, k + 1)
                nc.vector.scalar_tensor_tensor(coef[:, u:u + 1], inv[:, u, 1:2], neg_lam[:], sums[:, u, 0:1],
                                               ALU.mult, ALU.mult).then_inc(coefed, 1)
                dve.wait_ge(coefed, k + 1)

            def combine(h, i, g):
                u, ks = i % (AHEAD + 1), keys(i, g)
                if i and g < groups[i - 1]:
                    dve.wait_ge(turned, GB * h + before[i - 1] + g + 1)
                nc.vector.scalar_tensor_tensor(at[:, ks], sc[:, u, 1, ks], coef[:, u:u + 1], sc[:, u, 0, ks],
                                               ALU.mult, ALU.add).then_inc(combined, 1)

            def low(h, i, g):
                n, ks = before[i] + g, keys(i, g)
                dve.wait_ge(t_hi, GB * h + n + 1)
                nc.vector.tensor_tensor(tl[:, ks], pt[n % 2][:, 0:ks.stop - ks.start], f(th[:, ks]), ALU.subtract).then_inc(t_lo, 1)

            def finish(h, i):
                dve.wait_ge(pv, NQ * h + i + 2)
                if i >= 2:
                    dve.wait_ge(stored[i % 2], 16 * (NQ // 2 * h + i // 2))
                nc.vector.tensor_scalar(o[:, i % 2, :], po[i % 2][:], inv[:, i % (AHEAD + 1), 0:1], None, ALU.mult).then_inc(scaled, 1)

            with dve.Fori(0, B_HEADS) as h:
                for i in range(AHEAD):
                    for g in range(groups[i]):
                        copies(h, i, g)
                for i in range(NQ):
                    nxt = groups[i + AHEAD] if i + AHEAD < NQ else 0
                    weigh(h, i)
                    for g in range(min(2, groups[i])):
                        combine(h, i, g)
                    if i:
                        finish(h, i - 1)
                    for g in range(max(groups[i], nxt)):
                        if g < groups[i]:
                            low(h, i, g)
                        if g + 2 < groups[i]:
                            combine(h, i, g + 2)
                        if g < nxt:
                            copies(h, i + AHEAD, g)
                finish(h, NQ - 1)
                dve.wait_ge(stored[0], 16 * (NQ // 2) * (h + 1))
                dve.wait_ge(stored[1], 16 * (NQ // 2) * (h + 1))


def merge_phase(nc, ident, w_hi, w_lo, oa, ob, gates, x, subln_g, ln_g, ln_b, x1):
    KA, KB = A_Q // P, B_V // P
    with Phase(nc, "m") as ph:
        gt = ph.sb("gt", [P, 2, GATE])
        xin = ph.sb("xin", [P, 2, D])
        oin = ph.sb("oin", [P, 2, A_Q + B_V])
        abh, abl = ph.sb("abh", [P, D], F32R), ph.sb("abl", [P, D], F32R)
        mh, ml = ph.sb("mh", [P, D], F32R), ph.sb("ml", [P, D], F32R)
        pa = ph.sb("pa", [P, D])
        pb = ph.sb("pb", [P, D])
        y = ph.sb("y", [P, 2, D])
        gam = ph.sb("gam", [P, D])
        bet = ph.sb("bet", [P, D])
        sg = ph.sb("sg", [P, BV])
        eps = ph.sb("eps", [P, 1])
        ss, rt, ri = (ph.sb(n, [P, B_HEADS]) for n in ("ss", "rt", "ri"))
        st = ph.sb("st", [P, 2, 6])
        mv = ph.sb("mv", [P, 2])
        sd, rs = ph.sb("sd", [P, 1]), ph.sb("rs", [P, 1])
        pt = ph.ps("pt", [P, D])
        psa, psb, psw = ph.ps("psa", [P, D]), ph.ps("psb", [P, D]), ph.ps("psw", [P, D])
        passed = ph.sem("passed")
        vec_in, vec_step = ph.sem("vec_in"), ph.sem("vec_step")
        oin_in, gt_in, xin_in = ph.sems("oin_in", 2), ph.sems("gt_in", 2), ph.sems("xin_in", 2)
        squared, rooted, normed, rms_step, norm_step = (ph.sem(n) for n in ("squared", "rooted", "normed", "rms_step", "norm_step"))
        ab_turned, ab_hi, ab_lo = ph.sem("ab_turned"), ph.sem("ab_hi"), ph.sem("ab_lo")
        m_turned, m_hi, m_lo = ph.sem("m_turned"), ph.sem("m_hi"), ph.sem("m_lo")
        a_done, b_done, w_done = ph.sem("a_done"), ph.sem("b_done"), ph.sem("w_done")
        gated_a, gated_b, mixed, y_done = (ph.sem(n) for n in ("gated_a", "gated_b", "mixed", "y_done"))
        var_done, sd_done, centred, affine = (ph.sem(n) for n in ("var_done", "sd_done", "centred", "affine"))
        out_step, stored = ph.sem("out_step"), ph.sems("stored", 2)
        block = ph.block()

        def is_tile(t):
            return not isinstance(t, int) or 0 <= t < NT

        def over_steps(eng, step):
            step(0, 0, 0)
            step(1, 0, 1)
            with eng.Fori(1, NT // 2 - 1) as i:
                for u in range(2):
                    step(2 * i + u, i, u)
            for t in range(NT - 2, NT + 2):
                step(t, t // 2, t % 2)

        @block.sync
        def _(sp):
            for src, dst in ((ln_g, gam), (ln_b, bet)):
                sp.dma_start(dst[:], src.to_broadcast([P, D])).then_inc(vec_in, 16)
            sp.dma_start(sg[:], subln_g.to_broadcast([P, BV])).then_inc(vec_in, 16)

            def load_o(t, u):
                sp.dma_start(oin[:, u, 0:A_Q], oa[bass.ts(t, P), :]).then_inc(oin_in[u], 16)
                sp.dma_start(oin[:, u, A_Q:], ob[bass.ts(t, P), :]).then_inc(oin_in[u], 16)

            def load_g(t, u):
                sp.dma_start(gt[:, u, :], gates[bass.ts(t, P), :]).then_inc(gt_in[u], 16)

            def load_x(t, u):
                sp.dma_start(xin[:, u, :], x[0, bass.ts(t, P), :]).then_inc(xin_in[u], 16)

            def step(t, k, u):
                if is_tile(t + 2):
                    sp.wait_ge(ab_turned, t + 1)
                    load_o(t + 2, u)
                if is_tile(t - 1) and is_tile(t + 1):
                    sp.wait_ge(gated_b, t)
                    load_g(t + 1, 1 - u)
                if is_tile(t - 2) and is_tile(t):
                    sp.wait_ge(y_done, t - 1)
                    load_x(t, u)

            for u in range(2):
                load_o(u, u)
                load_g(u, u)
                load_x(u, u)
            over_steps(sp, step)

        @block.tensor
        def _(pe):
            def turn(src, done):
                for k in range(KD):
                    last = nc.tensor.transpose(pt[:, k * P:(k + 1) * P], src[:, k * P:(k + 1) * P], ident[:])
                last.then_inc(done, 1)

            def product(out, hi, lo, ks, w0, done):
                for k in ks:
                    for j in range(D // BANK):
                        js, at, kw = slice(j * BANK, (j + 1) * BANK), slice(k * P, (k + 1) * P), w0 + k
                        nc.tensor.matmul(out[:, js], hi[:, at], w_hi[:, kw, js], start=(k == ks[0]), stop=False)
                        nc.tensor.matmul(out[:, js], lo[:, at], w_hi[:, kw, js], start=False, stop=False)
                        last = nc.tensor.matmul(out[:, js], hi[:, at], w_lo[:, kw, js], start=False, stop=(k == ks[-1]))
                last.then_inc(done, 1)

            def step(t, k, u):
                if is_tile(t):
                    pe.wait_ge(ab_lo, t + 1)
                if is_tile(t - 1):
                    pe.wait_ge(mixed, t)
                    turn(pa, m_turned)
                if is_tile(t):
                    if is_tile(t - 1):
                        pe.wait_ge(gated_a, t)
                    product(psa, abh, abl, range(0, KA), 0, a_done)
                    if is_tile(t - 1):
                        pe.wait_ge(gated_b, t)
                    product(psb, abh, abl, range(KA, KA + KB), 0, b_done)
                if is_tile(t - 1):
                    pe.wait_ge(m_lo, t)
                if is_tile(t + 1):
                    pe.wait_ge(normed, t + 2)
                    turn(oin[:, 1 - u, :], ab_turned)
                if is_tile(t - 1):
                    if is_tile(t - 2):
                        pe.wait_ge(y_done, t - 1)
                    product(psw, mh, ml, range(KD), KA + KB, w_done)

            pe.wait_ge(normed, 1)
            turn(oin[:, 0, :], ab_turned)
            over_steps(pe, step)

        @block.scalar
        def _(act):
            act.wait_ge(vec_step, 2)
            for u in range(2):
                act.sem_inc(stored[u], 16)

            def root(t):
                act.wait_ge(squared, t + 1)
                nc.scalar.activation(rt[:], ss[:], ACT.Sqrt, bias=eps[:], scale=1.0 / BV).then_inc(rooted, 1)

            def high_ab(t):
                act.wait_ge(ab_turned, t + 1)
                nc.scalar.activation(abh[:], pt[:], ACT.Copy).then_inc(ab_hi, 1)

            def step(t, k, u):
                if is_tile(t - 1):
                    act.wait_ge(m_turned, t)
                    nc.scalar.activation(mh[:], pt[:], ACT.Copy).then_inc(m_hi, 1)
                if is_tile(t + 1):
                    root(t + 1)
                if is_tile(t - 2):
                    act.wait_ge(var_done, t - 1)
                    nc.scalar.activation(sd[:], mv[:, 1:2], ACT.Sqrt, bias=eps[:]).then_inc(sd_done, 1)
                if is_tile(t + 1):
                    high_ab(t + 1)
                if is_tile(t - 2):
                    act.wait_ge(affine, t - 1)
                    act.dma_start(x1[bass.ts(t - 2, P), :], y[:, u, :]).then_inc(stored[u], 16)

            root(0)
            high_ab(0)
            over_steps(act, step)
            for u in range(2):
                act.wait_ge(stored[u], 16 * (NT // 2 + 1))

        @block.gpsimd
        def _(pool):
            nc.gpsimd.memset(eps[:], EPS).then_inc(vec_step, 1)
            pool.wait_ge(vec_in, 48)

            def step(t, k, u):
                if is_tile(t - 2):
                    pool.wait_ge(centred, t - 1)
                    nc.gpsimd.tensor_tensor(y[:, u, :], y[:, u, :], gam[:], ALU.mult).then_inc(out_step, 1)
                    pool.wait_ge(out_step, t - 1)
                    nc.gpsimd.tensor_tensor(y[:, u, :], y[:, u, :], bet[:], ALU.add).then_inc(affine, 1)
                if is_tile(t):
                    pool.wait_ge(gated_b, t + 1)
                    nc.gpsimd.tensor_tensor(pa[:], pa[:], pb[:], ALU.add).then_inc(mixed, 1)

            over_steps(pool, step)

        @block.vector
        def _(dve):
            dve.wait_ge(vec_in, 48)
            nc.vector.tensor_scalar(sg[:], sg[:], 1.0 - LAM_INIT, None, ALU.mult).then_inc(vec_step, 1)
            dve.wait_ge(vec_step, 2)

            def heads(ap):
                return ap.rearrange("p (h d) -> p h d", h=B_HEADS)

            def rms(t, k, u):
                b = oin[:, u, A_Q:]
                dve.wait_ge(oin_in[u], 32 * (k + 1))
                nc.vector.tensor_tensor(pb[:, 0:B_V], b, b, ALU.mult).then_inc(rms_step, 1)
                dve.wait_ge(rms_step, 3 * t + 1)
                nc.vector.reduce_sum(ss[:], heads(pb[:, 0:B_V]), axis=AX.X).then_inc(squared, 1)
                dve.wait_ge(rooted, t + 1)
                nc.vector.reciprocal(ri[:], rt[:]).then_inc(rms_step, 1)
                dve.wait_ge(rms_step, 3 * t + 2)
                nc.vector.tensor_tensor(heads(b), heads(b), ri[:].unsqueeze(2).to_broadcast([P, B_HEADS, BV]), ALU.mult).then_inc(rms_step, 1)
                dve.wait_ge(rms_step, 3 * t + 3)
                nc.vector.tensor_tensor(heads(b), heads(b), sg[:].unsqueeze(1).to_broadcast([P, B_HEADS, BV]), ALU.mult).then_inc(normed, 1)

            def low_ab(t):
                dve.wait_ge(ab_hi, t + 1)
                nc.vector.tensor_tensor(abl[:], pt[:], f(abh[:]), ALU.subtract).then_inc(ab_lo, 1)

            def norm(t, k, u):
                dve.wait_ge(w_done, t + 1)
                dve.wait_ge(xin_in[u], 16 * (k + 1))
                dve.wait_ge(stored[u], 16 * (k + 1))
                nc.vector.scalar_tensor_tensor(y[:, u, :], xin[:, u, :], ALPHA, psw[:], ALU.mult, ALU.add).then_inc(y_done, 1)
                dve.wait_ge(y_done, t + 1)
                nc.vector.bn_stats(st[:, 0, :], y[:, u, 0:BANK])
                nc.vector.bn_stats(st[:, 1, :], y[:, u, BANK:]).then_inc(norm_step, 1)
                dve.wait_ge(norm_step, 2 * t + 1)
                settled(dve, passed)
                nc.vector.bn_aggr(mv[:], st[:]).then_inc(var_done, 1)
                dve.wait_ge(sd_done, t + 1)
                nc.vector.reciprocal(rs[:], sd[:]).then_inc(norm_step, 1)
                dve.wait_ge(norm_step, 2 * t + 2)
                nc.vector.tensor_scalar(y[:, u, :], y[:, u, :], mv[:, 0:1], rs[:], ALU.subtract, ALU.mult).then_inc(centred, 1)

            def step(t, k, u):
                if is_tile(t - 1):
                    dve.wait_ge(m_hi, t)
                    nc.vector.tensor_tensor(ml[:], pt[:], f(mh[:]), ALU.subtract).then_inc(m_lo, 1)
                if is_tile(t + 1):
                    rms(t + 1, k + u, 1 - u)
                if is_tile(t - 2):
                    norm(t - 2, k - 1, u)
                if is_tile(t):
                    dve.wait_ge(a_done, t + 1)
                    dve.wait_ge(gt_in[u], 16 * (k + 1))
                    nc.vector.tensor_tensor(pa[:], psa[:], gt[:, u, 0:D], ALU.mult).then_inc(gated_a, 1)
                    dve.wait_ge(b_done, t + 1)
                    nc.vector.tensor_tensor(pb[:], psb[:], gt[:, u, D:], ALU.mult).then_inc(gated_b, 1)
                if is_tile(t + 1):
                    low_ab(t + 1)

            rms(0, 0, 0)
            low_ab(0)
            over_steps(dve, step)


def route_phase(nc, ident, x1, w_group, b_group, w_router, b_router, slots, wts, bounds, slot_token):
    NL = NG + NE
    with Phase(nc, "r") as ph:
        xin = ph.sb("xin", [P, 2, D])
        th = ph.sb("th", [P, 2, D], F32R)
        tl = ph.sb("tl", [P, 2, D], F32R)
        wr = ph.sb("wr", [P, KD, NL])
        wr_hl = ph.sb("wr_hl", [P, KD, 2 * NL], F32R)
        wr_hi, wr_lo = wr_hl[:, :, 0:NL], wr_hl[:, :, NL:]
        br = ph.sb("br", [P, NL])
        lg = ph.sb("lg", [P, NT, NL])
        tri, ones = ph.sb("tri", [P, P]), ph.sb("ones", [P, P])
        desc_i, desc = ph.sb("desc_i", [P, EPG], I32), ph.sb("desc", [P, EPG])
        tok_i, tok = ph.sb("tok_i", [P, NT], I32), ph.sb("tok", [P, NT])
        zero = ph.sb("zero", [MAXT + 1, P])
        gm, km, z, pg, m1, m2, e2, rr = (ph.sb(n, [P, NT, 1]) for n in ("gm", "km", "z", "pg", "m1", "m2", "e2", "rr"))
        gk, gsel, gexp = (ph.sb(n, [P, NT, NG]) for n in ("gk", "gsel", "gexp"))
        el, ek, sel1, sel2, el2 = (ph.sb(n, [P, NT, EPG]) for n in ("el", "ek", "sel1", "sel2", "el2"))
        o1, o2, both, wide = (ph.sb(n, [P, NT, NG, EPG]) for n in ("o1", "o2", "both", "wide"))
        before = ph.sb("before", [P, NT + 1, NE])
        place = ph.sb("place", [P, NT, NE])
        cnt, cnt_f, tiles, first, ones32 = ph.sb("cnt", [P, NE], I32), *(ph.sb(n, [P, NE]) for n in ("cnt_f", "tiles", "first", "ones32"))
        incl = ph.sb("incl", [P, NE])
        base = ph.sb("base", [P, NE])
        slot_f = ph.sb("slot_f", [P, 2, NT])
        pt = ph.ps("pt", [P, 2, D])
        pl = ph.ps("pl", [P, 2, BANK])
        pp = ph.ps("pp", [P, NT, NE])
        pc = ph.ps("pc", [P, NE])
        loaded, w_loaded, consts, split = ph.sems("loaded", 2), ph.sem("w_loaded"), ph.sem("consts"), ph.sem("split")
        turned, t_hi, t_lo, product, logits = (ph.sem(n) for n in ("turned", "t_hi", "t_lo", "product", "logits"))
        chain, exp_in, exp_out, counted, zeroed, scattered = (ph.sem(n) for n in ("chain", "exp_in", "exp_out", "counted", "zeroed", "scattered"))
        placed, summed = ph.sem("placed"), ph.sem("summed")
        block = ph.block()

        @block.sync
        def _(sp):
            with nc.allow_non_contiguous_dma("short rows of the router's weights"):
                sp.dma_start(wr[:, :, 0:NG], w_group[0].rearrange("(k p) n -> p k n", p=P)).then_inc(w_loaded, 16)
                sp.dma_start(wr[:, :, NG:], w_router[0].rearrange("(k p) n -> p k n", p=P)).then_inc(w_loaded, 16)
            sp.dma_start(br[:, 0:NG], b_group.to_broadcast([P, NG])).then_inc(w_loaded, 16)
            sp.dma_start(br[:, NG:], b_router.to_broadcast([P, NE])).then_inc(w_loaded, 16)
            sp.wait_ge(consts, 7)
            sp.dma_start(slot_token.rearrange("(t p) n -> t (p n)", p=P), zero[:]).then_inc(zeroed, 16)
            with sp.Fori(0, NT // 2) as i:
                for u in range(2):
                    sp.wait_ge(turned, 2 * i + u + 1)
                    sp.dma_start(xin[:, u, :], x1[bass.ts(2 * i + u, P), :]).then_inc(loaded[u], 16)

        @block.gpsimd
        def _(pool):
            nc.gpsimd.memset(ones[:], 1.0).then_inc(consts, 1)
            nc.gpsimd.memset(tri[:], 1.0).then_inc(consts, 1)
            pool.wait_ge(consts, 2)
            nc.gpsimd.affine_select(out=tri[:], in_=tri[:], compare_op=ALU.is_ge, fill=0.0, base=-1,
                                    pattern=[[1, P]], channel_multiplier=-1).then_inc(consts, 1)
            nc.gpsimd.iota(desc_i[:], [[-1, EPG]], base=EPG, channel_multiplier=0).then_inc(consts, 1)
            nc.gpsimd.iota(tok_i[:], [[P, NT]], base=0, channel_multiplier=1).then_inc(consts, 1)
            nc.gpsimd.memset(ones32[:], 1.0).then_inc(consts, 1)
            nc.gpsimd.memset(zero[:], 0.0).then_inc(consts, 1)
            pool.wait_ge(zeroed, 16)
            pool.wait_ge(placed, 1)
            for t in range(NT):
                for c in range(2):
                    pool.indirect_dma_start(out=slot_token, out_offset=bass.IndirectOffsetOnAxis(ap=slots[:, c, t:t + 1], axis=0),
                                            in_=tok[:, t:t + 1], in_offset=None).then_inc(scattered, 16)
            pool.wait_ge(scattered, 16 * 2 * NT)

        @block.tensor
        def _(pe):
            pe.sem_inc(turned, 2)
            pe.wait_ge(split, 2)

            def turn(t, k, u):
                pe.wait_ge(loaded[u], 16 * (k + 1))
                pe.wait_ge(t_lo, t + 1)
                for c in range(KD):
                    last = nc.tensor.transpose(pt[:, u, c * P:(c + 1) * P], xin[:, u, c * P:(c + 1) * P], ident[:])
                last.then_inc(turned, 1)

            def logits_of(t, u):
                pe.wait_ge(t_lo, t + 3)
                pe.wait_ge(logits, t + 1)
                for c in range(KD):
                    at = slice(c * P, (c + 1) * P)

                    def high():
                        return nc.tensor.matmul(pl[:, u, 0:2 * NL], th[:, u, at], wr_hl[:, c, :], start=(c == 0), stop=(c == KD - 1))

                    if c == 0:
                        high()
                    nc.tensor.matmul(pl[:, u, 0:NL], tl[:, u, at], wr_hl[:, c, 0:NL], start=False, stop=False)
                    if c:
                        last = high()
                last.then_inc(product, 1)

            turn(0, 0, 0)
            with pe.Fori(0, NT // 2 - 1) as i:
                for u in range(2):
                    turn(2 * i + u + 1, i + u, 1 - u)
                    logits_of(2 * i + u, u)
            turn(NT - 1, NT // 2 - 1, 1)
            logits_of(NT - 2, 0)
            logits_of(NT - 1, 1)
            pe.wait_ge(counted, 1)
            nc.tensor.matmul(pp[:].rearrange("p t e -> p (t e)"), tri[:], both[:].rearrange("p t g e -> p (t g e)"), start=True, stop=False)
            nc.tensor.matmul(pp[:].rearrange("p t e -> p (t e)"), ones[:], before[:, 0:NT, :].rearrange("p t e -> p (t e)"), start=False, stop=True)
            nc.tensor.matmul(pc[:], ones[:], before[:, NT, :], start=True, stop=True).then_inc(product, 1)

        @block.scalar
        def _(act):
            act.wait_ge(w_loaded, 64)
            nc.scalar.activation(wr_hi, wr[:], ACT.Copy).then_inc(split, 1)
            with act.Fori(0, NT // 2) as i:
                for u in range(2):
                    act.wait_ge(turned, 2 * i + u + 3)
                    nc.scalar.activation(th[:, u, :], pt[:, u, :], ACT.Copy).then_inc(t_hi, 1)
            act.wait_ge(exp_in, 1)
            nc.scalar.activation(gexp[:], gexp[:], ACT.Exp).then_inc(exp_out, 1)
            act.wait_ge(exp_in, 2)
            nc.scalar.activation(e2[:], e2[:], ACT.Exp).then_inc(exp_out, 1)

        @block.vector
        def _(dve):
            dve.sem_inc(t_lo, 2)
            dve.sem_inc(logits, 2)
            dve.wait_ge(split, 1)
            nc.vector.tensor_tensor(wr_lo, wr[:], f(wr_hi), ALU.subtract).then_inc(split, 1)

            def low(t, u):
                dve.wait_ge(t_hi, t + 1)
                nc.vector.tensor_tensor(tl[:, u, :], pt[:, u, :], f(th[:, u, :]), ALU.subtract).then_inc(t_lo, 1)

            def read(t, u):
                dve.wait_ge(product, t + 1)
                nc.vector.tensor_tensor(lg[:, bass.ds(t, 1), :], pl[:, u:u + 1, 0:NL], br[:].unsqueeze(1), ALU.add).then_inc(summed, 1)
                dve.wait_ge(summed, t + 1)
                nc.vector.tensor_tensor(lg[:, bass.ds(t, 1), :], pl[:, u:u + 1, NL:2 * NL], lg[:, bass.ds(t, 1), :], ALU.add).then_inc(logits, 1)

            low(0, 0)
            with dve.Fori(0, NT // 2 - 1) as i:
                for u in range(2):
                    low(2 * i + u + 1, 1 - u)
                    read(2 * i + u, u)
            low(NT - 1, 1)
            read(NT - 2, 0)
            read(NT - 1, 1)
            dve.wait_ge(logits, NT + 2)
            step = [0]

            def link(ins):
                step[0] += 1
                ins.then_inc(chain, 1)
                dve.wait_ge(chain, step[0])

            def over(ap, n):
                return ap.to_broadcast([P, NT, n])

            tt, ts, red = nc.vector.tensor_tensor, nc.vector.tensor_scalar, nc.vector.tensor_reduce
            dve.wait_ge(consts, 7)
            link(nc.vector.tensor_copy(desc[:], desc_i[:]))
            link(nc.vector.tensor_copy(tok[:], tok_i[:]))

            def first_of_best(vals, best, key, sel, n):
                link(red(best[:], vals, axis=AX.X, op=ALU.max))
                link(tt(key[:], vals, over(best[:], n), ALU.is_equal))
                link(tt(key[:], key[:], desc[:, 0:n].unsqueeze(1).to_broadcast([P, NT, n]), ALU.mult))
                link(red(km[:], key[:], axis=AX.X, op=ALU.max))
                link(tt(sel[:], key[:], over(km[:], n), ALU.is_equal))

            first_of_best(lg[:, :, 0:NG], gm, gk, gsel, NG)
            tt(gexp[:], lg[:, :, 0:NG], over(gm[:], NG), ALU.subtract).then_inc(exp_in, 1)
            gate4 = gsel[:].unsqueeze(3).to_broadcast([P, NT, NG, EPG])
            link(tt(wide[:], lg[:, :, NG:].rearrange("p t (g e) -> p t g e", g=NG), gate4, ALU.mult))
            link(red(el[:], wide[:].rearrange("p t g e -> p t e g"), axis=AX.X, op=ALU.add))
            first_of_best(el[:], m1, ek, sel1, EPG)
            link(nc.vector.scalar_tensor_tensor(el2[:], sel1[:], NEG, el[:], ALU.mult, ALU.add))
            first_of_best(el2[:], m2, ek, sel2, EPG)
            tt(e2[:], m2[:], m1[:], ALU.subtract).then_inc(exp_in, 1)
            for sel, o in ((sel1, o1), (sel2, o2)):
                link(tt(o[:], sel[:].unsqueeze(2).to_broadcast([P, NT, NG, EPG]), gate4, ALU.mult))
            nc.vector.memset(before[:, 0, :], 0.0)
            link(tt(both[:], o1[:], o2[:], ALU.add))
            for t in range(NT):
                ins = tt(before[:, t + 1, :], before[:, t, :], both[:, t].rearrange("p g e -> p (g e)"), ALU.add)
                if t < NT - 1:
                    link(ins)
            ins.then_inc(counted, 1)
            dve.wait_ge(exp_out, 2)
            link(red(z[:], gexp[:], axis=AX.X, op=ALU.add))
            link(nc.vector.reciprocal(pg[:], z[:]))
            link(ts(rr[:], e2[:], 1.0, None, ALU.add))
            link(nc.vector.reciprocal(rr[:], rr[:]))
            link(tt(wts[:, 0, :].unsqueeze(2), pg[:], rr[:], ALU.mult))
            link(tt(wts[:, 1, :].unsqueeze(2), wts[:, 0, :].unsqueeze(2), e2[:], ALU.mult))
            dve.wait_ge(product, NT + 1)
            link(ts(cnt_f[:], pc[:], float(P - 1), None, ALU.add))
            link(nc.vector.tensor_copy(cnt[:], cnt_f[:]))
            link(ts(cnt[:], cnt[:], 7, None, ALU.arith_shift_right))
            link(nc.vector.tensor_copy(tiles[:], cnt[:]))
            link(ts(tiles[:], tiles[:], 1.0, None, ALU.max))
            link(nc.vector.tensor_tensor_scan(incl[:], ones32[:], tiles[:], 0.0, ALU.mult, ALU.add))
            link(tt(first[:], incl[:], tiles[:], ALU.subtract))
            nc.vector.memset(bounds[:, 0:1], 0)
            link(nc.vector.tensor_copy(bounds[:, 1:NE + 1], incl[:]))
            link(ts(base[:], first[:], float(P), None, ALU.mult))
            link(tt(place[:], pp[:], base[:].unsqueeze(1).to_broadcast([P, NT, NE]), ALU.add))
            for c, o in enumerate((o1, o2)):
                link(tt(wide[:].rearrange("p t g e -> p t (g e)"), o[:].rearrange("p t g e -> p t (g e)"), place[:], ALU.mult))
                link(red(slot_f[:, c, :].unsqueeze(2), wide[:].rearrange("p t g e -> p t (g e)"), axis=AX.X, op=ALU.add))
            nc.vector.tensor_copy(slots[:], slot_f[:]).then_inc(placed, 1)


def expert_phase(nc, ident, x1, slot_token, bounds, w_gate_up, w_down, ys):
    KF = FF // P
    NS = KD + KF
    PIECES = 2
    HP = FF // PIECES
    with Phase(nc, "e") as ph:
        raw = ph.sb("raw", [P, NS, D])
        wh = ph.sb("wh", [P, NS, D], F32R)
        wl = ph.sb("wl", [P, NS, D], F32R)
        xg = ph.sb("xg", [P, D])
        xh = ph.sb("xh", [P, D], F32R)
        xl = ph.sb("xl", [P, D], F32R)
        act_g = ph.sb("act_g", [P, FF])
        h = ph.sb("h", [P, FF])
        hh = ph.sb("hh", [P, FF], F32R)
        hl = ph.sb("hl", [P, FF], F32R)
        yo = ph.sb("yo", [P, D])
        zero = ph.sb("zero", [P, D])
        tab = ph.sb("tab", [MAXT + 1, P])
        idx = ph.sb("idx", [P, MAXT + 1], I32)
        idx1 = ph.sb("idx1", [P, 1], I32)
        p_gate, p_up = ph.ps("p_gate", [P, FF]), ph.ps("p_up", [P, FF])
        py, px = ph.ps("py", [P, D]), ph.ps("px", [P, D])
        phh = [ph.ps(f"phh{p}", [P, BANK]) for p in range(PIECES)]
        passed = ph.sem("passed")
        tab_in, tab_turned, tab_done = ph.sem("tab_in"), ph.sem("tab_turned"), ph.sem("tab_done")
        raw_in = ph.sems("raw_in", NS)
        w_hi, w_lo = ph.sem("w_hi"), ph.sem("w_lo")
        picked, gathered, x_turned, x_hi, x_lo = (ph.sem(n) for n in ("picked", "gathered", "x_turned", "x_hi", "x_lo"))
        gate_done, up_done, silu_done, h_done, h_turned, h_hi, h_lo = (
            ph.sem(n) for n in ("gate_done", "up_done", "silu_done", "h_done", "h_turned", "h_hi", "h_lo"))
        down_done, y_out, stored = ph.sem("down_done"), ph.sem("y_out"), ph.sem("stored")
        zeroed, rest = ph.sem("zeroed"), ph.sem("rest")
        block = ph.block()

        def tiles(eng, e):
            b0 = eng.value_load(bounds[0:1, bass.ds(e, 1)], min_val=0, max_val=MAXT - 1)
            b1 = eng.value_load(bounds[0:1, bass.ds(e + 1, 1)], min_val=1, max_val=MAXT)
            return b0, b1

        def all_tiles(eng):
            return eng.value_load(bounds[0:1, NE:NE + 1], min_val=NE, max_val=MAXT)

        def piece(p):
            return slice(p * HP, (p + 1) * HP)

        @block.sync
        def _(sp):
            sp.dma_start(tab[:], slot_token.rearrange("(t p) n -> t (p n)", p=P)).then_inc(tab_in, 16)

            def load(e, s):
                src = w_gate_up if s < KD else w_down
                k = s if s < KD else s - KD
                sp.dma_start(raw[:, s, :], src[0, bass.ds(e, 1), k * P:(k + 1) * P, :].rearrange("a p n -> p (a n)")).then_inc(raw_in[s], 16)

            for s in range(NS):
                load(0, s)
            sp.wait_ge(zeroed, 1)
            n = all_tiles(sp)
            with sp.Fori(0, n) as _g:
                sp.sem_inc(rest, 16)
            with sp.Fori(n, MAXT + 1) as g:
                sp.dma_start(ys[bass.ts(g, P), :], zero[:]).then_inc(rest, 16)
            with sp.Fori(0, NE - 1) as e:
                for s in range(NS):
                    sp.wait_ge(w_lo, NS * e + s + 1)
                    load(e + 1, s)
            sp.wait_ge(rest, (MAXT + 1) * 16)

        @block.gpsimd
        def _(pool):
            nc.gpsimd.memset(zero[:], 0.0).then_inc(zeroed, 1)

            def gather(g):
                settled(pool, passed)
                nc.gpsimd.tensor_copy(idx1[:], idx[:, bass.ds(g, 1)]).then_inc(picked, 1)
                pool.wait_ge(picked, g + 1)
                settled(pool, passed)
                pool.indirect_dma_start(out=xg[:], out_offset=None, in_=x1,
                                        in_offset=bass.IndirectOffsetOnAxis(ap=idx1[:, 0:1], axis=0)).then_inc(gathered, 16)

            pool.wait_ge(tab_done, 1)
            gather(0)
            n = all_tiles(pool)
            with pool.Fori(0, n) as g:
                pool.wait_ge(x_turned, g + 1)
                gather(g + 1)
            pool.wait_ge(gathered, 16 * (n + 1))

        @block.tensor
        def _(pe):
            pe.sem_inc(up_done, 1)
            pe.sem_inc(down_done, 1)
            pe.wait_ge(tab_in, 16)
            nc.tensor.transpose(px[:, 0:MAXT + 1], tab[:], ident[0:MAXT + 1, 0:MAXT + 1]).then_inc(tab_turned, 1)

            def turn_x(ks):
                for k in ks:
                    last = nc.tensor.transpose(px[:, k * P:(k + 1) * P], xg[:, k * P:(k + 1) * P], ident[:])
                return last

            pe.wait_ge(gathered, 16)
            pe.wait_ge(x_lo, 1)
            turn_x(range(KD)).then_inc(x_turned, 1)
            with pe.Fori(0, NE) as e:
                b0, b1 = tiles(pe, e)
                with pe.Fori(b0, b1) as g:
                    pe.wait_ge(x_lo, g + 2)
                    for out, done, js in ((p_gate, gate_done, slice(0, FF)), (p_up, up_done, slice(FF, 2 * FF))):
                        for k in range(KD):
                            if out is p_gate:
                                pe.wait_ge(w_lo, NS * e + k + 1)
                            at = slice(k * P, (k + 1) * P)
                            nc.tensor.matmul(out[:], xh[:, at], wh[:, k, js], start=(k == 0), stop=False)
                            nc.tensor.matmul(out[:], xl[:, at], wh[:, k, js], start=False, stop=False)
                            last = nc.tensor.matmul(out[:], xh[:, at], wl[:, k, js], start=False, stop=(k == KD - 1))
                        last.then_inc(done, 1)
                    pe.wait_ge(gathered, 16 * (g + 2))
                    for p in range(PIECES):
                        last = turn_x(range(p * KD // PIECES, (p + 1) * KD // PIECES))
                        if p == PIECES - 1:
                            last.then_inc(x_turned, 1)
                        pe.wait_ge(h_done, PIECES * g + p + 1)
                        for k in range(p * HP // P, (p + 1) * HP // P):
                            c = k * P - p * HP
                            last = nc.tensor.transpose(phh[p][:, c:c + P], h[:, k * P:(k + 1) * P], ident[:])
                        last.then_inc(h_turned, 1)
                    pe.wait_ge(y_out, g + 1)
                    for k in range(KF):
                        pe.wait_ge(h_lo, PIECES * g + k * P // HP + 1)
                        pe.wait_ge(w_lo, NS * e + KD + k + 1)
                        at = slice(k * P, (k + 1) * P)
                        for j in range(D // BANK):
                            js = slice(j * BANK, (j + 1) * BANK)
                            nc.tensor.matmul(py[:, js], hh[:, at], wh[:, KD + k, js], start=(k == 0), stop=False)
                            nc.tensor.matmul(py[:, js], hl[:, at], wh[:, KD + k, js], start=False, stop=False)
                            last = nc.tensor.matmul(py[:, js], hh[:, at], wl[:, KD + k, js], start=False, stop=(k == KF - 1))
                    last.then_inc(down_done, 1)

        @block.scalar
        def _(act):
            act.sem_inc(y_out, 1)
            act.sem_inc(stored, 16)

            def high(e, b0, slices):
                for s in slices:
                    act.wait_ge(raw_in[s], 16 * (e + 1))
                    act.wait_ge(up_done if s < KD else down_done, b0 + 1)
                    nc.scalar.activation(wh[:, s, :], raw[:, s, :], ACT.Copy).then_inc(w_hi, 1)

            def high_x(g):
                act.wait_ge(x_turned, g + 1)
                nc.scalar.activation(xh[:], px[:], ACT.Copy).then_inc(x_hi, 1)

            def result(g):
                act.wait_ge(down_done, g + 2)
                act.wait_ge(stored, 16 * (g + 1))
                nc.scalar.activation(yo[:], py[:], ACT.Copy).then_inc(y_out, 1)
                act.wait_ge(y_out, g + 2)
                act.dma_start(ys[bass.ts(g, P), :], yo[:]).then_inc(stored, 16)

            def tile(g):
                act.wait_ge(gate_done, g + 1)
                nc.scalar.activation(act_g[:], p_gate[:], ACT.Silu).then_inc(silu_done, 1)
                for p in range(PIECES):
                    act.wait_ge(h_turned, PIECES * g + p + 1)
                    nc.scalar.activation(hh[:, piece(p)], phh[p][:, 0:HP], ACT.Copy).then_inc(h_hi, 1)
                high_x(g + 1)

            def expert(e):
                b0, b1 = tiles(act, e)
                tile(b0)
                with act.If(b0 + 1 < b1):
                    with act.Fori(b0 + 1, b1) as g:
                        result(g - 1)
                        tile(g)
                return b1

            high_x(0)
            high(0, 0, range(NS))
            with act.Fori(0, NE - 1) as e:
                b1 = expert(e)
                high(e + 1, b1, range(KD))
                result(b1 - 1)
                high(e + 1, b1, range(KD, NS))
            b1 = expert(NE - 1)
            result(b1 - 1)
            act.wait_ge(stored, 16 * (b1 + 1))
            settled(act, passed)

        @block.vector
        def _(dve):
            dve.wait_ge(tab_turned, 1)
            nc.vector.tensor_copy(idx[:], px[:, 0:MAXT + 1]).then_inc(tab_done, 1)
            dve.wait_ge(tab_done, 1)
            dve.sem_inc(x_lo, 1)

            def low_x(g):
                dve.wait_ge(x_hi, g + 1)
                nc.vector.tensor_tensor(xl[:], px[:], f(xh[:]), ALU.subtract).then_inc(x_lo, 1)

            low_x(0)
            with dve.Fori(0, NE) as e:
                for s in range(NS):
                    dve.wait_ge(w_hi, NS * e + s + 1)
                    nc.vector.tensor_tensor(wl[:, s, :], raw[:, s, :], f(wh[:, s, :]), ALU.subtract).then_inc(w_lo, 1)
                b0, b1 = tiles(dve, e)
                with dve.Fori(b0, b1) as g:
                    dve.wait_ge(silu_done, g + 1)
                    dve.wait_ge(up_done, g + 2)
                    for p in range(PIECES):
                        nc.vector.tensor_tensor(h[:, piece(p)], act_g[:, piece(p)], p_up[:, piece(p)], ALU.mult).then_inc(h_done, 1)
                    for p in range(PIECES):
                        dve.wait_ge(h_hi, PIECES * g + p + 1)
                        nc.vector.tensor_tensor(hl[:, piece(p)], phh[p][:, 0:HP], f(hh[:, piece(p)]), ALU.subtract).then_inc(h_lo, 1)
                    low_x(g + 1)


def combine_phase(nc, x1, ys, slots, wts, ln_g, ln_b, out):
    NB = 4
    with Phase(nc, "o") as ph:
        xin, y1, y2, z = (ph.sb(n, [P, NB, D]) for n in ("xin", "y1", "y2", "z"))
        sl = ph.sb("sl", [P, NB, 2, 1], I32)
        ww = ph.sb("ww", [P, NB, 2, 1])
        gam, bet = ph.sb("gam", [P, D]), ph.sb("bet", [P, D])
        st, mv = ph.sb("st", [P, NB, 2, 6]), ph.sb("mv", [P, NB, 2])
        sd, rs, shift = (ph.sb(n, [P, NB]) for n in ("sd", "rs", "shift"))
        eps = ph.sb("eps", [P, 1])
        passed = ph.sem("passed")
        vec_in, eps_set, loaded = ph.sem("vec_in"), ph.sem("eps_set"), ph.sems("loaded", NB)
        picked, got = ph.sem("picked"), ph.sems("got", NB)
        scaled, weighed, first_in, summed, counted = (ph.sem(n) for n in ("scaled", "weighed", "first_in", "summed", "counted"))
        var_done, sd_done, inverted, shifted, normed, times, finished = (
            ph.sem(n) for n in ("var_done", "sd_done", "inverted", "shifted", "normed", "times", "finished"))
        stored = ph.sems("stored", NB)
        block = ph.block()

        def over_steps(eng, step):
            def static(t):
                step(t, lambda j: ((t - j) % NB, (t - j) // NB) if 0 <= t - j < NT else None)

            for t in range(NB):
                static(t)
            with eng.Fori(1, NT // NB) as i:
                for v in range(NB):
                    step(NB * i + v, lambda j, v=v: ((v - j) % NB, i + (v - j) // NB))
            for t in range(NT, NT + NB + 1):
                static(t)

        @block.sync
        def _(sp):
            for src, dst in ((ln_g, gam), (ln_b, bet)):
                sp.dma_start(dst[:], src.to_broadcast([P, D])).then_inc(vec_in, 16)
            for b in range(NB):
                sp.sem_inc(stored[b], 16)

            def step(t, of):
                if of(0):
                    b, k = of(0)
                    if of(NB):
                        sp.wait_ge(scaled, t - NB + 1)
                    sp.dma_start(xin[:, b, :], x1[bass.ts(t, P), :]).then_inc(loaded[b], 16)
                if of(4):
                    b, k = of(4)
                    sp.wait_ge(finished, t - 3)
                    sp.dma_start(out[0, bass.ts(t - 4, P), :], z[:, b, :]).then_inc(stored[b], 16)

            over_steps(sp, step)
            for b in range(NB):
                sp.wait_ge(stored[b], 16 * (NT // NB + 1))

        @block.gpsimd
        def _(pool):
            pool.wait_ge(vec_in, 32)

            def step(t, of):
                if of(0):
                    b, k = of(0)
                    if of(NB):
                        pool.wait_ge(summed, t - NB + 1)
                        settled(pool, passed)
                    nc.gpsimd.tensor_copy(sl[:, b, :, :], slots[:, :, bass.ds(t, 1)]).then_inc(picked, 1)
                    pool.wait_ge(picked, t + 1)
                    settled(pool, passed)
                    for c, y in enumerate((y1, y2)):
                        pool.indirect_dma_start(out=y[:, b, :], out_offset=None, in_=ys,
                                                in_offset=bass.IndirectOffsetOnAxis(ap=sl[:, b, c, :], axis=0)).then_inc(got[b], 16)
                if of(4):
                    b, k = of(4)
                    pool.wait_ge(times, t - 3)
                    nc.gpsimd.tensor_tensor(z[:, b, :], z[:, b, :], bet[:], ALU.add).then_inc(finished, 1)

            over_steps(pool, step)

        @block.scalar
        def _(act):
            act.wait_ge(eps_set, 1)

            def step(t, of):
                if of(1):
                    b, k = of(1)
                    act.wait_ge(loaded[b], 16 * (k + 1))
                    act.wait_ge(stored[b], 16 * (k + 1))
                    nc.scalar.activation(z[:, b, :], xin[:, b, :], ACT.Copy, scale=ALPHA).then_inc(scaled, 1)
                if of(2):
                    b, k = of(2)
                    act.wait_ge(var_done, t - 1)
                    nc.scalar.activation(sd[:, b:b + 1], mv[:, b, 1:2], ACT.Sqrt, bias=eps[:]).then_inc(sd_done, 1)
                if of(3):
                    b, k = of(3)
                    act.wait_ge(shifted, t - 2)
                    nc.scalar.activation(z[:, b, :], z[:, b, :], ACT.Identity, bias=shift[:, b:b + 1],
                                         scale=rs[:, b:b + 1]).then_inc(normed, 1)

            over_steps(act, step)

        @block.vector
        def _(dve):
            nc.vector.memset(eps[:], EPS).then_inc(eps_set, 1)
            dve.wait_ge(vec_in, 32)

            def step(t, of):
                if of(2):
                    b, k = of(2)
                    zb = z[:, b, :]
                    nc.vector.tensor_copy(ww[:, b, :, :], wts[:, :, bass.ds(t - 2, 1)]).then_inc(weighed, 1)
                    dve.wait_ge(weighed, t - 1)
                    dve.wait_ge(scaled, t - 1)
                    dve.wait_ge(got[b], 32 * (k + 1))
                    nc.vector.scalar_tensor_tensor(zb, y1[:, b, :], ww[:, b, 0, :], zb, ALU.mult, ALU.add).then_inc(first_in, 1)
                    dve.wait_ge(first_in, t - 1)
                    nc.vector.scalar_tensor_tensor(zb, y2[:, b, :], ww[:, b, 1, :], zb, ALU.mult, ALU.add).then_inc(summed, 1)
                    dve.wait_ge(summed, t - 1)
                    nc.vector.bn_stats(st[:, b, 0, :], z[:, b, 0:BANK])
                    nc.vector.bn_stats(st[:, b, 1, :], z[:, b, BANK:]).then_inc(counted, 1)
                if of(3):
                    b, k = of(3)
                    dve.wait_ge(sd_done, t - 2)
                    nc.vector.reciprocal(rs[:, b:b + 1], sd[:, b:b + 1]).then_inc(inverted, 1)
                if of(2):
                    b, k = of(2)
                    dve.wait_ge(counted, t - 1)
                    settled(dve, passed)
                    nc.vector.bn_aggr(mv[:, b, :], st[:, b, :, :]).then_inc(var_done, 1)
                if of(3):
                    b, k = of(3)
                    dve.wait_ge(inverted, t - 2)
                    nc.vector.scalar_tensor_tensor(shift[:, b:b + 1], mv[:, b, 0:1], -1.0, rs[:, b:b + 1],
                                                   ALU.mult, ALU.mult).then_inc(shifted, 1)
                if of(4):
                    b, k = of(4)
                    dve.wait_ge(normed, t - 3)
                    nc.vector.tensor_tensor(z[:, b, :], z[:, b, :], gam[:], ALU.mult).then_inc(times, 1)

            over_steps(dve, step)


def program(nc, a, out, phases=99):
    def dram(name, shape):
        return nc.dram_tensor(name, shape, F32, kind="Internal").ap()

    xt_hi, xt_lo = dram("xt_hi", (NT, P, D)), dram("xt_lo", (NT, P, D))
    qk_hi, qk_lo = dram("qk_hi", (NPIECE, P, SEQ)), dram("qk_lo", (NPIECE, P, SEQ))
    v_hi, v_lo = dram("v_hi", (NT, P, VW)), dram("v_lo", (NT, P, VW))
    gates = dram("gates", (SEQ, GATE))
    with ExitStack() as ctx:
        ident = ctx.enter_context(nc.sbuf_tensor("ident", [P, P], F32))
        constants_phase(nc, ident, None)
        with Phase(nc, "qkv") as ph:
            w_hi = ph.sb("w_hi", [P, KD, QKV], F32R)
            w_lo = ph.sb("w_lo", [P, KD, QKV], F32R)
            cos_t, sin_t, nsin_t = (ph.sb(n, [P, NT, HALF]) for n in ("cos", "sin", "nsin"))
            prepare_phase(nc, a["x"], a["w_in"], a["positions"], a["inv_freq"], ident, w_hi, w_lo,
                          cos_t, sin_t, nsin_t, xt_hi, xt_lo)
            project_phase(nc, w_hi, w_lo, cos_t, sin_t, nsin_t, ident, xt_hi, xt_lo, qk_hi, qk_lo, v_hi, v_lo)
        gates_phase(nc, a["w_in"], a["b_gate"], xt_hi, xt_lo, gates)
        ob = dram("ob", (SEQ, B_V))
        diff_attention_phase(nc, [a["lambda_q1"], a["lambda_k1"], a["lambda_q2"], a["lambda_k2"]], ident, qk_hi, qk_lo, v_hi, v_lo, ob)
        oa = dram("oa", (SEQ, A_Q))
        x1 = dram("x1", (SEQ, D))
        w_slices = [(a[w], k) for w in ("w_proj_a", "w_proj_b", "w_out") for k in range(a[w].shape[1] // P)]
        with Phase(nc, "mw") as ph:
            w_hi = ph.sb("w_hi", [P, len(w_slices), D], F32R)
            w_lo = ph.sb("w_lo", [P, len(w_slices), D], F32R)
            window_attention_phase(nc, a["sinks"], ident, qk_hi, qk_lo, v_hi, v_lo, oa, w_slices, w_hi, w_lo)
            merge_phase(nc, ident, w_hi, w_lo, oa, ob, gates, a["x"], a["subln_g"], a["ln1_g"], a["ln1_b"], x1)
        slots = ctx.enter_context(nc.sbuf_tensor("slots", [P, 2, NT], I32))
        wts = ctx.enter_context(nc.sbuf_tensor("wts", [P, 2, NT], F32))
        bounds = ctx.enter_context(nc.sbuf_tensor("bounds", [P, NE + 1], I32))
        slot_token = dram("slot_token", ((MAXT + 1) * P, 1))
        ys = dram("ys", ((MAXT + 1) * P, D))
        route_phase(nc, ident, x1, a["w_group"], a["b_group"], a["w_router"], a["b_router"], slots, wts, bounds, slot_token)
        expert_phase(nc, ident, x1, slot_token, bounds, a["w_gate_up"], a["w_down"], ys)
        combine_phase(nc, x1, ys, slots, wts, a["ln2_g"], a["ln2_b"], out)


def rotary_frequencies():
    exponent = np.arange(0, HD, 2, dtype=np.float32) / np.float32(HD)
    return (np.float32(1.0) / np.float32(10000.0) ** exponent).astype(np.float32)[None]


_INS = ["x", "positions", "w_in", "b_gate", "sinks", "lambda_q1", "lambda_k1", "lambda_q2", "lambda_k2", "subln_g",
        "w_proj_a", "w_proj_b", "w_out", "ln1_g", "ln1_b", "w_group", "b_group", "w_router", "b_router", "w_gate_up",
        "w_down", "ln2_g", "ln2_b"]


def kernel(**inputs):
    import concourse.bacc as bacc
    from concourse.bass_utils import run_bass_kernel_spmd

    nc = bacc.Bacc("TRN2", target_bir_lowering=False, num_devices=1)
    arrays = {name: np.ascontiguousarray(inputs[name]) for name in _INS}
    arrays["inv_freq"] = rotary_frequencies()
    aps = {name: nc.dram_tensor(name, v.shape, mybir.dt.from_np(v.dtype), kind="ExternalInput").ap()
           for name, v in arrays.items()}
    out = nc.dram_tensor("out", (1, SEQ, D), F32, kind="ExternalOutput").ap()
    program(nc, aps, out)
    result = run_bass_kernel_spmd(nc, [arrays], core_ids=[0])
    return result.results[0]["out"]
```

```python
import math
from contextlib import ExitStack

import numpy as np

import concourse.bass as bass
from concourse import mybir
from concourse.alu_op_type import AluOpType as ALU

F32 = mybir.dt.float32
F32R = mybir.dt.float32r
I32 = mybir.dt.int32
ACT = mybir.ActivationFunctionType
AX = mybir.AxisListType

P = 128
SEQ = 2048
D = 1024
KD = D // P
NT = SEQ // P
CHUNK = 64
HD = 64
HALF = HD // 2
A_HEADS = 8
A_KV = 2
B_HEADS = 4
BV = 128
NG = 4
EPG = 8
NE = NG * EPG
FF = 512
ALPHA = 2.0 ** 0.25
EPS = 1e-5
NEG = -1e30
SCALE = HD ** -0.5
LAM_INIT = 0.8 - 0.6 * math.exp(0.0)

A_Q = A_HEADS * HD
A_K = A_KV * HD
B_QK = B_HEADS * 2 * HD
B_V = B_HEADS * BV
QKV = A_Q + 2 * A_K + 2 * B_QK + B_V
GATE = 2 * D
BANK = 512

GROUPS = [(0, 512, 0), (512, 128, 128), (768, 512, 0), (1280, 512, 0), (1792, 0, 512)]
PIECE0 = [0, 4, 5, 9]
NPIECE = 13
VW = A_K + B_V
MAXT = (2 * SEQ) // P + NE - 1


class Phase:

    def __init__(self, nc, name):
        self.nc, self.name, self.ctx, self.used = nc, name, ExitStack(), []

    def __enter__(self):
        self.ctx.__enter__()
        return self

    def __exit__(self, *a):
        done = self.ctx.__exit__(*a)
        if self.used:
            self.nc.clear_and_free_semaphores(self.used)
            self.nc.all_engine_barrier()
        return done

    def sb(self, name, shape, dt=F32):
        return self.ctx.enter_context(self.nc.sbuf_tensor(f"{self.name}_{name}", shape, dt))

    def ps(self, name, shape, dt=F32):
        return self.ctx.enter_context(self.nc.psum_tensor(f"{self.name}_{name}", shape, dt))

    def sem(self, name):
        self.used.append(self.nc.alloc_semaphore(f"{self.name}_{name}"))
        return self.used[-1]

    def sems(self, name, n):
        return [self.sem(f"{name}{i}") for i in range(n)]

    def block(self):
        return self.ctx.enter_context(self.nc.Block())


def settled(eng, passed):
    eng.sem_inc(passed, 1)


def f(ap):
    return ap.bitcast(F32)


def constants_phase(nc, ident, identr):
    with Phase(nc, "c") as ph:
        zeroed, made = ph.sem("zeroed"), ph.sem("made")
        block = ph.block()

        @block.gpsimd
        def _(pool):
            nc.gpsimd.memset(ident[:], 0.0).then_inc(zeroed, 1)
            pool.wait_ge(zeroed, 1)
            nc.gpsimd.affine_select(out=ident[:], in_=ident[:], compare_op=ALU.not_equal, fill=1.0, base=0,
                                    pattern=[[-1, P]], channel_multiplier=1).then_inc(made, 1)
            pool.wait_ge(made, 1)


def prepare_phase(nc, w_in, positions, inv_freq, w_hi, w_lo, cos_t, sin_t, nsin_t):
    NB = 4
    POOL_LOW = (1, 4, 6)
    two_pi = 2.0 * math.pi
    PI_IN = 3.1415925
    c1 = 6.28125
    c2 = float(np.float32(1.934051513671875e-3))
    c3 = float(two_pi - c1 - c2)
    with Phase(nc, "p") as ph:
        raw = ph.sb("raw", [P, NB, QKV])
        pos_i = ph.sb("pos_i", [P, NT], I32)
        pos_f = ph.sb("pos_f", [P, NT])
        inv = ph.sb("inv", [P, HALF])
        ang = ph.sb("ang", [P, NT, HALF])
        turns = ph.sb("turns", [P, NT, HALF])
        turns_i = ph.sb("turns_i", [P, NT, HALF], I32)
        red = ph.sb("red", [P, NT, HALF])
        w_loaded, w_his, w_los = ph.sems("w_loaded", NB), ph.sem("w_his"), ph.sems("w_los", NB)
        tables_in, table_step, angles, tables = ph.sem("tables_in"), ph.sem("table_step"), ph.sems("angles", 2), ph.sem("tables")
        tmp = ph.sb("tmp", [P, NT, HALF])
        block = ph.block()

        def low(eng, engine, k):
            eng.wait_ge(w_his, k + 1)
            engine.tensor_tensor(w_lo[:, k, 0:QKV], raw[:, k % NB, :], f(w_hi[:, k, 0:QKV]), ALU.subtract).then_inc(w_los[k % NB], 1)

        @block.gpsimd
        def _(pool):
            for k in POOL_LOW:
                low(pool, nc.gpsimd, k)

        @block.sync
        def _(sp):
            with nc.allow_non_contiguous_dma("one position a partition"):
                sp.dma_start(pos_i[:], positions.rearrange("b (t p) -> p (b t)", p=P)).then_inc(tables_in, 16)
            sp.dma_start(inv[:], inv_freq.to_broadcast([P, HALF])).then_inc(tables_in, 16)
            for k in range(KD):
                if k >= NB:
                    sp.wait_ge(w_los[k % NB], k // NB)
                sp.dma_start(raw[:, k % NB, :], w_in[0, k * P:(k + 1) * P, 0:QKV]).then_inc(w_loaded[k % NB], 16)

        @block.scalar
        def _(act):
            for k in range(KD):
                act.wait_ge(w_loaded[k % NB], 16 * (k // NB + 1))
                nc.scalar.activation(w_hi[:, k, 0:QKV], raw[:, k % NB, :], ACT.Copy).then_inc(w_his, 1)
            for n, (table, reduced) in enumerate(((sin_t, red), (cos_t, turns))):
                act.wait_ge(angles[n], 1)
                nc.scalar.activation(table[:], reduced[:], ACT.Sin).then_inc(tables, 1)
            act.wait_ge(tables, 2)
            nc.scalar.activation(nsin_t[:], sin_t[:], ACT.Copy, scale=-1.0).then_inc(tables, 1)
            act.wait_ge(tables, 3)

        @block.vector
        def _(dve):
            steps = [0]

            def link(ins):
                steps[0] += 1
                ins.then_inc(table_step, 1)
                dve.wait_ge(table_step, steps[0])

            rest = [k for k in range(KD) if k not in POOL_LOW]

            def lows(n):
                for _ in range(n):
                    low(dve, nc.vector, rest.pop(0))

            lows(1)
            dve.wait_ge(tables_in, 32)
            link(nc.vector.tensor_copy(pos_f[:], pos_i[:]))
            link(nc.vector.tensor_tensor(ang[:], pos_f[:].unsqueeze(2).to_broadcast([P, NT, HALF]),
                                         inv[:].unsqueeze(1).to_broadcast([P, NT, HALF]), ALU.mult))
            for n, out in enumerate((red, turns)):
                lows(1)
                link(nc.vector.tensor_scalar(out[:], ang[:], 1.0 / two_pi, 0.25 * n, ALU.mult, ALU.add))
                link(nc.vector.tensor_copy(turns_i[:], out[:]))
                link(nc.vector.tensor_copy(out[:], turns_i[:]))
                link(nc.vector.scalar_tensor_tensor(tmp[:], out[:], -c1, ang[:], ALU.mult, ALU.add))
                link(nc.vector.scalar_tensor_tensor(tmp[:], out[:], -c2, tmp[:], ALU.mult, ALU.add))
                link(nc.vector.scalar_tensor_tensor(tmp[:], out[:], -c3, tmp[:], ALU.mult, ALU.add))
                link(nc.vector.tensor_scalar(tmp[:], tmp[:], 0.5 * math.pi * n, None, ALU.add))
                link(nc.vector.tensor_scalar(out[:], tmp[:], math.pi, -two_pi, ALU.is_gt, ALU.mult))
                link(nc.vector.tensor_tensor(tmp[:], tmp[:], out[:], ALU.add))
                link(nc.vector.tensor_scalar(out[:], tmp[:], -math.pi, two_pi, ALU.is_lt, ALU.mult))
                link(nc.vector.tensor_tensor(tmp[:], tmp[:], out[:], ALU.add))
                link(nc.vector.tensor_scalar(tmp[:], tmp[:], PI_IN, None, ALU.min))
                nc.vector.tensor_scalar(out[:], tmp[:], -PI_IN, None, ALU.max).then_inc(angles[n], 1)
            lows(len(rest))
            for u in range(NB):
                dve.wait_ge(w_los[u], KD // NB)


def project_phase(nc, x, w_hi, w_lo, cos_t, sin_t, nsin_t, ident, xt_hi, xt_lo, qk_hi, qk_lo, v_hi, v_lo):
    HX = D // 2
    with Phase(nc, "j") as ph:
        x_in = ph.sb("x_in", [P, 2, D])
        xh = ph.sb("xh", [P, 2, D], F32R)
        xl = ph.sb("xl", [P, 2, D], F32R)
        by_cos = ph.sb("by_cos", [P, 2, BANK])
        by_sin = ph.sb("by_sin", [P, 2, BANK])
        turned = ph.sb("turned", [P, 2, BANK])
        qkh = ph.sb("qkh", [P, NPIECE, P], F32R)
        qkl = ph.sb("qkl", [P, NPIECE, P], F32R)
        vh = ph.sb("vh", [P, VW], F32R)
        vl = ph.sb("vl", [P, VW], F32R)
        pg = [ph.ps(f"pg{j}", [P, BANK]) for j in range(5)]
        pt = [ph.ps(f"pt{j}", [P, BANK]) for j in range(2)]
        px = ph.ps("px", [P, HX])
        x_loaded = ph.sems("x_loaded", 2)
        x_turned, x_hi, x_lo, x_stored = ph.sem("x_turned"), ph.sem("x_hi"), ph.sem("x_lo"), ph.sems("x_stored", 2)
        product = ph.sems("product", 5)
        v_hi_done, v_lo_done = ph.sem("v_hi_done"), ph.sem("v_lo_done")
        scaled, rotated = ph.sem("scaled"), ph.sem("rotated")
        transposed, qk_hi_done, qk_lo_done = ph.sem("transposed"), ph.sem("qk_hi_done"), ph.sem("qk_lo_done")
        stored = ph.sem("stored")
        block = ph.block()
        ROT = [j for j, g in enumerate(GROUPS) if g[1]]
        VOFF = {1: 0, 4: A_K}

        @block.sync
        def _(sp):
            def load(t, u):
                sp.dma_start(x_in[:, u, :], x[0, bass.ts(t, P), :]).then_inc(x_loaded[u], 16)

            def store(t, u):
                sp.wait_ge(x_lo, 2 * t + 3)
                sp.dma_start(xt_hi[bass.ds(t, 1)], f(xh[:, u, :])).then_inc(x_stored[u], 16)
                sp.dma_start(xt_lo[bass.ds(t, 1)], f(xl[:, u, :])).then_inc(x_stored[u], 16)

            for u in range(2):
                sp.sem_inc(x_stored[u], 32)
                load(u, u)
            with sp.Fori(0, NT // 2 - 1) as i:
                for u in range(2):
                    t = 2 * i + u
                    sp.wait_ge(x_turned, 2 * t + 2)
                    load(t + 2, u)
                    store(t, u)
            store(NT - 2, 0)
            store(NT - 1, 1)
            for u in range(2):
                sp.wait_ge(x_stored[u], 32 * (NT // 2 + 1))

        def over_tiles(eng, tile):
            with eng.Fori(0, NT // 2 - 1) as i:
                for u in range(2):
                    tile(2 * i + u, i, u, False)
            tile(NT - 2, NT // 2 - 1, 0, False)
            tile(NT - 1, NT // 2 - 1, 1, True)

        @block.tensor
        def _(pe):
            pe.sem_inc(transposed, 2)

            def group(i, u, j):
                t = 2 * i + u
                c0, rot, v = GROUPS[j]
                if v:
                    pe.wait_ge(v_lo_done, 2 * t + (1 if j == 1 else 2))
                if rot:
                    pe.wait_ge(scaled, 4 * t + ROT.index(j) + 1)
                for k in range(KD):
                    ks, cs = slice(k * P, (k + 1) * P), slice(c0, c0 + rot + v)
                    out = pg[j][:, 0:rot + v]
                    nc.tensor.matmul(out, xh[:, u, ks], w_hi[:, k, cs], start=(k == 0), stop=False)
                    nc.tensor.matmul(out, xl[:, u, ks], w_hi[:, k, cs], start=False, stop=False)
                    last = nc.tensor.matmul(out, xh[:, u, ks], w_lo[:, k, cs], start=False, stop=(k == KD - 1))
                last.then_inc(product[j], 1)

            def turn(i, u, r):
                n = 4 * (2 * i + u) + r
                pe.wait_ge(rotated, n + 3)
                pe.wait_ge(qk_lo_done, n + 1)
                for c in range(GROUPS[ROT[r]][1] // P):
                    last = nc.tensor.transpose(pt[r % 2][:, c * P:(c + 1) * P], turned[:, r % 2, c * P:(c + 1) * P], ident[:])
                last.then_inc(transposed, 1)

            def turn_x(t, k, u, half):
                if half == 0:
                    pe.wait_ge(x_loaded[u], 16 * (k + 1))
                pe.wait_ge(x_lo, 2 * t + half + 1)
                for c in range(0, HX, P):
                    at = half * HX + c
                    last = nc.tensor.transpose(px[:, c:c + P], x_in[:, u, at:at + P], ident[:])
                last.then_inc(x_turned, 1)

            def tile(t, i, u, last):
                def next_x(half):
                    if not last:
                        turn_x(t + 1, i + u, 1 - u, half)

                pe.wait_ge(x_lo, 2 * t + 3)
                group(i, u, 0)
                group(i, u, 1)
                next_x(0)
                group(i, u, 2)
                turn(i, u, 0)
                group(i, u, 3)
                next_x(1)
                turn(i, u, 1)
                turn(i, u, 2)
                group(i, u, 4)
                turn(i, u, 3)

            turn_x(0, 0, 0, 0)
            turn_x(0, 0, 0, 1)
            over_tiles(pe, tile)

        @block.gpsimd
        def _(pool):
            pool.sem_inc(rotated, 2)
            with pool.Fori(0, NT) as t:
                for r in range(4):
                    n, w = 4 * t + r, GROUPS[ROT[r]][1]
                    pool.wait_ge(scaled, n + 5)
                    pool.wait_ge(transposed, n + 1)
                    nc.gpsimd.tensor_tensor(turned[:, r % 2, 0:w], by_cos[:, r % 2, 0:w], by_sin[:, r % 2, 0:w],
                                            ALU.add).then_inc(rotated, 1)

        @block.scalar
        def _(act):
            act.sem_inc(stored, 64)

            def high_x(t, k, u, half):
                act.wait_ge(x_turned, 2 * t + half + 1)
                if half == 0:
                    act.wait_ge(x_stored[u], 32 * (k + 1))
                nc.scalar.activation(xh[:, u, half * HX:(half + 1) * HX], px[:], ACT.Copy).then_inc(x_hi, 1)

            def tile(t, i, u, last):
                def next_x(half):
                    if not last:
                        high_x(t + 1, i + u, 1 - u, half)

                def pieces(r):
                    w = GROUPS[ROT[r]][1]
                    act.wait_ge(transposed, 4 * t + r + 3)
                    out = qkh[:, PIECE0[r]:PIECE0[r] + w // P, :].rearrange("p c n -> p (c n)")
                    nc.scalar.activation(out, pt[r % 2][:, 0:w], ACT.Copy).then_inc(qk_hi_done, 1)

                def v_part(j):
                    _, rot, v = GROUPS[j]
                    act.wait_ge(product[j], t + 1)
                    nc.scalar.activation(vh[:, VOFF[j]:VOFF[j] + v], pg[j][:, rot:rot + v], ACT.Copy).then_inc(v_hi_done, 1)

                act.wait_ge(stored, 64 * (t + 1))
                v_part(1)
                next_x(0)
                pieces(0)
                next_x(1)
                pieces(1)
                pieces(2)
                v_part(4)
                pieces(3)
                act.wait_ge(v_lo_done, 2 * t + 4)
                act.wait_ge(qk_lo_done, 4 * t + 6)
                cols = bass.ts(t, P)
                act.dma_start(qk_hi[:, :, cols].rearrange("c p n -> p c n"), f(qkh[:])).then_inc(stored, 16)
                act.dma_start(qk_lo[:, :, cols].rearrange("c p n -> p c n"), f(qkl[:])).then_inc(stored, 16)
                act.dma_start(v_hi[bass.ds(t, 1)].rearrange("a p n -> p (a n)"), f(vh[:])).then_inc(stored, 16)
                act.dma_start(v_lo[bass.ds(t, 1)].rearrange("a p n -> p (a n)"), f(vl[:])).then_inc(stored, 16)

            high_x(0, 0, 0, 0)
            high_x(0, 0, 0, 1)
            over_tiles(act, tile)
            act.wait_ge(stored, 64 * (NT + 1))

        @block.vector
        def _(dve):
            dve.sem_inc(scaled, 4)
            dve.sem_inc(v_lo_done, 2)
            dve.sem_inc(qk_lo_done, 2)
            dve.sem_inc(x_lo, 1)

            def low_x(t, u, half):
                dve.wait_ge(x_hi, 2 * t + half + 1)
                at = slice(half * HX, (half + 1) * HX)
                nc.vector.tensor_tensor(xl[:, u, at], px[:], f(xh[:, u, at]), ALU.subtract).then_inc(x_lo, 1)

            def tile(t, i, u, last):
                def next_x(half):
                    if not last:
                        low_x(t + 1, 1 - u, half)

                def rotate(r):
                    j = ROT[r]
                    w, b = GROUPS[j][1], r % 2
                    n = w // HD
                    dve.wait_ge(product[j], t + 1)
                    if j == 1:
                        dve.wait_ge(v_hi_done, 2 * t + 1)
                    dve.wait_ge(rotated, 4 * t + r + 1)
                    src = pg[j][:, 0:w].rearrange("p (h s d) -> p h s d", h=n, s=2)
                    out = by_sin[:, b, 0:w].rearrange("p (h s d) -> p h s d", h=n, s=2)
                    nc.vector.tensor_tensor(by_cos[:, b, 0:w].rearrange("p (h d) -> p h d", d=HALF),
                                            pg[j][:, 0:w].rearrange("p (h d) -> p h d", d=HALF),
                                            cos_t[:, bass.ds(t, 1), :].to_broadcast([P, 2 * n, HALF]), ALU.mult)
                    nc.vector.tensor_tensor(out[:, :, 0, :], src[:, :, 1, :],
                                            nsin_t[:, bass.ds(t, 1), :].to_broadcast([P, n, HALF]), ALU.mult)
                    last = nc.vector.tensor_tensor(out[:, :, 1, :], src[:, :, 0, :],
                                                   sin_t[:, bass.ds(t, 1), :].to_broadcast([P, n, HALF]), ALU.mult)
                    last.then_inc(scaled, 1)

                def low_v(j):
                    _, rot, v = GROUPS[j]
                    dve.wait_ge(v_hi_done, 2 * t + (1 if j == 1 else 2))
                    at = slice(VOFF[j], VOFF[j] + v)
                    nc.vector.tensor_tensor(vl[:, at], pg[j][:, rot:rot + v], f(vh[:, at]), ALU.subtract).then_inc(v_lo_done, 1)

                def low(r):
                    w = GROUPS[ROT[r]][1]
                    dve.wait_ge(qk_hi_done, 4 * t + r + 1)
                    at = slice(PIECE0[r], PIECE0[r] + w // P)
                    nc.vector.tensor_tensor(qkl[:, at, :].rearrange("p c n -> p (c n)"), pt[r % 2][:, 0:w],
                                            f(qkh[:, at, :]).rearrange("p c n -> p (c n)"), ALU.subtract).then_inc(qk_lo_done, 1)

                dve.wait_ge(stored, 64 * (t + 1))
                rotate(0)
                rotate(1)
                low_v(1)
                next_x(0)
                rotate(2)
                low(0)
                rotate(3)
                next_x(1)
                low(1)
                low(2)
                low_v(4)
                low(3)

            low_x(0, 0, 0)
            low_x(0, 0, 1)
            over_tiles(dve, tile)


def gates_phase(nc, w_in, b_gate, xt_hi, xt_lo, gates):
    with Phase(nc, "g") as ph:
        raw = ph.sb("raw", [P, 2, GATE])
        w_hi = ph.sb("w_hi", [P, KD, GATE], F32R)
        w_lo = ph.sb("w_lo", [P, KD, GATE], F32R)
        xh = ph.sb("xh", [P, 2, D], F32R)
        xl = ph.sb("xl", [P, 2, D], F32R)
        bias = ph.sb("bias", [P, GATE])
        out = ph.sb("out", [P, GATE])
        pg = [ph.ps(f"pg{j}", [P, BANK]) for j in range(8)]
        w_loaded, w_his, w_los = ph.sems("w_loaded", 2), ph.sem("w_his"), ph.sem("w_los")
        x_loaded, b_loaded = ph.sems("x_loaded", 2), ph.sem("b_loaded")
        product, biased, gated, stored = ph.sem("product"), ph.sem("biased"), ph.sem("gated"), ph.sem("stored")
        block = ph.block()
        NG4 = GATE // BANK

        @block.sync
        def _(sp):
            def load(t, u):
                sp.dma_start(f(xh[:, u, :]), xt_hi[bass.ds(t, 1)]).then_inc(x_loaded[u], 16)
                sp.dma_start(f(xl[:, u, :]), xt_lo[bass.ds(t, 1)]).then_inc(x_loaded[u], 16)

            for u in range(2):
                load(u, u)
            with sp.Fori(0, KD // 2) as i:
                for w in range(2):
                    k = 2 * i + w
                    sp.wait_ge(w_los, k + 1)
                    sp.dma_start(raw[:, w, :], w_in[0, bass.ts(k, P), QKV:QKV + GATE]).then_inc(w_loaded[w], 16)
            sp.dma_start(bias[:], b_gate.to_broadcast([P, GATE])).then_inc(b_loaded, 16)
            with sp.Fori(1, NT // 2) as i:
                for u in range(2):
                    t = 2 * i + u
                    sp.wait_ge(product, NG4 * (t - 1))
                    load(t, u)

        @block.tensor
        def _(pe):
            for u in range(2):
                pe.wait_ge(x_loaded[u], 32)
            for k in range(KD):
                pe.wait_ge(w_los, 3 + k)
                ks = slice(k * P, (k + 1) * P)
                for u in range(2):
                    for j in range(NG4):
                        cs, bank = slice(j * BANK, (j + 1) * BANK), pg[4 * u + j]
                        nc.tensor.matmul(bank[:], xh[:, u, ks], w_hi[:, k, cs], start=(k == 0), stop=False)
                        nc.tensor.matmul(bank[:], xl[:, u, ks], w_hi[:, k, cs], start=False, stop=False)
                        last = nc.tensor.matmul(bank[:], xh[:, u, ks], w_lo[:, k, cs], start=False, stop=(k == KD - 1))
                        if k == KD - 1:
                            last.then_inc(product, 1)
            with pe.Fori(1, NT // 2) as i:
                for u in range(2):
                    t = 2 * i + u
                    pe.wait_ge(x_loaded[u], 32 * (i + 1))
                    for j in range(NG4):
                        pe.wait_ge(biased, NG4 * t + j + 1)
                        bank = pg[4 * u + j]
                        for k in range(KD):
                            ks, cs = slice(k * P, (k + 1) * P), slice(j * BANK, (j + 1) * BANK)
                            nc.tensor.matmul(bank[:], xh[:, u, ks], w_hi[:, k, cs], start=(k == 0), stop=False)
                            nc.tensor.matmul(bank[:], xl[:, u, ks], w_hi[:, k, cs], start=False, stop=False)
                            last = nc.tensor.matmul(bank[:], xh[:, u, ks], w_lo[:, k, cs], start=False, stop=(k == KD - 1))
                        last.then_inc(product, 1)

        @block.vector
        def _(dve):
            dve.sem_inc(w_los, 2)
            dve.sem_inc(biased, 2 * NG4)
            with dve.Fori(0, KD) as k:
                dve.wait_ge(w_his, k + 1)
                nc.vector.tensor_tensor(w_lo[:, bass.ds(k, 1), :], raw[:, bass.ds(k % 2, 1), :],
                                        f(w_hi[:, bass.ds(k, 1), :]), ALU.subtract).then_inc(w_los, 1)
            dve.wait_ge(b_loaded, 16)
            with dve.Fori(0, NT // 2) as i:
                for u in range(2):
                    for j in range(NG4):
                        t = 2 * i + u
                        dve.wait_ge(product, NG4 * t + j + 1)
                        if j == 0:
                            dve.wait_ge(stored, 16 * (t + 1))
                        at = slice(j * BANK, (j + 1) * BANK)
                        nc.vector.tensor_tensor(out[:, at], pg[4 * u + j][:], bias[:, at], ALU.add).then_inc(biased, 1)

        @block.scalar
        def _(act):
            act.sem_inc(stored, 16)
            with act.Fori(0, KD // 2) as i:
                for w in range(2):
                    k = 2 * i + w
                    act.wait_ge(w_loaded[w], 16 * (i + 1))
                    nc.scalar.activation(w_hi[:, bass.ds(k, 1), :], raw[:, w:w + 1, :], ACT.Copy).then_inc(w_his, 1)
            with act.Fori(0, NT) as t:
                act.wait_ge(biased, NG4 * t + 3 * NG4)
                nc.scalar.activation(out[:], out[:], ACT.Sigmoid).then_inc(gated, 1)
                act.wait_ge(gated, t + 1)
                act.dma_start(gates[bass.ts(t, P), :], out[:]).then_inc(stored, 16)
            act.wait_ge(stored, 16 * (NT + 1))


def window_attention_phase(nc, sinks, ident, qk_hi, qk_lo, v_hi, v_lo, oa, w_slices, w_hi, w_lo):
    assert len(w_slices) == NT
    W = CHUNK + P
    GH = A_HEADS // A_KV
    assert A_KV == 2
    UNITS = A_KV * NT
    with Phase(nc, "a") as ph:
        qs = ph.sb("qs", [P, 2, A_HEADS, P], F32R)
        kh = ph.sb("kh", [P, 2, A_KV, W], F32R)
        kl = ph.sb("kl", [P, 2, A_KV, W], F32R)
        vp = ph.sb("vp", [CHUNK, 2, A_KV, 2, HD], F32R)
        vc = ph.sb("vc", [P, 2, A_KV, 2, HD], F32R)
        pr = ph.sb("pr", [P, A_KV, GH, W])
        tph = ph.sb("tph", [CHUNK, A_KV, GH, P], F32R)
        tpl = ph.sb("tpl", [CHUNK, A_KV, GH, P], F32R)
        tch = ph.sb("tch", [P, A_KV, GH, P], F32R)
        tcl = ph.sb("tcl", [P, A_KV, GH, P], F32R)
        parts = ph.sb("parts", [P, A_KV, GH, 2, HD])
        o = ph.sb("o", [P, 2, A_KV, GH, HD])
        sink = ph.sb("sink", [P, A_KV, GH])
        mx, m, nb, se, den, inv, sums, diff = (ph.sb(n, [P, A_KV, GH]) for n in
                                               ("mx", "m", "nb", "se", "den", "inv", "sums", "diff"))
        raw = ph.sb("raw", [P, 2, D])
        mask_f = ph.sb("mask_f", [P, P + 2 * W])
        mask = ph.sb("mask", [P, P + 2 * W], F32R)
        bank = [ph.ps(f"s{g}", [P, GH // 2, BANK]) for g in range(A_KV)]
        tp = ph.ps("tp", [CHUNK, GH, P])
        tc = ph.ps("tc", [P, GH, P])
        po = [ph.ps(f"o{g}", [P, GH, 2, HD]) for g in range(A_KV)]
        qk_loaded, v_loaded = ph.sems("qk_loaded", 2), ph.sems("v_loaded", 2)
        mask_step, sink_in, stand_in = ph.sem("mask_step"), ph.sem("sink_in"), ph.sem("stand_in")
        scores, maxed, summed, exped = ph.sem("scores"), ph.sem("maxed"), ph.sem("summed"), ph.sem("exped")
        turned, t_hi, t_lo, pv, scaled = (ph.sem(n) for n in ("turned", "t_hi", "t_lo", "pv", "scaled"))
        added, stored = ph.sem("added"), ph.sems("stored", 2)
        w_in, w_his, w_los = ph.sems("w_in", 2), ph.sem("w_his"), ph.sem("w_los")
        block = ph.block()

        def score(g, j):
            return bank[g][:, j // 2, (j % 2) * W:(j % 2 + 1) * W]

        @block.sync
        def _(sp):
            sp.dma_start(sink[:], sinks.rearrange("a (g h) -> a g h", g=A_KV).to_broadcast([P, A_KV, GH])).then_inc(sink_in, 16)
            for u in range(2):
                sp.sem_inc(stored[u], 16)

            def load_qk(t, u):
                cols = bass.ts(t, P)
                first = isinstance(t, int) and t == 0
                for half, src in ((0, qk_hi), (1, qk_lo)):
                    rows = slice(half * HD, (half + 1) * HD)
                    sp.dma_start(f(qs[rows, u]), src[0:4, :, cols].rearrange("c (b p) n -> p (c b) n", b=2)).then_inc(qk_loaded[u], 16)
                    for dst, ksrc in ((kh, qk_hi), (kl, qk_lo)):
                        k = ksrc[4].rearrange("(g p) n -> p g n", g=A_KV)
                        if first:
                            sp.dma_start(f(dst[rows, u, :, 0:CHUNK]), k[:, :, 0:CHUNK]).then_inc(stand_in, 16)
                            sp.dma_start(f(dst[rows, u, :, CHUNK:W]), k[:, :, cols]).then_inc(qk_loaded[u], 16)
                        else:
                            sp.dma_start(f(dst[rows, u]), k[:, :, bass.ds(t * P - CHUNK, W)]).then_inc(qk_loaded[u], 16)

            def load_v(t, u):
                first = isinstance(t, int) and t == 0
                tile, rows = (slice(0, 1), slice(0, CHUNK)) if first else (bass.ds(t - 1, 1), slice(CHUNK, P))
                for half, src in enumerate((v_hi, v_lo)):
                    for dst, at in ((vp, (tile, rows)), (vc, (bass.ds(t, 1), slice(0, P)))):
                        sp.dma_start(f(dst[:, u, :, half, :]), src[at[0], at[1], 0:A_K].rearrange("a p (g d) -> p (a g) d", g=A_KV)).then_inc(v_loaded[u], 16)

            def store(t, u):
                sp.wait_ge(added, 2 * t + 2)
                sp.dma_start(oa[bass.ts(t, P), :], o[:, u].rearrange("p g h d -> p (g h d)")).then_inc(stored[u], 16)

            def step(s, u):
                sp.wait_ge(scores, 2 * s + 2)
                load_qk(s + 2, u)
                sp.wait_ge(pv, 2 * s)
                load_v(s + 1, 1 - u)
                store(s - 1, 1 - u)

            load_qk(0, 0)
            load_v(0, 0)
            load_qk(1, 1)
            load_v(1, 1)
            sp.wait_ge(scores, 2)
            load_qk(2, 0)
            with sp.Fori(0, NT // 2 - 2) as i:
                step(2 * i + 1, 1)
                step(2 * i + 2, 0)
            step(NT - 3, 1)
            sp.wait_ge(pv, 2 * (NT - 2))
            load_v(NT - 1, 1)
            for t in range(NT - 3, NT):
                store(t, t % 2)
            for u in range(2):
                sp.wait_ge(stored[u], 16 * (NT // 2 + 1))

        @block.gpsimd
        def _(pool):
            nc.gpsimd.memset(mask_f[:], 0.0).then_inc(mask_step, 1)
            pool.wait_ge(mask_step, 1)
            nc.gpsimd.memset(mask_f[0:1, 0:CHUNK], 1.0).then_inc(mask_step, 1)
            nc.gpsimd.memset(mask_f[32:33, CHUNK:P], 1.0).then_inc(mask_step, 1)
            for first in range(2):
                m0 = P + W * first
                nc.gpsimd.memset(mask_f[0:1, m0 + P:m0 + W], NEG).then_inc(mask_step, 1)
                nc.gpsimd.memset(mask_f[32:33, m0:m0 + CHUNK], NEG).then_inc(mask_step, 1)
            nc.gpsimd.memset(mask_f[0:1, P + W:P + W + CHUNK], NEG).then_inc(mask_step, 1)

            def low_w(n):
                pool.wait_ge(w_his, n + 1)
                nc.gpsimd.tensor_tensor(w_lo[:, n, :], raw[:, n % 2, :], f(w_hi[:, n, :]), ALU.subtract).then_inc(w_los, 1)

            def sum_parts(t):
                pool.wait_ge(stored[t % 2], 16 * (t // 2 + 1))
                for g in range(A_KV):
                    pool.wait_ge(scaled, 2 * t + g + 3)
                    nc.gpsimd.tensor_tensor(o[:, t % 2, g], parts[:, g, :, 0, :], parts[:, g, :, 1, :], ALU.add).then_inc(added, 1)

            for n, (w, k) in enumerate(w_slices):
                if n >= 2:
                    pool.wait_ge(w_los, n - 1)
                pool.dma_start(raw[:, n % 2, :], w[0, k * P:(k + 1) * P, :]).then_inc(w_in[n % 2], 16)
                if n:
                    low_w(n - 1)
                    sum_parts(n - 1)
            low_w(NT - 1)
            sum_parts(NT - 1)

        def over_tiles(eng, unit):
            for g in range(A_KV):
                unit(g, 0, 0, g, n0=True if g == 0 else False, tail=False)
            with eng.Fori(0, NT // 2 - 1) as i:
                for w in range(2):
                    for g in range(A_KV):
                        unit(2 * (2 * i + 1 + w) + g, i + w, 1 - w, g, n0=False, tail=False)
            for g in range(A_KV):
                unit(UNITS - 2 + g, NT // 2 - 1, 1, g, n0=False, tail=True)

        def tile_of(k, u):
            return 2 * k + u

        @block.tensor
        def _(pe):
            pe.wait_ge(mask_step, 9)

            def scores_of(k, u, g, first):
                if g == 0:
                    pe.wait_ge(qk_loaded[u], 6 * 16 * (k + 1))
                for j in range(GH):
                    q = qs[:, u, GH * g + j, :]
                    nc.tensor.matmul(score(g, j), q, kh[:, u, g, :], start=True, stop=False)
                    nc.tensor.matmul(score(g, j), q, kl[:, u, g, :], start=False, stop=False)
                    m0 = P + W * first
                    last = nc.tensor.matmul(score(g, j), mask[:, 0:P], mask[:, m0:m0 + W], start=False, stop=True)
                last.then_inc(scores, 1)

            def values_of(n, k, u, g):
                pe.wait_ge(t_lo, 2 * n + 4)
                pe.wait_ge(scaled, n + 1)
                if g == 0:
                    pe.wait_ge(v_loaded[u], 4 * 16 * (k + 1))
                for j in range(GH):
                    both, high = po[g][:, j].rearrange("p s d -> p (s d)"), po[g][:, j, 0, :]
                    nc.tensor.matmul(both, tch[:, g, j, :], vc[:, u, g].rearrange("p s d -> p (s d)"), start=True, stop=False)
                    nc.tensor.matmul(high, tcl[:, g, j, :], vc[:, u, g, 0, :], start=False, stop=False)
                    nc.tensor.matmul(high, tpl[:, g, j, :], vp[:, u, g, 0, :], start=False, stop=False)
                    last = nc.tensor.matmul(both, tph[:, g, j, :], vp[:, u, g].rearrange("p s d -> p (s d)"), start=False, stop=True)
                last.then_inc(pv, 1)

            def unit(n, k, u, g, n0, tail):
                pe.wait_ge(exped, n + 1)
                pe.wait_ge(t_lo, 2 * n + 2)
                for j in range(GH):
                    nc.tensor.transpose(tc[:, j, :], pr[:, g, j, CHUNK:W], ident[:])
                    last = nc.tensor.transpose(tp[:, j, :], pr[:, g, j, 0:CHUNK], ident[:])
                last.then_inc(turned, 1)
                if not tail:
                    scores_of(k + u, 1 - u, g, 0)
                if not n0:
                    if g:
                        values_of(n - 1, k, u, 0)
                    else:
                        values_of(n - 1, k - (1 - u), 1 - u, 1)

            pe.wait_ge(stand_in, 4 * 16)
            scores_of(0, 0, 0, 1)
            scores_of(0, 0, 1, 1)
            over_tiles(pe, unit)
            values_of(UNITS - 1, NT // 2 - 1, 1, 1)

        @block.scalar
        def _(act):
            def exps(n, g):
                act.wait_ge(maxed, 3 * n + 3)
                for j in range(GH):
                    nc.scalar.activation(pr[:, g, j, :], score(g, j), ACT.Exp, bias=nb[:, g, j:j + 1], scale=SCALE,
                                         accum_out=sums[:, g, j:j + 1])
                nc.scalar.activation(se[:, g, :], diff[:, g, :], ACT.Exp).then_inc(exped, 1)

            def unit(n, k, u, g, n0, tail):
                act.wait_ge(turned, n + 1)
                nc.scalar.activation(tph[:, g], tp[:], ACT.Copy).then_inc(t_hi, 1)
                nc.scalar.activation(tch[:, g], tc[:], ACT.Copy).then_inc(t_hi, 1)
                if not (tail and g):
                    exps(n + 1, 1 - g)
                if g:
                    act.wait_ge(w_in[u], 16 * (k + 1))
                    nc.scalar.activation(w_hi[:, bass.ds(tile_of(k, u), 1), :], raw[:, u:u + 1, :], ACT.Copy).then_inc(w_his, 1)

            exps(0, 0)
            over_tiles(act, unit)

        @block.vector
        def _(dve):
            dve.sem_inc(t_lo, 2)
            dve.sem_inc(scaled, 2)
            dve.wait_ge(mask_step, 8)
            nc.vector.tensor_copy(mask[:], mask_f[:]).then_inc(mask_step, 1)
            dve.wait_ge(sink_in, 16)

            def maxima(n, g):
                dve.wait_ge(scores, n + 1)
                nc.vector.tensor_reduce(mx[:, g, :].rearrange("p (a b) -> p a b", b=2),
                                        bank[g][:, :, 0:2 * W].rearrange("p a (b w) -> p a b w", b=2),
                                        axis=AX.X, op=ALU.max).then_inc(maxed, 1)
                dve.wait_ge(maxed, 3 * n + 1)
                nc.vector.scalar_tensor_tensor(m[:, g, :], mx[:, g, :], SCALE, sink[:, g, :], ALU.mult, ALU.max).then_inc(maxed, 1)
                dve.wait_ge(maxed, 3 * n + 2)
                nc.vector.tensor_tensor(diff[:, g, :], sink[:, g, :], m[:, g, :], ALU.subtract)
                nc.vector.tensor_scalar(nb[:, g, :], m[:, g, :], -1.0, None, ALU.mult).then_inc(maxed, 1)

            def scale(n, k, u, g):
                dve.wait_ge(pv, n + 1)
                if not isinstance(n, int) or n >= 2:
                    dve.wait_ge(added, n - 1)
                nc.vector.tensor_tensor(parts[:, g].rearrange("p h s d -> p h (s d)"), po[g][:].rearrange("p h s d -> p h (s d)"),
                                        inv[:, g, :].unsqueeze(2).to_broadcast([P, GH, 2 * HD]), ALU.mult).then_inc(scaled, 1)

            def unit(n, k, u, g, n0, tail):
                dve.wait_ge(t_hi, 2 * n + 1)
                nc.vector.tensor_tensor(tpl[:, g], tp[:], f(tph[:, g]), ALU.subtract).then_inc(t_lo, 1)
                dve.wait_ge(t_hi, 2 * n + 2)
                nc.vector.tensor_tensor(tcl[:, g], tc[:], f(tch[:, g]), ALU.subtract).then_inc(t_lo, 1)
                dve.wait_ge(exped, n + 1)
                nc.vector.tensor_tensor(den[:, g, :], sums[:, g, :], se[:, g, :], ALU.add).then_inc(summed, 1)
                dve.wait_ge(summed, 2 * n + 1)
                nc.vector.reciprocal(inv[:, g, :], den[:, g, :]).then_inc(summed, 1)
                if not tail:
                    maxima(n + 2, g)
                if not n0:
                    dve.wait_ge(summed, 2 * n)
                    if g:
                        scale(n - 1, k, u, 0)
                    else:
                        scale(n - 1, k - (1 - u), 1 - u, 1)

            maxima(0, 0)
            maxima(1, 1)
            over_tiles(dve, unit)
            dve.wait_ge(summed, 2 * UNITS)
            scale(UNITS - 1, NT // 2 - 1, 1, 1)


def diff_attention_phase(nc, lambdas, ident, qk_hi, qk_lo, v_hi, v_lo, ob):
    MAPS = 2
    NQ = SEQ // P
    NCH = SEQ // BANK
    AHEAD = 3
    groups = [(i * P + P + BANK - 1) // BANK for i in range(NQ)]
    before = [sum(groups[:i]) for i in range(NQ + 1)]
    GB = before[NQ]
    SB = MAPS * GB

    def keys(i, g):
        return slice(g * BANK, min((g + 1) * BANK, (i + 1) * P))

    steps = [(i, g) for i in range(NQ) for g in range(groups[i])]
    first_step = before[:NQ]
    scores_at, exps_at, combine_at = [[] for _ in steps], [[] for _ in steps], [[] for _ in steps]
    for n, (i, g) in enumerate(steps):
        if i + AHEAD < NQ:
            scores_at[n] += [(i + AHEAD, g)] + ([(i + AHEAD, g + 1)] if g + 1 == groups[i] < groups[i + AHEAD] else [])
        if i:
            combine_at[max(n - 2, first_step[i - 1])].append((i, g))
    for i in range(1, NQ):
        exps_at[max(first_step[i - 1] - 1, 0)].append((i, 0))
        exps_at[first_step[i - 1]].append((i, 1))

    with Phase(nc, "b") as ph:
        qs = ph.sb("qs", [P, MAPS, SEQ], F32R)
        kh = ph.sb("kh", [P, MAPS, SEQ], F32R)
        kl = ph.sb("kl", [P, MAPS, SEQ], F32R)
        vhl = ph.sb("vhl", [P, NT, 2, BV], F32R)
        sc = ph.sb("sc", [P, AHEAD + 1, MAPS, SEQ])
        at = ph.sb("at", [P, SEQ])
        th = ph.sb("th", [P, SEQ], F32R)
        tl = ph.sb("tl", [P, SEQ], F32R)
        parts = ph.sb("parts", [P, 2, 2, BV])
        o = ph.sb("o", [P, 2, BV])
        mx = ph.sb("mx", [P, AHEAD + 1, MAPS, NCH])
        mall = ph.sb("mall", [P, AHEAD + 1, MAPS])
        nb = ph.sb("nb", [P, AHEAD + 1, MAPS])
        sums = ph.sb("sums", [P, AHEAD + 1, MAPS])
        inv = ph.sb("inv", [P, AHEAD + 1, MAPS])
        coef = ph.sb("coef", [P, AHEAD + 1])
        lam_in = ph.sb("lam_in", [P, 4, HD])
        lam_prod = ph.sb("lam_prod", [P, 2, HD])
        lam_sum = ph.sb("lam_sum", [P, 2])
        lam_exp = ph.sb("lam_exp", [P, 2])
        neg_lam = ph.sb("neg_lam", [P, 1])
        mask_f = ph.sb("mask_f", [P, 2, P])
        mask = ph.sb("mask", [P, 2, P], F32R)
        bank = [ph.ps(f"s{j}", [P, BANK]) for j in range(4)]
        pt = [ph.ps(f"t{j}", [P, BANK]) for j in range(2)]
        po = [ph.ps(f"o{j}", [P, 2 * BV]) for j in range(2)]
        qk_loaded, v_loaded = ph.sems("qk_loaded", NCH), ph.sems("v_loaded", NCH)
        scores, copied, biased, exped = ph.sem("scores"), ph.sem("copied"), ph.sem("biased"), ph.sem("exped")
        combined, turned, t_hi, t_lo = ph.sem("combined"), ph.sem("turned"), ph.sem("t_hi"), ph.sem("t_lo")
        pv, scaled, added, stored = ph.sem("pv"), ph.sem("scaled"), ph.sem("added"), ph.sems("stored", 2)
        lam_loaded, lam_step, lam_ready, mask_step = ph.sem("lam_loaded"), ph.sem("lam_step"), ph.sem("lam_ready"), ph.sem("mask_step")
        maxed, inverted, coefed = ph.sem("maxed"), ph.sem("inverted"), ph.sem("coefed")
        block = ph.block()

        @block.sync
        def _(sp):
            for n, lam in enumerate(lambdas):
                sp.dma_start(lam_in[:, n, :], lam.to_broadcast([P, HD])).then_inc(lam_loaded, 16)
            with sp.Fori(0, B_HEADS) as h:
                sp.wait_ge(scores, SB * h + 1)
                for c in range(NCH):
                    cols = slice(c * BANK, (c + 1) * BANK)

                    def part(src, piece):
                        return src[bass.ds(h + piece, 1), :, cols].rearrange("a (m p) n -> p (a m) n", m=MAPS)

                    for half, q_src in ((0, qk_hi), (1, qk_lo)):
                        at_ = slice(half * HD, (half + 1) * HD)
                        sp.dma_start(f(qs[at_, :, cols]), part(q_src, 5)).then_inc(qk_loaded[c], 16)
                        sp.dma_start(f(kh[at_, :, cols]), part(qk_hi, 9)).then_inc(qk_loaded[c], 16)
                        sp.dma_start(f(kl[at_, :, cols]), part(qk_lo, 9)).then_inc(qk_loaded[c], 16)
                sp.wait_ge(pv, NQ * h + 1)
                for c in range(NCH):
                    ts = slice(4 * c, 4 * c + 4)
                    vc = bass.ds(h * BV + A_K, BV)
                    sp.dma_start(f(vhl[:, ts, 0, :]), v_hi[ts, :, vc].rearrange("t p n -> p t n")).then_inc(v_loaded[c], 16)
                    sp.dma_start(f(vhl[:, ts, 1, :]), v_lo[ts, :, vc].rearrange("t p n -> p t n")).then_inc(v_loaded[c], 16)

        @block.gpsimd
        def _(pool):
            nc.gpsimd.memset(mask_f[:], 0.0).then_inc(mask_step, 1)
            pool.wait_ge(mask_step, 1)
            nc.gpsimd.memset(mask_f[0:1, 0, 0:CHUNK], 1.0).then_inc(mask_step, 1)
            nc.gpsimd.memset(mask_f[0:1, 1, CHUNK:P], NEG).then_inc(mask_step, 1)
            with pool.Fori(0, B_HEADS) as h:
                for i in range(NQ):
                    pool.wait_ge(scaled, NQ * h + i + 3)
                    if i >= 2:
                        pool.wait_ge(stored[i % 2], 16 * (NQ // 2 * h + i // 2))
                    nc.gpsimd.tensor_tensor(o[:, i % 2, :], parts[:, i % 2, 0, :], parts[:, i % 2, 1, :], ALU.add).then_inc(added, 1)
                    pool.wait_ge(added, NQ * h + i + 1)
                    pool.dma_start(ob[i * P:(i + 1) * P, bass.ds(h * BV, BV)], o[:, i % 2, :]).then_inc(stored[i % 2], 16)
                for u in range(2):
                    pool.wait_ge(stored[u], 16 * (NQ // 2) * (h + 1))

        @block.tensor
        def _(pe):
            pe.sem_inc(scores, 1)
            pe.sem_inc(pv, 1)
            pe.wait_ge(mask_step, 4)

            def scores_of(h, i, g):
                ks = keys(i, g)
                diag = ks.stop == (i + 1) * P
                if i % 4 == 0 and diag:
                    pe.wait_ge(qk_loaded[g], 96 * (h + 1))
                for m in range(MAPS):
                    n = MAPS * (before[i] + g) + m
                    pe.wait_ge(copied, SB * h + n + 1)
                    q = qs[:, m, i * P:(i + 1) * P]
                    out = bank[n % 4][:, 0:ks.stop - ks.start]
                    nc.tensor.matmul(out, q, kh[:, m, ks], start=True, stop=False)
                    last = nc.tensor.matmul(out, q, kl[:, m, ks], start=False, stop=not diag)
                    if diag:
                        last = nc.tensor.matmul(out[:, i * P - ks.start:], mask[:, 0, :], mask[:, 1, :], start=False, stop=True)
                    last.then_inc(scores, 1)

            def turn(h, i, g):
                n = before[i] + g
                pe.wait_ge(combined, GB * h + n + 1)
                pe.wait_ge(t_lo, GB * h + n + 1)
                ks = keys(i, g)
                for c in range(ks.start, ks.stop, P):
                    last = nc.tensor.transpose(pt[n % 2][:, c - ks.start:c - ks.start + P], at[:, c:c + P], ident[:])
                last.then_inc(turned, 1)

            def values_of(h, i, g):
                pe.wait_ge(t_lo, GB * h + before[i] + g + 3)
                ks = keys(i, g)
                if g == 0:
                    pe.wait_ge(scaled, NQ * h + i + 1)
                if i % 4 == 0 and ks.stop == (i + 1) * P:
                    pe.wait_ge(v_loaded[g], 32 * (h + 1))
                for c in range(ks.start, ks.stop, P):
                    b, bs = c // P, slice(c, c + P)
                    if b:
                        nc.tensor.matmul(po[i % 2][:, 0:BV], tl[:, bs], vhl[:, b, 0, :], start=False, stop=False)
                    last = nc.tensor.matmul(po[i % 2][:], th[:, bs], vhl[:, b].rearrange("p s d -> p (s d)"), start=(b == 0), stop=(0 < b == i))
                    if not b:
                        last = nc.tensor.matmul(po[i % 2][:, 0:BV], tl[:, bs], vhl[:, b, 0, :], start=False, stop=(b == i))
                if ks.stop == (i + 1) * P:
                    last.then_inc(pv, 1)

            with pe.Fori(0, B_HEADS) as h:
                for i in range(AHEAD):
                    for g in range(groups[i]):
                        scores_of(h, i, g)
                turn(h, 0, 0)
                for n, (i, g) in enumerate(steps):
                    for made in scores_at[n]:
                        scores_of(h, *made)
                    if n + 1 < GB:
                        turn(h, *steps[n + 1])
                    values_of(h, i, g)

        @block.scalar
        def _(act):
            act.wait_ge(lam_step, 2)
            nc.scalar.activation(lam_exp[:], lam_sum[:], ACT.Exp).then_inc(lam_ready, 1)

            def exps(h, i, m):
                u, L = i % (AHEAD + 1), (i + 1) * P
                act.wait_ge(biased, NQ * h + i + 1)
                nc.scalar.activation(sc[:, u, m, 0:L], sc[:, u, m, 0:L], ACT.Exp, bias=nb[:, u, m:m + 1],
                                     scale=SCALE, accum_out=sums[:, u, m:m + 1]).then_inc(exped, 1)

            def high(h, i, g):
                n, ks = before[i] + g, keys(i, g)
                act.wait_ge(turned, GB * h + n + 1)
                if i and groups[i - 1] == 1 and g == 0:
                    act.wait_ge(pv, NQ * h + i + 1)
                nc.scalar.activation(th[:, ks], pt[n % 2][:, 0:ks.stop - ks.start], ACT.Copy).then_inc(t_hi, 1)

            def finish(h, i):
                act.wait_ge(inverted, NQ * h + i + 1)
                act.wait_ge(pv, NQ * h + i + 2)
                if i >= 2:
                    act.wait_ge(added, NQ * h + i - 1)
                nc.scalar.activation(parts[:, i % 2].rearrange("p s d -> p (s d)"), po[i % 2][:], ACT.Copy, scale=inv[:, i % (AHEAD + 1), 0:1]).then_inc(scaled, 1)

            act.wait_ge(lam_step, 4)
            with act.Fori(0, B_HEADS) as h:
                for m in range(MAPS):
                    exps(h, 0, m)
                for n, (i, g) in enumerate(steps):
                    high(h, i, g)
                    for taken in exps_at[n]:
                        exps(h, *taken)
                    if i and g == 0:
                        finish(h, i - 1)
                finish(h, NQ - 1)
                act.wait_ge(added, NQ * (h + 1))

        @block.vector
        def _(dve):
            dve.sem_inc(copied, 4)
            dve.sem_inc(t_lo, 2)
            dve.wait_ge(mask_step, 3)
            nc.vector.tensor_copy(mask[:], mask_f[:]).then_inc(mask_step, 1)
            dve.wait_ge(lam_loaded, 64)
            nc.vector.tensor_tensor(lam_prod[:], lam_in[:, 0:4:2, :], lam_in[:, 1:4:2, :], ALU.mult).then_inc(lam_step, 1)
            dve.wait_ge(lam_step, 1)
            nc.vector.reduce_sum(lam_sum[:], lam_prod[:], axis=AX.X).then_inc(lam_step, 1)
            dve.wait_ge(lam_ready, 1)
            nc.vector.tensor_tensor(neg_lam[:], lam_exp[:, 1:2], lam_exp[:, 0:1], ALU.subtract).then_inc(lam_step, 1)
            dve.wait_ge(lam_step, 3)
            nc.vector.tensor_scalar(neg_lam[:], neg_lam[:], -LAM_INIT, None, ALU.add).then_inc(lam_step, 1)
            dve.wait_ge(lam_step, 4)
            dve.sem_inc(scaled, 2)

            def copies(h, i, g):
                u, ks = i % (AHEAD + 1), keys(i, g)
                for m in range(MAPS):
                    n = MAPS * (before[i] + g) + m
                    dve.wait_ge(scores, SB * h + n + 2)
                    nc.vector.tensor_scalar(sc[:, u, m, ks], bank[n % 4][:, 0:ks.stop - ks.start], 1.0, NEG, ALU.mult, ALU.max,
                                            accum_out=mx[:, u, m, g:g + 1]).then_inc(copied, 1)

            def maximum(h, i):
                u = i % (AHEAD + 1)
                dve.wait_ge(copied, SB * h + MAPS * before[i + 1] + 4)
                nc.vector.reduce_max(mall[:, u, :], mx[:, u, :, 0:groups[i]], axis=AX.X).then_inc(maxed, 1)

            def bias(h, i):
                u = i % (AHEAD + 1)
                dve.wait_ge(maxed, NQ * h + i + 1)
                nc.vector.tensor_scalar(nb[:, u, :], mall[:, u, :], -SCALE, None, ALU.mult).then_inc(biased, 1)

            def invert(h, i):
                u, k = i % (AHEAD + 1), NQ * h + i
                dve.wait_ge(exped, MAPS * (k + 1))
                if i > AHEAD:
                    dve.wait_ge(scaled, k + 2 - AHEAD)
                nc.vector.reciprocal(inv[:, u, :], sums[:, u, :]).then_inc(inverted, 1)

            def weigh(h, i):
                u, k = i % (AHEAD + 1), NQ * h + i
                dve.wait_ge(inverted, k + 1)
                nc.vector.scalar_tensor_tensor(coef[:, u:u + 1], inv[:, u, 1:2], neg_lam[:], sums[:, u, 0:1],
                                               ALU.mult, ALU.mult).then_inc(coefed, 1)
                dve.wait_ge(coefed, k + 1)

            def combine(h, i, g):
                u, ks = i % (AHEAD + 1), keys(i, g)
                if i and g < groups[i - 1]:
                    dve.wait_ge(turned, GB * h + before[i - 1] + g + 1)
                nc.vector.scalar_tensor_tensor(at[:, ks], sc[:, u, 1, ks], coef[:, u:u + 1], sc[:, u, 0, ks],
                                               ALU.mult, ALU.add).then_inc(combined, 1)

            def low(h, i, g):
                n, ks = before[i] + g, keys(i, g)
                dve.wait_ge(t_hi, GB * h + n + 1)
                nc.vector.tensor_tensor(tl[:, ks], pt[n % 2][:, 0:ks.stop - ks.start], f(th[:, ks]), ALU.subtract).then_inc(t_lo, 1)

            with dve.Fori(0, B_HEADS) as h:
                for i in range(AHEAD):
                    for g in range(groups[i]):
                        copies(h, i, g)
                    maximum(h, i)
                    bias(h, i)
                invert(h, 0)
                weigh(h, 0)
                combine(h, 0, 0)
                copied_blocks = []
                for n, (i, g) in enumerate(steps):
                    begun = [j for j, c in combine_at[n] if c == 0]
                    low(h, i, g)
                    for j in copied_blocks:
                        maximum(h, j)
                    for j in begun:
                        invert(h, j)
                    for j in copied_blocks:
                        bias(h, j)
                    for j in begun:
                        weigh(h, j)
                    for made in combine_at[n]:
                        combine(h, *made)
                    for made in scores_at[n]:
                        copies(h, *made)
                    copied_blocks = [j for j, c in scores_at[n] if c == groups[j] - 1]


def merge_phase(nc, ident, w_hi, w_lo, oa, ob, gates, x, subln_g, ln_g, ln_b, x1):
    KA, KB = A_Q // P, B_V // P
    with Phase(nc, "m") as ph:
        gt = ph.sb("gt", [P, 2, GATE])
        xin = ph.sb("xin", [P, 2, D])
        oin = ph.sb("oin", [P, 2, A_Q + B_V])
        abh, abl = ph.sb("abh", [P, D], F32R), ph.sb("abl", [P, D], F32R)
        mh, ml = ph.sb("mh", [P, D], F32R), ph.sb("ml", [P, D], F32R)
        pa = ph.sb("pa", [P, D])
        pb = ph.sb("pb", [P, D])
        y = ph.sb("y", [P, 2, D])
        gam = ph.sb("gam", [P, D])
        bet = ph.sb("bet", [P, D])
        sg = ph.sb("sg", [P, BV])
        eps = ph.sb("eps", [P, 1])
        ss, rt, ri = (ph.sb(n, [P, B_HEADS]) for n in ("ss", "rt", "ri"))
        st = ph.sb("st", [P, 2, 6])
        mv = ph.sb("mv", [P, 2])
        sd, rs = ph.sb("sd", [P, 1]), ph.sb("rs", [P, 1])
        pt = ph.ps("pt", [P, D])
        psa, psb, psw = ph.ps("psa", [P, D]), ph.ps("psb", [P, D]), ph.ps("psw", [P, D])
        passed = ph.sem("passed")
        vec_in, vec_step = ph.sem("vec_in"), ph.sem("vec_step")
        oin_in, gt_in, xin_in = ph.sems("oin_in", 2), ph.sems("gt_in", 2), ph.sems("xin_in", 2)
        squared, rooted, normed, rms_step, norm_step = (ph.sem(n) for n in ("squared", "rooted", "normed", "rms_step", "norm_step"))
        ab_turned, ab_hi, ab_lo = ph.sem("ab_turned"), ph.sem("ab_hi"), ph.sem("ab_lo")
        m_turned, m_hi, m_lo = ph.sem("m_turned"), ph.sem("m_hi"), ph.sem("m_lo")
        a_done, b_done, w_done = ph.sem("a_done"), ph.sem("b_done"), ph.sem("w_done")
        gated_a, gated_b, mixed, y_done = (ph.sem(n) for n in ("gated_a", "gated_b", "mixed", "y_done"))
        var_done, sd_done, centred, affine = (ph.sem(n) for n in ("var_done", "sd_done", "centred", "affine"))
        out_step, stored = ph.sem("out_step"), ph.sems("stored", 2)
        block = ph.block()

        def is_tile(t):
            return not isinstance(t, int) or 0 <= t < NT

        def over_steps(eng, step):
            step(0, 0, 0)
            step(1, 0, 1)
            with eng.Fori(1, NT // 2 - 1) as i:
                for u in range(2):
                    step(2 * i + u, i, u)
            for t in range(NT - 2, NT + 2):
                step(t, t // 2, t % 2)

        @block.sync
        def _(sp):
            for src, dst in ((ln_g, gam), (ln_b, bet)):
                sp.dma_start(dst[:], src.to_broadcast([P, D])).then_inc(vec_in, 16)
            sp.dma_start(sg[:], subln_g.to_broadcast([P, BV])).then_inc(vec_in, 16)

            def load_o(t, u):
                sp.dma_start(oin[:, u, 0:A_Q], oa[bass.ts(t, P), :]).then_inc(oin_in[u], 16)
                sp.dma_start(oin[:, u, A_Q:], ob[bass.ts(t, P), :]).then_inc(oin_in[u], 16)

            def load_g(t, u):
                sp.dma_start(gt[:, u, :], gates[bass.ts(t, P), :]).then_inc(gt_in[u], 16)

            def load_x(t, u):
                sp.dma_start(xin[:, u, :], x[0, bass.ts(t, P), :]).then_inc(xin_in[u], 16)

            def step(t, k, u):
                if is_tile(t + 2):
                    sp.wait_ge(ab_turned, t + 1)
                    load_o(t + 2, u)
                if is_tile(t - 1) and is_tile(t + 1):
                    sp.wait_ge(gated_b, t)
                    load_g(t + 1, 1 - u)
                if is_tile(t - 2) and is_tile(t):
                    sp.wait_ge(y_done, t - 1)
                    load_x(t, u)

            for u in range(2):
                load_o(u, u)
                load_g(u, u)
                load_x(u, u)
            over_steps(sp, step)

        @block.tensor
        def _(pe):
            def turn(src, done):
                for k in range(KD):
                    last = nc.tensor.transpose(pt[:, k * P:(k + 1) * P], src[:, k * P:(k + 1) * P], ident[:])
                last.then_inc(done, 1)

            def product(out, hi, lo, ks, w0, done):
                for k in ks:
                    for j in range(D // BANK):
                        js, at, kw = slice(j * BANK, (j + 1) * BANK), slice(k * P, (k + 1) * P), w0 + k
                        nc.tensor.matmul(out[:, js], hi[:, at], w_hi[:, kw, js], start=(k == ks[0]), stop=False)
                        nc.tensor.matmul(out[:, js], lo[:, at], w_hi[:, kw, js], start=False, stop=False)
                        last = nc.tensor.matmul(out[:, js], hi[:, at], w_lo[:, kw, js], start=False, stop=(k == ks[-1]))
                last.then_inc(done, 1)

            def step(t, k, u):
                if is_tile(t):
                    pe.wait_ge(ab_lo, t + 1)
                if is_tile(t - 1):
                    pe.wait_ge(mixed, t)
                    turn(pa, m_turned)
                if is_tile(t):
                    if is_tile(t - 1):
                        pe.wait_ge(gated_a, t)
                    product(psa, abh, abl, range(0, KA), 0, a_done)
                    if is_tile(t - 1):
                        pe.wait_ge(gated_b, t)
                    product(psb, abh, abl, range(KA, KA + KB), 0, b_done)
                if is_tile(t - 1):
                    pe.wait_ge(m_lo, t)
                if is_tile(t + 1):
                    pe.wait_ge(normed, t + 2)
                    turn(oin[:, 1 - u, :], ab_turned)
                if is_tile(t - 1):
                    if is_tile(t - 2):
                        pe.wait_ge(y_done, t - 1)
                    product(psw, mh, ml, range(KD), KA + KB, w_done)

            pe.wait_ge(normed, 1)
            turn(oin[:, 0, :], ab_turned)
            over_steps(pe, step)

        @block.scalar
        def _(act):
            act.wait_ge(vec_step, 2)
            for u in range(2):
                act.sem_inc(stored[u], 16)

            def root(t):
                act.wait_ge(squared, t + 1)
                nc.scalar.activation(rt[:], ss[:], ACT.Sqrt, bias=eps[:], scale=1.0 / BV).then_inc(rooted, 1)

            def high_ab(t):
                act.wait_ge(ab_turned, t + 1)
                nc.scalar.activation(abh[:], pt[:], ACT.Copy).then_inc(ab_hi, 1)

            def step(t, k, u):
                if is_tile(t - 1):
                    act.wait_ge(m_turned, t)
                    nc.scalar.activation(mh[:], pt[:], ACT.Copy).then_inc(m_hi, 1)
                if is_tile(t + 1):
                    root(t + 1)
                if is_tile(t - 2):
                    act.wait_ge(var_done, t - 1)
                    nc.scalar.activation(sd[:], mv[:, 1:2], ACT.Sqrt, bias=eps[:]).then_inc(sd_done, 1)
                if is_tile(t + 1):
                    high_ab(t + 1)
                if is_tile(t - 2):
                    act.wait_ge(affine, t - 1)
                    act.dma_start(x1[bass.ts(t - 2, P), :], y[:, u, :]).then_inc(stored[u], 16)

            root(0)
            high_ab(0)
            over_steps(act, step)
            for u in range(2):
                act.wait_ge(stored[u], 16 * (NT // 2 + 1))

        @block.gpsimd
        def _(pool):
            nc.gpsimd.memset(eps[:], EPS).then_inc(vec_step, 1)
            pool.wait_ge(vec_in, 48)

            def step(t, k, u):
                if is_tile(t - 2):
                    pool.wait_ge(centred, t - 1)
                    nc.gpsimd.tensor_tensor(y[:, u, :], y[:, u, :], gam[:], ALU.mult).then_inc(out_step, 1)
                    pool.wait_ge(out_step, t - 1)
                    nc.gpsimd.tensor_tensor(y[:, u, :], y[:, u, :], bet[:], ALU.add).then_inc(affine, 1)
                if is_tile(t):
                    pool.wait_ge(gated_b, t + 1)
                    nc.gpsimd.tensor_tensor(pa[:], pa[:], pb[:], ALU.add).then_inc(mixed, 1)

            over_steps(pool, step)

        @block.vector
        def _(dve):
            dve.wait_ge(vec_in, 48)
            nc.vector.tensor_scalar(sg[:], sg[:], 1.0 - LAM_INIT, None, ALU.mult).then_inc(vec_step, 1)
            dve.wait_ge(vec_step, 2)

            def heads(ap):
                return ap.rearrange("p (h d) -> p h d", h=B_HEADS)

            def rms(t, k, u):
                b = oin[:, u, A_Q:]
                dve.wait_ge(oin_in[u], 32 * (k + 1))
                nc.vector.tensor_tensor(pb[:, 0:B_V], b, b, ALU.mult).then_inc(rms_step, 1)
                dve.wait_ge(rms_step, 3 * t + 1)
                nc.vector.reduce_sum(ss[:], heads(pb[:, 0:B_V]), axis=AX.X).then_inc(squared, 1)
                dve.wait_ge(rooted, t + 1)
                nc.vector.reciprocal(ri[:], rt[:]).then_inc(rms_step, 1)
                dve.wait_ge(rms_step, 3 * t + 2)
                nc.vector.tensor_tensor(heads(b), heads(b), ri[:].unsqueeze(2).to_broadcast([P, B_HEADS, BV]), ALU.mult).then_inc(rms_step, 1)
                dve.wait_ge(rms_step, 3 * t + 3)
                nc.vector.tensor_tensor(heads(b), heads(b), sg[:].unsqueeze(1).to_broadcast([P, B_HEADS, BV]), ALU.mult).then_inc(normed, 1)

            def low_ab(t):
                dve.wait_ge(ab_hi, t + 1)
                nc.vector.tensor_tensor(abl[:], pt[:], f(abh[:]), ALU.subtract).then_inc(ab_lo, 1)

            def norm(t, k, u):
                dve.wait_ge(w_done, t + 1)
                dve.wait_ge(xin_in[u], 16 * (k + 1))
                dve.wait_ge(stored[u], 16 * (k + 1))
                nc.vector.scalar_tensor_tensor(y[:, u, :], xin[:, u, :], ALPHA, psw[:], ALU.mult, ALU.add).then_inc(y_done, 1)
                dve.wait_ge(y_done, t + 1)
                nc.vector.bn_stats(st[:, 0, :], y[:, u, 0:BANK])
                nc.vector.bn_stats(st[:, 1, :], y[:, u, BANK:]).then_inc(norm_step, 1)
                dve.wait_ge(norm_step, 2 * t + 1)
                settled(dve, passed)
                nc.vector.bn_aggr(mv[:], st[:]).then_inc(var_done, 1)
                dve.wait_ge(sd_done, t + 1)
                nc.vector.reciprocal(rs[:], sd[:]).then_inc(norm_step, 1)
                dve.wait_ge(norm_step, 2 * t + 2)
                nc.vector.tensor_scalar(y[:, u, :], y[:, u, :], mv[:, 0:1], rs[:], ALU.subtract, ALU.mult).then_inc(centred, 1)

            def step(t, k, u):
                if is_tile(t - 1):
                    dve.wait_ge(m_hi, t)
                    nc.vector.tensor_tensor(ml[:], pt[:], f(mh[:]), ALU.subtract).then_inc(m_lo, 1)
                if is_tile(t + 1):
                    rms(t + 1, k + u, 1 - u)
                if is_tile(t - 2):
                    norm(t - 2, k - 1, u)
                if is_tile(t):
                    dve.wait_ge(a_done, t + 1)
                    dve.wait_ge(gt_in[u], 16 * (k + 1))
                    nc.vector.tensor_tensor(pa[:], psa[:], gt[:, u, 0:D], ALU.mult).then_inc(gated_a, 1)
                    dve.wait_ge(b_done, t + 1)
                    nc.vector.tensor_tensor(pb[:], psb[:], gt[:, u, D:], ALU.mult).then_inc(gated_b, 1)
                if is_tile(t + 1):
                    low_ab(t + 1)

            rms(0, 0, 0)
            low_ab(0)
            over_steps(dve, step)


def route_phase(nc, ident, x1, w_group, b_group, w_router, b_router, slots, wts, bounds, slot_token, raw, load_raw):
    NL = NG + NE
    B = BANK // P
    NBATCH = NT // B
    with Phase(nc, "r") as ph:
        xin = ph.sb("xin", [P, B, D])
        th = ph.sb("th", [P, 2, KD, B * P], F32R)
        tl = ph.sb("tl", [P, 2, KD, B * P], F32R)
        lt = ph.sb("lt", [2 * NL, 2, BANK])
        fold = ph.sb("fold", [2 * NL, NL])
        wr = ph.sb("wr", [P, KD, NL])
        wr_hl = ph.sb("wr_hl", [P, KD, 2 * NL], F32R)
        wr_hi, wr_lo = wr_hl[:, :, 0:NL], wr_hl[:, :, NL:]
        br = ph.sb("br", [P, NL])
        lg = ph.sb("lg", [P, NT, NL])
        tri, ones = ph.sb("tri", [P, P]), ph.sb("ones", [P, P])
        desc_i, desc = ph.sb("desc_i", [P, EPG], I32), ph.sb("desc", [P, EPG])
        tok_i, tok = ph.sb("tok_i", [P, NT], I32), ph.sb("tok", [P, NT])
        zero = ph.sb("zero", [MAXT + 1, P])
        gm, km, z, pg, m1, m2, e2, rr = (ph.sb(n, [P, NT, 1]) for n in ("gm", "km", "z", "pg", "m1", "m2", "e2", "rr"))
        gk, gsel, gexp = (ph.sb(n, [P, NT, NG]) for n in ("gk", "gsel", "gexp"))
        el, ek, sel1, sel2, el2 = (ph.sb(n, [P, NT, EPG]) for n in ("el", "ek", "sel1", "sel2", "el2"))
        o1, o2, both, wide = (ph.sb(n, [P, NT, NG, EPG]) for n in ("o1", "o2", "both", "wide"))
        before = ph.sb("before", [P, NT + 1, NE])
        place = ph.sb("place", [P, NT, NE])
        cnt, cnt_f, tiles, first, ones32 = ph.sb("cnt", [P, NE], I32), *(ph.sb(n, [P, NE]) for n in ("cnt_f", "tiles", "first", "ones32"))
        incl = ph.sb("incl", [P, NE])
        base = ph.sb("base", [P, NE])
        slot_f = ph.sb("slot_f", [P, 2, NT])
        pt = ph.ps("pt", [P, 2, D])
        plt = ph.ps("plt", [2 * NL, BANK])
        pl = ph.ps("pl", [P, B, NL])
        pp = ph.ps("pp", [P, NT, NE])
        pc = ph.ps("pc", [P, NE])
        lt_done, folded, fold_step = ph.sem("lt_done"), ph.sem("folded"), ph.sem("fold_step")
        loaded, w_loaded, consts, split = ph.sems("loaded", B), ph.sem("w_loaded"), ph.sem("consts"), ph.sem("split")
        turned, t_hi, t_lo, product, logits = (ph.sem(n) for n in ("turned", "t_hi", "t_lo", "product", "logits"))
        chain, exp_in, exp_out, counted, zeroed, scattered = (ph.sem(n) for n in ("chain", "exp_in", "exp_out", "counted", "zeroed", "scattered"))
        placed, raw_in = ph.sem("placed"), ph.sem("raw_in")
        block = ph.block()

        @block.sync
        def _(sp):
            with nc.allow_non_contiguous_dma("short rows of the router's weights"):
                sp.dma_start(wr[:, :, 0:NG], w_group[0].rearrange("(k p) n -> p k n", p=P)).then_inc(w_loaded, 16)
                sp.dma_start(wr[:, :, NG:], w_router[0].rearrange("(k p) n -> p k n", p=P)).then_inc(w_loaded, 16)
            sp.dma_start(br[:, 0:NG], b_group.to_broadcast([P, NG])).then_inc(w_loaded, 16)
            sp.dma_start(br[:, NG:], b_router.to_broadcast([P, NE])).then_inc(w_loaded, 16)
            sp.wait_ge(consts, 7)
            sp.dma_start(slot_token.rearrange("(t p) n -> t (p n)", p=P), zero[:]).then_inc(zeroed, 16)
            with sp.Fori(0, NBATCH) as i:
                for u in range(B):
                    sp.wait_ge(turned, B * i + u + 1)
                    sp.dma_start(xin[:, u, :], x1[bass.ts(B * i + u, P), :]).then_inc(loaded[u], 16)
            for n in range(raw.shape[1]):
                load_raw(sp, raw, 0, n).then_inc(raw_in, 16)
            sp.wait_ge(raw_in, 16 * raw.shape[1])

        @block.gpsimd
        def _(pool):
            nc.gpsimd.memset(ones[:], 1.0).then_inc(consts, 1)
            nc.gpsimd.memset(tri[:], 1.0).then_inc(consts, 1)
            pool.wait_ge(consts, 2)
            nc.gpsimd.affine_select(out=tri[:], in_=tri[:], compare_op=ALU.is_ge, fill=0.0, base=-1,
                                    pattern=[[1, P]], channel_multiplier=-1).then_inc(consts, 1)
            nc.gpsimd.iota(desc_i[:], [[-1, EPG]], base=EPG, channel_multiplier=0).then_inc(consts, 1)
            nc.gpsimd.iota(tok_i[:], [[P, NT]], base=0, channel_multiplier=1).then_inc(consts, 1)
            nc.gpsimd.memset(ones32[:], 1.0).then_inc(consts, 1)
            nc.gpsimd.memset(zero[:], 0.0).then_inc(consts, 1)
            nc.gpsimd.memset(fold[:], 0.0).then_inc(fold_step, 1)
            for part in range(2):
                pool.wait_ge(fold_step, part + 1)
                nc.gpsimd.affine_select(out=fold[:], in_=fold[:], compare_op=ALU.not_equal, fill=1.0, base=-part * NL,
                                        pattern=[[-1, NL]], channel_multiplier=1).then_inc(fold_step, 1)
            pool.wait_ge(zeroed, 16)
            pool.wait_ge(placed, 1)
            for t in range(NT):
                for c in range(2):
                    pool.indirect_dma_start(out=slot_token, out_offset=bass.IndirectOffsetOnAxis(ap=slots[:, c, t:t + 1], axis=0),
                                            in_=tok[:, t:t + 1], in_offset=None).then_inc(scattered, 16)
            pool.wait_ge(scattered, 16 * 2 * NT)

        @block.tensor
        def _(pe):
            pe.sem_inc(turned, B)
            pe.wait_ge(split, 2)
            pe.wait_ge(fold_step, 3)

            def turn(i, v):
                t = B * i + v
                pe.wait_ge(loaded[v], 16 * (i + 1))
                pe.wait_ge(t_lo, t + 1)
                for c in range(KD):
                    last = nc.tensor.transpose(pt[:, v % 2, c * P:(c + 1) * P], xin[:, v, c * P:(c + 1) * P], ident[:])
                last.then_inc(turned, 1)

            def logits_of(i, w):
                pe.wait_ge(t_lo, B * i + B + 2)
                pe.wait_ge(lt_done, i + 1)
                for c in range(KD):
                    def high():
                        return nc.tensor.matmul(plt[:], wr_hl[:, c, :], th[:, w, c, :], start=(c == 0), stop=(c == KD - 1))

                    if c == 0:
                        high()
                    nc.tensor.matmul(plt[0:NL, :], wr_hl[:, c, 0:NL], tl[:, w, c, :], start=False, stop=False)
                    if c:
                        last = high()
                last.then_inc(product, 1)

            def folds(i, w):
                pe.wait_ge(lt_done, i + 2)
                pe.wait_ge(logits, i + 1)
                for v in range(B):
                    last = nc.tensor.matmul(pl[:, v, :], lt[:, w, v * P:(v + 1) * P], fold[:], start=True, stop=True)
                last.then_inc(folded, 1)

            for i in range(NBATCH + 2):
                if i < NBATCH:
                    for v in range(B):
                        turn(i, v)
                if i >= 2:
                    folds(i - 2, i % 2)
                if 1 <= i <= NBATCH:
                    logits_of(i - 1, (i - 1) % 2)
            pe.wait_ge(counted, 1)
            nc.tensor.matmul(pp[:].rearrange("p t e -> p (t e)"), tri[:], both[:].rearrange("p t g e -> p (t g e)"), start=True, stop=False)
            nc.tensor.matmul(pp[:].rearrange("p t e -> p (t e)"), ones[:], before[:, 0:NT, :].rearrange("p t e -> p (t e)"), start=False, stop=True)
            nc.tensor.matmul(pc[:], ones[:], before[:, NT, :], start=True, stop=True).then_inc(product, 1)

        @block.scalar
        def _(act):
            act.wait_ge(w_loaded, 64)
            nc.scalar.activation(wr_hi, wr[:], ACT.Copy).then_inc(split, 1)
            act.sem_inc(lt_done, 1)

            def copy_logits(i):
                act.wait_ge(product, i + 1)
                nc.scalar.activation(lt[:, i % 2, :], plt[:], ACT.Copy).then_inc(lt_done, 1)

            for i in range(NBATCH):
                for v in range(B):
                    act.wait_ge(turned, B * i + v + 1 + B)
                    nc.scalar.activation(th[:, i % 2, :, v * P:(v + 1) * P], pt[:, v % 2, :].rearrange("p (c n) -> p c n", c=KD),
                                         ACT.Copy).then_inc(t_hi, 1)
                if i:
                    copy_logits(i - 1)
            copy_logits(NBATCH - 1)
            act.wait_ge(exp_in, 1)
            nc.scalar.activation(gexp[:], gexp[:], ACT.Exp).then_inc(exp_out, 1)
            act.wait_ge(exp_in, 2)
            nc.scalar.activation(e2[:], e2[:], ACT.Exp).then_inc(exp_out, 1)

        @block.vector
        def _(dve):
            dve.sem_inc(t_lo, 2)
            dve.sem_inc(logits, 1)
            dve.wait_ge(split, 1)
            nc.vector.tensor_tensor(wr_lo, wr[:], f(wr_hi), ALU.subtract).then_inc(split, 1)

            def read(i):
                dve.wait_ge(folded, i + 1)
                nc.vector.tensor_tensor(lg[:, B * i:B * (i + 1), :], pl[:], br[:].unsqueeze(1).to_broadcast([P, B, NL]), ALU.add).then_inc(logits, 1)

            for i in range(NBATCH):
                for v in range(B):
                    dve.wait_ge(t_hi, B * i + v + 1)
                    at = slice(v * P, (v + 1) * P)
                    nc.vector.tensor_tensor(tl[:, i % 2, :, at], pt[:, v % 2, :].rearrange("p (c n) -> p c n", c=KD),
                                            f(th[:, i % 2, :, at]), ALU.subtract).then_inc(t_lo, 1)
                if i >= 2:
                    read(i - 2)
            for i in range(NBATCH - 2, NBATCH):
                read(i)
            dve.wait_ge(logits, NBATCH + 1)
            step = [0]

            def link(ins):
                step[0] += 1
                ins.then_inc(chain, 1)
                dve.wait_ge(chain, step[0])

            def over(ap, n):
                return ap.to_broadcast([P, NT, n])

            tt, ts, red = nc.vector.tensor_tensor, nc.vector.tensor_scalar, nc.vector.tensor_reduce
            dve.wait_ge(consts, 7)
            link(nc.vector.tensor_copy(desc[:], desc_i[:]))
            link(nc.vector.tensor_copy(tok[:], tok_i[:]))

            def first_of_best(vals, best, key, sel, n):
                link(red(best[:], vals, axis=AX.X, op=ALU.max))
                link(tt(key[:], vals, over(best[:], n), ALU.is_equal))
                link(tt(key[:], key[:], desc[:, 0:n].unsqueeze(1).to_broadcast([P, NT, n]), ALU.mult))
                link(red(km[:], key[:], axis=AX.X, op=ALU.max))
                link(tt(sel[:], key[:], over(km[:], n), ALU.is_equal))

            first_of_best(lg[:, :, 0:NG], gm, gk, gsel, NG)
            tt(gexp[:], lg[:, :, 0:NG], over(gm[:], NG), ALU.subtract).then_inc(exp_in, 1)
            gate4 = gsel[:].unsqueeze(3).to_broadcast([P, NT, NG, EPG])
            link(tt(wide[:], lg[:, :, NG:].rearrange("p t (g e) -> p t g e", g=NG), gate4, ALU.mult))
            link(red(el[:], wide[:].rearrange("p t g e -> p t e g"), axis=AX.X, op=ALU.add))
            first_of_best(el[:], m1, ek, sel1, EPG)
            link(nc.vector.scalar_tensor_tensor(el2[:], sel1[:], NEG, el[:], ALU.mult, ALU.add))
            first_of_best(el2[:], m2, ek, sel2, EPG)
            tt(e2[:], m2[:], m1[:], ALU.subtract).then_inc(exp_in, 1)
            for sel, o in ((sel1, o1), (sel2, o2)):
                link(tt(o[:], sel[:].unsqueeze(2).to_broadcast([P, NT, NG, EPG]), gate4, ALU.mult))
            nc.vector.memset(before[:, 0, :], 0.0)
            link(tt(both[:], o1[:], o2[:], ALU.add))
            for t in range(NT):
                ins = tt(before[:, t + 1, :], before[:, t, :], both[:, t].rearrange("p g e -> p (g e)"), ALU.add)
                if t < NT - 1:
                    link(ins)
            ins.then_inc(counted, 1)
            dve.wait_ge(exp_out, 2)
            link(red(z[:], gexp[:], axis=AX.X, op=ALU.add))
            link(nc.vector.reciprocal(pg[:], z[:]))
            link(ts(rr[:], e2[:], 1.0, None, ALU.add))
            link(nc.vector.reciprocal(rr[:], rr[:]))
            link(tt(wts[:, 0, :].unsqueeze(2), pg[:], rr[:], ALU.mult))
            link(tt(wts[:, 1, :].unsqueeze(2), wts[:, 0, :].unsqueeze(2), e2[:], ALU.mult))
            dve.wait_ge(product, NBATCH + 1)
            link(ts(cnt_f[:], pc[:], float(P - 1), None, ALU.add))
            link(nc.vector.tensor_copy(cnt[:], cnt_f[:]))
            link(ts(cnt[:], cnt[:], 7, None, ALU.arith_shift_right))
            link(nc.vector.tensor_copy(tiles[:], cnt[:]))
            link(ts(tiles[:], tiles[:], 1.0, None, ALU.max))
            link(nc.vector.tensor_tensor_scan(incl[:], ones32[:], tiles[:], 0.0, ALU.mult, ALU.add))
            link(tt(first[:], incl[:], tiles[:], ALU.subtract))
            nc.vector.memset(bounds[:, 0:1], 0)
            link(nc.vector.tensor_copy(bounds[:, 1:NE + 1], incl[:]))
            link(ts(base[:], first[:], float(P), None, ALU.mult))
            link(tt(place[:], pp[:], base[:].unsqueeze(1).to_broadcast([P, NT, NE]), ALU.add))
            for c, o in enumerate((o1, o2)):
                link(tt(wide[:].rearrange("p t g e -> p t (g e)"), o[:].rearrange("p t g e -> p t (g e)"), place[:], ALU.mult))
                link(red(slot_f[:, c, :].unsqueeze(2), wide[:].rearrange("p t g e -> p t (g e)"), axis=AX.X, op=ALU.add))
            nc.vector.tensor_copy(slots[:], slot_f[:]).then_inc(placed, 1)


def expert_phase(nc, ident, x1, slot_token, bounds, raw, load_raw, ys):
    EARLY = 4
    LATE_X = 6
    POOL_LOW = (1, 2, 3)
    KF = FF // P
    NS = KD + KF
    PIECES = 2
    HP = FF // PIECES
    HX = D // 2
    with Phase(nc, "e") as ph:
        wh = ph.sb("wh", [P, NS + EARLY, D], F32R)
        wl = ph.sb("wl", [P, NS + EARLY, D], F32R)
        xg = ph.sb("xg", [P, D])
        xh = ph.sb("xh", [P, D], F32R)
        xl = ph.sb("xl", [P, D], F32R)
        act_g = ph.sb("act_g", [P, FF])
        h = ph.sb("h", [P, FF])
        hh = ph.sb("hh", [P, FF], F32R)
        hl = ph.sb("hl", [P, FF], F32R)
        yo = ph.sb("yo", [P, D])
        zero = ph.sb("zero", [P, D])
        tab = ph.sb("tab", [MAXT + 1, P])
        idx = ph.sb("idx", [P, MAXT + 1], I32)
        idx1 = ph.sb("idx1", [P, 1], I32)
        p_gate, p_up = ph.ps("p_gate", [P, FF]), [ph.ps(f"p_up{p}", [P, BANK]) for p in range(PIECES)]
        py, px = ph.ps("py", [P, D]), ph.ps("px", [P, HX])
        phh = [ph.ps(f"phh{p}", [P, BANK]) for p in range(PIECES)]
        passed = ph.sem("passed")
        tab_in, tab_turned, tab_done = ph.sem("tab_in"), ph.sem("tab_turned"), ph.sem("tab_done")
        raw_in = ph.sems("raw_in", NS)
        w_hi, w_lo, w_lo_pool = ph.sem("w_hi"), ph.sem("w_lo"), ph.sem("w_lo_pool")
        picked, gathered, x_turned, x_hi, x_lo = (ph.sem(n) for n in ("picked", "gathered", "x_turned", "x_hi", "x_lo"))
        gate_done, up_done, silu_done, h_done, h_turned, h_hi, h_lo = (
            ph.sem(n) for n in ("gate_done", "up_done", "silu_done", "h_done", "h_turned", "h_hi", "h_lo"))
        down_done, y_out, stored = ph.sem("down_done"), ph.sem("y_out"), ph.sem("stored")
        zeroed, rest = ph.sem("zeroed"), ph.sem("rest")
        block = ph.block()

        def tiles(eng, e):
            b0 = eng.value_load(bounds[0:1, bass.ds(e, 1)], min_val=0, max_val=MAXT - 1)
            b1 = eng.value_load(bounds[0:1, bass.ds(e + 1, 1)], min_val=1, max_val=MAXT)
            return b0, b1

        def all_tiles(eng):
            return eng.value_load(bounds[0:1, NE:NE + 1], min_val=NE, max_val=MAXT)

        def slot(e, s):
            return bass.ds(s + (EARLY * (e % 2) if s < EARLY else EARLY), 1)

        VECTOR_LOW = [s for s in range(NS) if s not in POOL_LOW]

        def wait_low(eng, e, s):
            if s in POOL_LOW:
                eng.wait_ge(w_lo_pool, len(POOL_LOW) * e + POOL_LOW.index(s) + 1)
            else:
                eng.wait_ge(w_lo, len(VECTOR_LOW) * e + VECTOR_LOW.index(s) + 1)

        def low(eng, e, s, done):
            eng.wait_ge(w_hi, NS * e + s + 1)
            (nc.gpsimd if done is w_lo_pool else nc.vector).tensor_tensor(
                wl[:, slot(e, s), :], raw[:, s:s + 1, :], f(wh[:, slot(e, s), :]), ALU.subtract).then_inc(done, 1)

        def piece(p):
            return slice(p * HP, (p + 1) * HP)

        @block.sync
        def _(sp):
            sp.dma_start(tab[:], slot_token.rearrange("(t p) n -> t (p n)", p=P)).then_inc(tab_in, 16)

            sp.wait_ge(zeroed, 1)
            n = all_tiles(sp)
            with sp.Fori(0, n) as _g:
                sp.sem_inc(rest, 16)
            with sp.Fori(n, MAXT + 1) as g:
                sp.dma_start(ys[bass.ts(g, P), :], zero[:]).then_inc(rest, 16)
            with sp.Fori(0, NE - 1) as e:
                for s in range(NS):
                    wait_low(sp, e, s)
                    load_raw(sp, raw, e + 1, s).then_inc(raw_in[s], 16)
            sp.wait_ge(rest, (MAXT + 1) * 16)

        @block.gpsimd
        def _(pool):
            nc.gpsimd.memset(zero[:], 0.0).then_inc(zeroed, 1)

            def gather(g):
                settled(pool, passed)
                nc.gpsimd.tensor_copy(idx1[:], idx[:, bass.ds(g, 1)]).then_inc(picked, 1)
                pool.wait_ge(picked, g + 1)
                settled(pool, passed)
                pool.indirect_dma_start(out=xg[:], out_offset=None, in_=x1,
                                        in_offset=bass.IndirectOffsetOnAxis(ap=idx1[:, 0:1], axis=0)).then_inc(gathered, 16)

            def expert(e, last):
                b0, b1 = tiles(pool, e)
                pool.wait_ge(x_turned, 2 * b0 + 2)
                gather(b0 + 1)
                if not last:
                    for s in POOL_LOW:
                        low(pool, e + 1, s, w_lo_pool)
                with pool.If(b0 + 1 < b1):
                    with pool.Fori(b0 + 1, b1) as g:
                        pool.wait_ge(x_turned, 2 * g + 2)
                        gather(g + 1)
                return b1

            pool.wait_ge(tab_done, 1)
            gather(0)
            for s in POOL_LOW:
                low(pool, 0, s, w_lo_pool)
            with pool.Fori(0, NE - 1) as e:
                expert(e, False)
            b1 = expert(NE - 1, True)
            pool.wait_ge(gathered, 16 * (b1 + 1))

        @block.tensor
        def _(pe):
            pe.sem_inc(up_done, 1)
            pe.sem_inc(down_done, 1)
            pe.wait_ge(tab_in, 16)
            nc.tensor.transpose(px[:, 0:MAXT + 1], tab[:], ident[0:MAXT + 1, 0:MAXT + 1]).then_inc(tab_turned, 1)

            def turn_x(g, half):
                pe.wait_ge(x_lo, 2 * g + half + 1)
                for c in range(0, HX, P):
                    at = half * HX + c
                    last = nc.tensor.transpose(px[:, c:c + P], xg[:, at:at + P], ident[:])
                last.then_inc(x_turned, 1)

            def turn_h(g, p):
                pe.wait_ge(h_done, PIECES * g + p + 1)
                for c in range(0, HP, P):
                    at = p * HP + c
                    last = nc.tensor.transpose(phh[p][:, c:c + P], h[:, at:at + P], ident[:])
                last.then_inc(h_turned, 1)

            def gate_or_up(g, e, out, js, done):
                for k in range(KD):
                    if out is p_gate:
                        if k % (KD // 2) == 0:
                            pe.wait_ge(x_lo, 2 * g + 2 + 2 * k // KD)
                        wait_low(pe, e, k)
                    if out is p_up[1] and k == KD // 2:
                        turn_h(g, 0)
                    at = slice(k * P, (k + 1) * P)
                    hi, lo = wh[:, slot(e, k), js], wl[:, slot(e, k), js]
                    nc.tensor.matmul(out[:, 0:js.stop - js.start], xh[:, at], hi, start=(k == 0), stop=False)
                    nc.tensor.matmul(out[:, 0:js.stop - js.start], xl[:, at], hi, start=False, stop=False)
                    last = nc.tensor.matmul(out[:, 0:js.stop - js.start], xh[:, at], lo, start=False, stop=(k == KD - 1))
                last.then_inc(done, 1)

            def down(g, e, p):
                pe.wait_ge(h_lo, PIECES * g + p + 1)
                for k in range(p * HP // P, (p + 1) * HP // P):
                    wait_low(pe, e, KD + k)
                    at, n = slice(k * P, (k + 1) * P), EARLY + KD + k
                    for j in range(D // BANK):
                        js = slice(j * BANK, (j + 1) * BANK)
                        nc.tensor.matmul(py[:, js], hh[:, at], wh[:, n, js], start=(k == 0), stop=False)
                        nc.tensor.matmul(py[:, js], hl[:, at], wh[:, n, js], start=False, stop=False)
                        last = nc.tensor.matmul(py[:, js], hh[:, at], wl[:, n, js], start=False, stop=(k == KF - 1))
                return last

            pe.wait_ge(gathered, 16)
            turn_x(0, 0)
            turn_x(0, 1)
            with pe.Fori(0, NE) as e:
                b0, b1 = tiles(pe, e)
                with pe.Fori(b0, b1) as g:
                    gate_or_up(g, e, p_gate, slice(0, FF), gate_done)
                    for p in range(PIECES):
                        gate_or_up(g, e, p_up[p], slice(FF + p * HP, FF + (p + 1) * HP), up_done)
                    pe.wait_ge(gathered, 16 * (g + 2))
                    turn_x(g + 1, 0)
                    turn_h(g, 1)
                    pe.wait_ge(y_out, g + 1)
                    down(g, e, 0)
                    turn_x(g + 1, 1)
                    down(g, e, 1).then_inc(down_done, 1)

        @block.scalar
        def _(act):
            act.sem_inc(stored, 16)

            def high(e, b0, slices):
                for s in slices:
                    if not (isinstance(e, int) and e == 0):
                        act.wait_ge(raw_in[s], 16 * e)
                    if s >= EARLY:
                        if s < KD:
                            act.wait_ge(up_done, PIECES * b0 + 1)
                        else:
                            act.wait_ge(down_done, b0 + 1)
                    nc.scalar.activation(wh[:, slot(e, s), :], raw[:, s:s + 1, :], ACT.Copy).then_inc(w_hi, 1)

            def high_x(g, half):
                act.wait_ge(x_turned, 2 * g + half + 1)
                nc.scalar.activation(xh[:, half * HX:(half + 1) * HX], px[:], ACT.Copy).then_inc(x_hi, 1)

            def store(g):
                act.wait_ge(y_out, g + 2)
                act.dma_start(ys[bass.ts(g, P), :], yo[:]).then_inc(stored, 16)

            def tile(g, early_of=None):
                act.wait_ge(gate_done, g + 1)
                nc.scalar.activation(act_g[:], p_gate[:], ACT.Silu).then_inc(silu_done, 1)
                if early_of is not None:
                    high(early_of, None, range(EARLY - 1))
                for p in range(PIECES):
                    act.wait_ge(h_turned, PIECES * g + p + 1)
                    nc.scalar.activation(hh[:, piece(p)], phh[p][:, 0:HP], ACT.Copy).then_inc(h_hi, 1)
                high_x(g + 1, 0)
                if early_of is not None:
                    high(early_of, None, range(EARLY - 1, EARLY))

            def expert(e, last):
                b0, b1 = tiles(act, e)
                tile(b0, None if last else e + 1)
                with act.If(b0 + 1 < b1):
                    with act.Fori(b0 + 1, b1) as g:
                        high_x(g, 1)
                        tile(g)
                        store(g - 1)
                return b1

            high_x(0, 0)
            high_x(0, 1)
            high(0, 0, range(NS))
            with act.Fori(0, NE - 1) as e:
                b1 = expert(e, False)
                high(e + 1, b1, range(EARLY, LATE_X))
                high_x(b1, 1)
                high(e + 1, b1, range(LATE_X, KD))
                high(e + 1, b1, range(KD, NS))
                store(b1 - 1)
            b1 = expert(NE - 1, True)
            high_x(b1, 1)
            store(b1 - 1)
            act.wait_ge(stored, 16 * (b1 + 1))
            settled(act, passed)

        @block.vector
        def _(dve):
            dve.wait_ge(tab_turned, 1)
            nc.vector.tensor_copy(idx[:], px[:, 0:MAXT + 1]).then_inc(tab_done, 1)
            dve.wait_ge(tab_done, 1)
            dve.sem_inc(x_lo, 1)

            def low_x(g, half):
                dve.wait_ge(x_hi, 2 * g + half + 1)
                at = slice(half * HX, (half + 1) * HX)
                nc.vector.tensor_tensor(xl[:, at], px[:], f(xh[:, at]), ALU.subtract).then_inc(x_lo, 1)

            def tile(g, early_of=None):
                def multiply(p):
                    dve.wait_ge(up_done, PIECES * g + p + 2)
                    nc.vector.tensor_tensor(h[:, piece(p)], act_g[:, piece(p)], p_up[p][:, 0:HP], ALU.mult).then_inc(h_done, 1)

                def low_h(p):
                    dve.wait_ge(h_hi, PIECES * g + p + 1)
                    nc.vector.tensor_tensor(hl[:, piece(p)], phh[p][:, 0:HP], f(hh[:, piece(p)]), ALU.subtract).then_inc(h_lo, 1)

                dve.wait_ge(silu_done, g + 1)
                multiply(0)
                if early_of is not None:
                    for s in range(EARLY):
                        if s not in POOL_LOW:
                            low(dve, early_of, s, w_lo)
                low_h(0)
                multiply(1)
                low_h(1)
                low_x(g + 1, 0)

            def expert(e, last):
                b0, b1 = tiles(dve, e)
                tile(b0, None if last else e + 1)
                with dve.If(b0 + 1 < b1):
                    with dve.Fori(b0 + 1, b1) as g:
                        low_x(g, 1)
                        result(g - 1)
                        tile(g)
                return b1

            def result(g):
                dve.wait_ge(down_done, g + 2)
                dve.wait_ge(stored, 16 * (g + 1))
                nc.vector.tensor_scalar(yo[:], py[:], 1.0, None, ALU.mult).then_inc(y_out, 1)

            dve.sem_inc(y_out, 1)
            low_x(0, 0)
            low_x(0, 1)
            for s in VECTOR_LOW:
                low(dve, 0, s, w_lo)
            with dve.Fori(0, NE - 1) as e:
                b1 = expert(e, False)
                for s in range(EARLY, NS):
                    if s == LATE_X:
                        low_x(b1, 1)
                    if s == KD:
                        result(b1 - 1)
                    low(dve, e + 1, s, w_lo)
            b1 = expert(NE - 1, True)
            low_x(b1, 1)
            result(b1 - 1)


def combine_phase(nc, x1, ys, slots, wts, ln_g, ln_b, out):
    NB = 4
    with Phase(nc, "o") as ph:
        xin, y1, y2, z = (ph.sb(n, [P, NB, D]) for n in ("xin", "y1", "y2", "z"))
        sl = ph.sb("sl", [P, NB, 2, 1], I32)
        ww = ph.sb("ww", [P, NB, 2, 1])
        gam, bet = ph.sb("gam", [P, D]), ph.sb("bet", [P, D])
        st, mv = ph.sb("st", [P, NB, 2, 6]), ph.sb("mv", [P, NB, 2])
        sd, rs, shift = (ph.sb(n, [P, NB]) for n in ("sd", "rs", "shift"))
        eps = ph.sb("eps", [P, 1])
        passed = ph.sem("passed")
        vec_in, eps_set, loaded = ph.sem("vec_in"), ph.sem("eps_set"), ph.sems("loaded", NB)
        picked, got = ph.sem("picked"), ph.sems("got", NB)
        scaled, weighed, first_in, summed, counted = (ph.sem(n) for n in ("scaled", "weighed", "first_in", "summed", "counted"))
        var_done, sd_done, inverted, shifted, normed, times, finished = (
            ph.sem(n) for n in ("var_done", "sd_done", "inverted", "shifted", "normed", "times", "finished"))
        stored = ph.sems("stored", NB)
        block = ph.block()

        def over_steps(eng, step):
            def static(t):
                step(t, lambda j: ((t - j) % NB, (t - j) // NB) if 0 <= t - j < NT else None)

            for t in range(NB):
                static(t)
            with eng.Fori(1, NT // NB) as i:
                for v in range(NB):
                    step(NB * i + v, lambda j, v=v: ((v - j) % NB, i + (v - j) // NB))
            for t in range(NT, NT + NB + 1):
                static(t)

        @block.sync
        def _(sp):
            for src, dst in ((ln_g, gam), (ln_b, bet)):
                sp.dma_start(dst[:], src.to_broadcast([P, D])).then_inc(vec_in, 16)
            for b in range(NB):
                sp.sem_inc(stored[b], 16)

            def step(t, of):
                if of(0):
                    b, k = of(0)
                    if of(NB):
                        sp.wait_ge(scaled, t - NB + 1)
                    sp.dma_start(xin[:, b, :], x1[bass.ts(t, P), :]).then_inc(loaded[b], 16)
                if of(4):
                    b, k = of(4)
                    sp.wait_ge(finished, t - 3)
                    sp.dma_start(out[0, bass.ts(t - 4, P), :], z[:, b, :]).then_inc(stored[b], 16)

            over_steps(sp, step)
            for b in range(NB):
                sp.wait_ge(stored[b], 16 * (NT // NB + 1))

        @block.gpsimd
        def _(pool):
            pool.wait_ge(vec_in, 32)

            def step(t, of):
                if of(0):
                    b, k = of(0)
                    if of(NB):
                        pool.wait_ge(summed, t - NB + 1)
                        settled(pool, passed)
                    nc.gpsimd.tensor_copy(sl[:, b, :, :], slots[:, :, bass.ds(t, 1)]).then_inc(picked, 1)
                    pool.wait_ge(picked, t + 1)
                    settled(pool, passed)
                    for c, y in enumerate((y1, y2)):
                        pool.indirect_dma_start(out=y[:, b, :], out_offset=None, in_=ys,
                                                in_offset=bass.IndirectOffsetOnAxis(ap=sl[:, b, c, :], axis=0)).then_inc(got[b], 16)
                if of(4):
                    b, k = of(4)
                    pool.wait_ge(times, t - 3)
                    nc.gpsimd.tensor_tensor(z[:, b, :], z[:, b, :], bet[:], ALU.add).then_inc(finished, 1)

            over_steps(pool, step)

        @block.scalar
        def _(act):
            act.wait_ge(eps_set, 1)

            def step(t, of):
                if of(1):
                    b, k = of(1)
                    act.wait_ge(loaded[b], 16 * (k + 1))
                    act.wait_ge(stored[b], 16 * (k + 1))
                    nc.scalar.activation(z[:, b, :], xin[:, b, :], ACT.Copy, scale=ALPHA).then_inc(scaled, 1)
                if of(2):
                    b, k = of(2)
                    act.wait_ge(var_done, t - 1)
                    nc.scalar.activation(sd[:, b:b + 1], mv[:, b, 1:2], ACT.Sqrt, bias=eps[:]).then_inc(sd_done, 1)
                if of(3):
                    b, k = of(3)
                    act.wait_ge(shifted, t - 2)
                    nc.scalar.activation(z[:, b, :], z[:, b, :], ACT.Identity, bias=shift[:, b:b + 1],
                                         scale=rs[:, b:b + 1]).then_inc(normed, 1)

            over_steps(act, step)

        @block.vector
        def _(dve):
            nc.vector.memset(eps[:], EPS).then_inc(eps_set, 1)
            dve.wait_ge(vec_in, 32)

            def step(t, of):
                if of(2):
                    b, k = of(2)
                    zb = z[:, b, :]
                    nc.vector.tensor_copy(ww[:, b, :, :], wts[:, :, bass.ds(t - 2, 1)]).then_inc(weighed, 1)
                    dve.wait_ge(weighed, t - 1)
                    dve.wait_ge(scaled, t - 1)
                    dve.wait_ge(got[b], 32 * (k + 1))
                    nc.vector.scalar_tensor_tensor(zb, y1[:, b, :], ww[:, b, 0, :], zb, ALU.mult, ALU.add).then_inc(first_in, 1)
                    dve.wait_ge(first_in, t - 1)
                    nc.vector.scalar_tensor_tensor(zb, y2[:, b, :], ww[:, b, 1, :], zb, ALU.mult, ALU.add).then_inc(summed, 1)
                    dve.wait_ge(summed, t - 1)
                    nc.vector.bn_stats(st[:, b, 0, :], z[:, b, 0:BANK])
                    nc.vector.bn_stats(st[:, b, 1, :], z[:, b, BANK:]).then_inc(counted, 1)
                if of(3):
                    b, k = of(3)
                    dve.wait_ge(sd_done, t - 2)
                    nc.vector.reciprocal(rs[:, b:b + 1], sd[:, b:b + 1]).then_inc(inverted, 1)
                if of(2):
                    b, k = of(2)
                    dve.wait_ge(counted, t - 1)
                    settled(dve, passed)
                    nc.vector.bn_aggr(mv[:, b, :], st[:, b, :, :]).then_inc(var_done, 1)
                if of(3):
                    b, k = of(3)
                    dve.wait_ge(inverted, t - 2)
                    nc.vector.scalar_tensor_tensor(shift[:, b:b + 1], mv[:, b, 0:1], -1.0, rs[:, b:b + 1],
                                                   ALU.mult, ALU.mult).then_inc(shifted, 1)
                if of(4):
                    b, k = of(4)
                    dve.wait_ge(normed, t - 3)
                    nc.vector.tensor_tensor(z[:, b, :], z[:, b, :], gam[:], ALU.mult).then_inc(times, 1)

            over_steps(dve, step)


def program(nc, a, out, phases=99):
    def dram(name, shape):
        return nc.dram_tensor(name, shape, F32, kind="Internal").ap()

    xt_hi, xt_lo = dram("xt_hi", (NT, P, D)), dram("xt_lo", (NT, P, D))
    qk_hi, qk_lo = dram("qk_hi", (NPIECE, P, SEQ)), dram("qk_lo", (NPIECE, P, SEQ))
    v_hi, v_lo = dram("v_hi", (NT, P, VW)), dram("v_lo", (NT, P, VW))
    gates = dram("gates", (SEQ, GATE))
    with ExitStack() as ctx:
        ident = ctx.enter_context(nc.sbuf_tensor("ident", [P, P], F32))
        constants_phase(nc, ident, None)
        with Phase(nc, "qkv") as ph:
            w_hi = ph.sb("w_hi", [P, KD, QKV], F32R)
            w_lo = ph.sb("w_lo", [P, KD, QKV], F32R)
            cos_t, sin_t, nsin_t = (ph.sb(n, [P, NT, HALF]) for n in ("cos", "sin", "nsin"))
            prepare_phase(nc, a["w_in"], a["positions"], a["inv_freq"], w_hi, w_lo, cos_t, sin_t, nsin_t)
            project_phase(nc, a["x"], w_hi, w_lo, cos_t, sin_t, nsin_t, ident, xt_hi, xt_lo, qk_hi, qk_lo, v_hi, v_lo)
        gates_phase(nc, a["w_in"], a["b_gate"], xt_hi, xt_lo, gates)
        ob = dram("ob", (SEQ, B_V))
        diff_attention_phase(nc, [a["lambda_q1"], a["lambda_k1"], a["lambda_q2"], a["lambda_k2"]], ident, qk_hi, qk_lo, v_hi, v_lo, ob)
        oa = dram("oa", (SEQ, A_Q))
        x1 = dram("x1", (SEQ, D))
        w_slices = [(a[w], k) for w in ("w_proj_a", "w_proj_b", "w_out") for k in range(a[w].shape[1] // P)]
        with Phase(nc, "mw") as ph:
            w_hi = ph.sb("w_hi", [P, len(w_slices), D], F32R)
            w_lo = ph.sb("w_lo", [P, len(w_slices), D], F32R)
            window_attention_phase(nc, a["sinks"], ident, qk_hi, qk_lo, v_hi, v_lo, oa, w_slices, w_hi, w_lo)
            merge_phase(nc, ident, w_hi, w_lo, oa, ob, gates, a["x"], a["subln_g"], a["ln1_g"], a["ln1_b"], x1)
        slots = ctx.enter_context(nc.sbuf_tensor("slots", [P, 2, NT], I32))
        wts = ctx.enter_context(nc.sbuf_tensor("wts", [P, 2, NT], F32))
        bounds = ctx.enter_context(nc.sbuf_tensor("bounds", [P, NE + 1], I32))
        slot_token = dram("slot_token", ((MAXT + 1) * P, 1))
        ys = dram("ys", ((MAXT + 1) * P, D))

        def load_raw(sp, raw, e, s):
            src, k = (a["w_gate_up"], s) if s < KD else (a["w_down"], s - KD)
            return sp.dma_start(raw[:, s, :], src[0, bass.ds(e, 1), k * P:(k + 1) * P, :].rearrange("a p n -> p (a n)"))

        with Phase(nc, "rw") as ph:
            raw = ph.sb("raw", [P, KD + FF // P, D])
            route_phase(nc, ident, x1, a["w_group"], a["b_group"], a["w_router"], a["b_router"], slots, wts, bounds, slot_token,
                        raw, load_raw)
            expert_phase(nc, ident, x1, slot_token, bounds, raw, load_raw, ys)
        combine_phase(nc, x1, ys, slots, wts, a["ln2_g"], a["ln2_b"], out)


def rotary_frequencies():
    exponent = np.arange(0, HD, 2, dtype=np.float32) / np.float32(HD)
    return (np.float32(1.0) / np.float32(10000.0) ** exponent).astype(np.float32)[None]


_INS = ["x", "positions", "w_in", "b_gate", "sinks", "lambda_q1", "lambda_k1", "lambda_q2", "lambda_k2", "subln_g",
        "w_proj_a", "w_proj_b", "w_out", "ln1_g", "ln1_b", "w_group", "b_group", "w_router", "b_router", "w_gate_up",
        "w_down", "ln2_g", "ln2_b"]


def kernel(**inputs):
    import concourse.bacc as bacc
    from concourse.bass_utils import run_bass_kernel_spmd

    nc = bacc.Bacc("TRN2", target_bir_lowering=False, num_devices=1)
    arrays = {name: np.ascontiguousarray(inputs[name]) for name in _INS}
    arrays["inv_freq"] = rotary_frequencies()
    aps = {name: nc.dram_tensor(name, v.shape, mybir.dt.from_np(v.dtype), kind="ExternalInput").ap()
           for name, v in arrays.items()}
    out = nc.dram_tensor("out", (1, SEQ, D), F32, kind="ExternalOutput").ap()
    program(nc, aps, out)
    result = run_bass_kernel_spmd(nc, [arrays], core_ids=[0])
    return result.results[0]["out"]
```
